# Optimizing a Trainium2 kernel written in Bass

```python
import math
import jax
import jax.numpy as jnp
from jax import lax
import numpy as np

D_MODEL = 1024
BATCH = 1
SEQ = 256
DEPTH = 2

GRID_W = 64
CTX_LEN = 256
HEAD_DIM = 64
GROUP_WIDTH = D_MODEL // 4
MIX_WIDTH = 4 * GROUP_WIDTH
GROUP_HEADS = GROUP_WIDTH // HEAD_DIM
GQA_KV_HEADS = 2
GQA_Q_PER_KV = GROUP_HEADS // GQA_KV_HEADS
DIFF_QK_DIM = HEAD_DIM // 2
HGRN_KEY_DIM = HEAD_DIM
SCAN_CHUNK = 64
Q_BLOCK = 128
ROPE_BASE = 10000.0
N_EXPERTS = 32
N_EXPERT_GROUPS = 8
EXPERTS_PER_GROUP = N_EXPERTS // N_EXPERT_GROUPS
TOP_K = 2
EXPERT_FF = 512
MOE_BLOCK = 256
NORM_EPS = 1e-6
IN_SPLITS = (
    GROUP_WIDTH, GROUP_WIDTH, GROUP_WIDTH, GROUP_WIDTH,
    GROUP_WIDTH, GQA_KV_HEADS * HEAD_DIM, GQA_KV_HEADS * HEAD_DIM,
    GROUP_WIDTH, GROUP_WIDTH, GROUP_WIDTH, GROUP_WIDTH, GROUP_WIDTH,
    GROUP_WIDTH, GROUP_WIDTH, GROUP_WIDTH,
)
IN_WIDTH = sum(IN_SPLITS)

kernel_name = 'hybrid_prefix_diffusion_block'

def rms_norm(x, gain):
    xf = x.astype(jnp.float32)
    y = xf * lax.rsqrt(jnp.mean(xf * xf, axis=-1, keepdims=True) + NORM_EPS)
    return (y * gain.astype(jnp.float32)).astype(x.dtype)

def modulate(x, shift, scale):
    return x * (1 + scale) + shift

def split_heads(a, n_heads):
    return a.reshape(*a.shape[:-1], n_heads, a.shape[-1] // n_heads)

def split_columns(z):
    idx, acc = [], 0
    for w in IN_SPLITS[:-1]:
        acc += w
        idx.append(acc)
    return jnp.split(z, idx, axis=-1)

def axial_rope(rows, rot_dim):
    n_freq = rot_dim // 4
    inv_freq = ROPE_BASE ** (-jnp.arange(n_freq, dtype=jnp.float32) / n_freq)
    row = jnp.broadcast_to(jnp.arange(rows, dtype=jnp.float32)[:, None], (rows, GRID_W)).reshape(-1)
    col = jnp.broadcast_to(jnp.arange(GRID_W, dtype=jnp.float32)[None, :], (rows, GRID_W)).reshape(-1)
    ang = jnp.concatenate([row[:, None] * inv_freq, col[:, None] * inv_freq], axis=-1)
    return jnp.cos(ang), jnp.sin(ang)

def apply_rope(x, cos, sin):
    shape = (cos.shape[0],) + (1,) * (x.ndim - 3) + (cos.shape[-1],)
    cs, sn = cos.reshape(shape), sin.reshape(shape)
    half = x.shape[-1] // 2
    xf = x.astype(jnp.float32)
    x1, x2 = xf[..., :half], xf[..., half:]
    return jnp.concatenate([x1 * cs - x2 * sn, x2 * cs + x1 * sn], axis=-1).astype(x.dtype)

def sweep_query_blocks(fn, q):
    b, t = q.shape[:2]
    nb = t // Q_BLOCK
    qb = jnp.moveaxis(q.reshape(b, nb, Q_BLOCK, *q.shape[2:]), 1, 0)
    ob = lax.map(fn, qb)
    return jnp.moveaxis(ob, 0, 1).reshape(b, t, *ob.shape[3:])

def gqa_attention(q, k, v):
    scale = q.shape[-1] ** -0.5

    def block(qb):
        s = jnp.einsum('bqhgd,bshd->bhgqs', qb, k, preferred_element_type=jnp.float32) * scale
        p = jax.nn.softmax(s, axis=-1).astype(v.dtype)
        return jnp.einsum('bhgqs,bshd->bqhgd', p, v)
    return sweep_query_blocks(block, q)

def differential_attention(q, k, v, lam):
    scale = q.shape[-1] ** -0.5

    def block(qb):
        s = jnp.einsum('bqhmd,bshmd->bhmqs', qb, k, preferred_element_type=jnp.float32) * scale
        p = jax.nn.softmax(s, axis=-1)
        w = (p[:, :, 0] - lam * p[:, :, 1]).astype(v.dtype)
        return jnp.einsum('bhqs,bshd->bqhd', w, v)
    return sweep_query_blocks(block, q)

def linear_recurrence(q, k, v, log_a, s0):
    b, h, t, _ = q.shape
    dv = v.shape[-1]
    n = t // SCAN_CHUNK

    def to_chunks(a):
        return jnp.moveaxis(a.reshape(b, h, n, SCAN_CHUNK, a.shape[-1]), 2, 0)
    causal = jnp.tril(jnp.ones((SCAN_CHUNK, SCAN_CHUNK), bool))[:, :, None]

    def step(state, inp):
        qc, kc, vc, lac = inp
        qf, kf, vf = qc.astype(jnp.float32), kc.astype(jnp.float32), vc.astype(jnp.float32)
        cum = jnp.cumsum(lac.astype(jnp.float32), axis=2)
        o_inter = jnp.einsum('bhtd,bhdv->bhtv', qf * jnp.exp(cum), state)
        rel = cum[:, :, :, None, :] - cum[:, :, None, :, :]
        decay = jnp.where(causal, jnp.exp(jnp.where(causal, rel, 0.0)), 0.0)
        scores = jnp.einsum('bhtd,bhsd,bhtsd->bhts', qf, kf, decay)
        o_intra = jnp.einsum('bhts,bhsv->bhtv', scores, vf)
        last = cum[:, :, -1:, :]
        new_state = jnp.exp(last[:, :, 0, :, None]) * state + jnp.einsum(
            'bhsd,bhsv->bhdv', kf * jnp.exp(last - cum), vf)
        return new_state, o_inter + o_intra

    s_t, o = lax.scan(step, s0.astype(jnp.float32),
                      (to_chunks(q), to_chunks(k), to_chunks(v), to_chunks(log_a)))
    o = jnp.moveaxis(o, 0, 2).reshape(b, h, t, dv)
    return o.astype(v.dtype), s_t

def two_way_prefix_scan(lat, ctx):
    def flip(a):
        return jnp.flip(a, axis=2)
    q, kf, kb, v, af, ab = lat
    qc, kcf, kcb, vc, acf, acb = ctx
    s0 = jnp.zeros((q.shape[0], q.shape[1], q.shape[-1], v.shape[-1]), jnp.float32)
    oc_f, s_f = linear_recurrence(qc, kcf, vc, acf, s0)
    oc_b, s_b = linear_recurrence(flip(qc), flip(kcb), flip(vc), flip(acb), s0)
    o_f, _ = linear_recurrence(q, kf, v, af, s_f)
    o_b, _ = linear_recurrence(flip(q), flip(kb), flip(v), flip(ab), s_b)
    return o_f + flip(o_b), oc_f + flip(oc_b)

def retention_mixer(parts, parts_c, decay_logit, norm_g, rope, need_ctx):
    def prep(p, rotate):
        q, k, v, g = p
        q = split_heads(q, GROUP_HEADS) * HEAD_DIM ** -0.5
        k = split_heads(k, GROUP_HEADS)
        if rotate:
            q, k = apply_rope(q, *rope), apply_rope(k, *rope)
        return (jnp.swapaxes(q, 1, 2), jnp.swapaxes(k, 1, 2),
                jnp.swapaxes(split_heads(v, GROUP_HEADS), 1, 2), g)
    q, k, v, g = prep(parts, True)
    qc, kc, vc, gc = prep(parts_c, False)
    log_gamma = jax.nn.log_sigmoid(decay_logit.astype(jnp.float32))[:, None, :, None, None]

    def log_decay(a, direction):
        return jnp.broadcast_to(log_gamma[direction], a.shape)
    o, oc = two_way_prefix_scan((q, k, k, v, log_decay(k, 0), log_decay(k, 1)),
                                (qc, kc, kc, vc, log_decay(kc, 0), log_decay(kc, 1)))

    def readout(o_, g_):
        return rms_norm(jnp.swapaxes(o_, 1, 2), norm_g).reshape(g_.shape) * jax.nn.silu(g_)
    return readout(o, g), (readout(oc, gc) if need_ctx else None)

def hgrn2_mixer(parts, parts_c, lower_bound, norm_g, need_ctx):
    lb = lower_bound.astype(jnp.float32).reshape(2, GROUP_HEADS, 1, HGRN_KEY_DIM)

    def bhtd(a):
        return jnp.swapaxes(split_heads(a, GROUP_HEADS), 1, 2)

    def gate(z, d):
        z = bhtd(z).astype(jnp.float32)
        f = lb[d] + (1 - lb[d]) * jax.nn.sigmoid(z)
        return (1 - lb[d]) * jax.nn.sigmoid(-z), jnp.log(f)

    def prep(p):
        q, zf, zb, i, g = p
        k_f, lf_f = gate(zf, 0)
        k_b, lf_b = gate(zb, 1)
        return (bhtd(q), k_f, k_b, bhtd(i), lf_f, lf_b), g
    lat, g = prep(parts)
    ctx, gc = prep(parts_c)
    o, oc = two_way_prefix_scan(lat, ctx)

    def readout(o_, g_):
        return rms_norm(jnp.swapaxes(o_, 1, 2), norm_g).reshape(g_.shape) * jax.nn.silu(g_)
    return readout(o, g), (readout(oc, gc) if need_ctx else None)

def gqa_mixer(parts, parts_c, qn_g, kn_g, rope, need_ctx):
    def prep(p, rotate):
        q, k, v = p
        q = rms_norm(split_heads(q, GROUP_HEADS), qn_g)
        k = rms_norm(split_heads(k, GQA_KV_HEADS), kn_g)
        if rotate:
            q, k = apply_rope(q, *rope), apply_rope(k, *rope)
        q = q.reshape(*q.shape[:2], GQA_KV_HEADS, GQA_Q_PER_KV, HEAD_DIM)
        return q, k, split_heads(v, GQA_KV_HEADS)
    q, k, v = prep(parts, True)
    qc, kc, vc = prep(parts_c, False)
    k_all = jnp.concatenate([kc, k], axis=1)
    v_all = jnp.concatenate([vc, v], axis=1)

    def flat(o_):
        return o_.reshape(*o_.shape[:2], GROUP_WIDTH)
    o = flat(gqa_attention(q, k_all, v_all))
    return o, (flat(gqa_attention(qc, kc, vc)) if need_ctx else None)

def diff_mixer(parts, parts_c, lam_params, norm_g, lambda_init, rope, need_ctx):
    def prep(p, rotate):
        q, k, v = p
        q = q.reshape(*q.shape[:-1], GROUP_HEADS, 2, DIFF_QK_DIM)
        k = k.reshape(*k.shape[:-1], GROUP_HEADS, 2, DIFF_QK_DIM)
        if rotate:
            q, k = apply_rope(q, *rope), apply_rope(k, *rope)
        return q, k, split_heads(v, GROUP_HEADS)
    lp = lam_params.astype(jnp.float32)
    lam = jnp.exp(jnp.sum(lp[0] * lp[1])) - jnp.exp(jnp.sum(lp[2] * lp[3])) + lambda_init
    q, k, v = prep(parts, True)
    qc, kc, vc = prep(parts_c, False)
    k_all = jnp.concatenate([kc, k], axis=1)
    v_all = jnp.concatenate([vc, v], axis=1)

    def readout(o_):
        return (rms_norm(o_, norm_g) * (1 - lambda_init)).reshape(*o_.shape[:2], GROUP_WIDTH)
    o = readout(differential_attention(q, k_all, v_all, lam))
    return o, (readout(differential_attention(qc, kc, vc, lam)) if need_ctx else None)

def routed_moe(h, router_w, router_bias, w_gate, w_up, w_down):
    n, d = h.shape
    scores = jax.nn.sigmoid(jnp.dot(h, router_w, preferred_element_type=jnp.float32))
    sel = (scores + router_bias.astype(jnp.float32)).reshape(n, N_EXPERT_GROUPS, EXPERTS_PER_GROUP)
    group_score = lax.top_k(sel, 2)[0].sum(-1)
    best_group = jnp.argmax(group_score, axis=-1)
    in_group = sel[jnp.arange(n), best_group]
    _, local = lax.top_k(in_group, TOP_K)
    expert = best_group[:, None] * EXPERTS_PER_GROUP + local
    gate = jnp.take_along_axis(scores, expert, axis=1)
    gate = gate / jnp.sum(gate, axis=-1, keepdims=True)

    m = n * TOP_K
    e_flat = expert.reshape(m)
    tok = jnp.repeat(jnp.arange(n), TOP_K)
    order = jnp.argsort(e_flat)
    e_s, tok_s, w_s = e_flat[order], tok[order], gate.reshape(m)[order]
    counts = jnp.bincount(e_flat, length=N_EXPERTS)
    padded = (counts + MOE_BLOCK - 1) // MOE_BLOCK * MOE_BLOCK
    start = jnp.cumsum(counts) - counts
    pend = jnp.cumsum(padded)
    pstart = pend - padded
    dest = pstart[e_s] + jnp.arange(m) - start[e_s]
    n_blocks = -(-m // MOE_BLOCK) + N_EXPERTS
    rows = n_blocks * MOE_BLOCK
    xs = jnp.zeros((rows, d), h.dtype).at[dest].set(h[tok_s])
    block_expert = jnp.clip(jnp.searchsorted(pend, jnp.arange(n_blocks) * MOE_BLOCK, side='right'),
                            0, N_EXPERTS - 1)

    def expert_block(args):
        xb, e = args
        a = jnp.dot(xb, w_gate[e])
        u = jnp.dot(xb, w_up[e])
        return jnp.dot(jax.nn.silu(a) * u, w_down[e])
    ys = lax.map(expert_block, (xs.reshape(n_blocks, MOE_BLOCK, d), block_expert)).reshape(rows, d)
    y = jnp.zeros((n, d), jnp.float32).at[tok_s].add(ys[dest].astype(jnp.float32) * w_s[:, None])
    return y.astype(h.dtype)

def trunk_layer(layer, x, xc, c, c_ctx, rope_hd, rope_diff, w_mod, b_mod, norm1_g, norm2_g,
                w_in, ret_decay_logit, ret_norm_g, gqa_qnorm_g, gqa_knorm_g, hgrn_lower_bound,
                hgrn_norm_g, diff_lambda, diff_norm_g, w_out, router_w, router_bias,
                moe_w_gate, moe_w_up, moe_w_down, need_ctx):
    b, t, d = x.shape
    mod = jnp.dot(jax.nn.silu(c), w_mod) + b_mod
    mod_c = jnp.dot(jax.nn.silu(c_ctx), w_mod) + b_mod
    sh1, sc1, g1, sh2, sc2, g2 = jnp.split(mod[:, None, :], 6, axis=-1)
    sh1c, sc1c, g1c, sh2c, sc2c, g2c = jnp.split(mod_c, 6, axis=-1)

    h = modulate(rms_norm(x, norm1_g), sh1, sc1)
    hc = modulate(rms_norm(xc, norm1_g), sh1c, sc1c)
    p = split_columns(jnp.dot(h, w_in))
    pc = split_columns(jnp.dot(hc, w_in))
    lambda_init = 0.8 - 0.6 * math.exp(-0.3 * layer)
    o_ret, oc_ret = retention_mixer(p[0:4], pc[0:4], ret_decay_logit, ret_norm_g, rope_hd, need_ctx)
    o_gqa, oc_gqa = gqa_mixer(p[4:7], pc[4:7], gqa_qnorm_g, gqa_knorm_g, rope_hd, need_ctx)
    o_hg, oc_hg = hgrn2_mixer(p[7:12], pc[7:12], hgrn_lower_bound, hgrn_norm_g, need_ctx)
    o_df, oc_df = diff_mixer(p[12:15], pc[12:15], diff_lambda, diff_norm_g, lambda_init,
                             rope_diff, need_ctx)
    x = x + g1 * jnp.dot(jnp.concatenate([o_ret, o_gqa, o_hg, o_df], axis=-1), w_out)
    h2 = modulate(rms_norm(x, norm2_g), sh2, sc2).reshape(b * t, d)
    if not need_ctx:
        y = routed_moe(h2, router_w, router_bias, moe_w_gate, moe_w_up, moe_w_down)
        return x + g2 * y.reshape(b, t, d), xc
    xc = xc + g1c * jnp.dot(jnp.concatenate([oc_ret, oc_gqa, oc_hg, oc_df], axis=-1), w_out)
    h2c = modulate(rms_norm(xc, norm2_g), sh2c, sc2c).reshape(-1, d)
    y = routed_moe(jnp.concatenate([h2, h2c], axis=0), router_w, router_bias,
                   moe_w_gate, moe_w_up, moe_w_down)
    x = x + g2 * y[:b * t].reshape(b, t, d)
    xc = xc + g2c * y[b * t:].reshape(xc.shape)
    return x, xc

def setup_inputs(seed: int = 0) -> dict:
    key = jax.random.key(seed)
    ks = jax.random.split(key, 24)

    def nrm(k, shape, s):
        return jax.random.normal(k, shape, jnp.float32) * s
    gamma = 1.0 - jnp.exp2(-5.0 - jnp.arange(GROUP_HEADS, dtype=jnp.float32))
    ret_logit = jnp.log(gamma) - jnp.log1p(-gamma)
    return {
        'x': nrm(ks[0], (BATCH, SEQ, D_MODEL), 1.0),
        'c': nrm(ks[1], (BATCH, D_MODEL), 1.0),
        'ctx': nrm(ks[2], (BATCH, CTX_LEN, D_MODEL), 1.0),
        'c_ctx': nrm(ks[3], (D_MODEL,), 1.0),
        'w_mod': nrm(ks[4], (DEPTH, D_MODEL, 6 * D_MODEL), 0.5 * D_MODEL ** -0.5),
        'b_mod': nrm(ks[5], (DEPTH, 6 * D_MODEL), 0.01),
        'norm1_g': 1.0 + nrm(ks[6], (DEPTH, D_MODEL), 0.02),
        'norm2_g': 1.0 + nrm(ks[7], (DEPTH, D_MODEL), 0.02),
        'w_in': nrm(ks[8], (DEPTH, D_MODEL, IN_WIDTH), D_MODEL ** -0.5),
        'ret_decay_logit': ret_logit + nrm(ks[9], (DEPTH, 2, GROUP_HEADS), 0.1),
        'ret_norm_g': 1.0 + nrm(ks[10], (DEPTH, HEAD_DIM), 0.02),
        'gqa_qnorm_g': 1.0 + nrm(ks[11], (DEPTH, HEAD_DIM), 0.02),
        'gqa_knorm_g': 1.0 + nrm(ks[12], (DEPTH, HEAD_DIM), 0.02),
        'hgrn_lb_logit': nrm(ks[13], (2, DEPTH, GROUP_WIDTH), 0.5),
        'hgrn_norm_g': 1.0 + nrm(ks[14], (DEPTH, HEAD_DIM), 0.02),
        'diff_lambda': nrm(ks[15], (DEPTH, 4, DIFF_QK_DIM), 0.1),
        'diff_norm_g': 1.0 + nrm(ks[16], (DEPTH, HEAD_DIM), 0.02),
        'w_out': nrm(ks[17], (DEPTH, MIX_WIDTH, D_MODEL), MIX_WIDTH ** -0.5),
        'router_w': nrm(ks[18], (D_MODEL, N_EXPERTS), D_MODEL ** -0.5),
        'router_bias': nrm(ks[19], (N_EXPERTS,), 0.01),
        'moe_w_gate': nrm(ks[20], (DEPTH, N_EXPERTS, D_MODEL, EXPERT_FF), D_MODEL ** -0.5),
        'moe_w_up': nrm(ks[21], (DEPTH, N_EXPERTS, D_MODEL, EXPERT_FF), D_MODEL ** -0.5),
        'moe_w_down': nrm(ks[22], (DEPTH, N_EXPERTS, EXPERT_FF, D_MODEL), EXPERT_FF ** -0.5),
        'final_norm_g': 1.0 + nrm(ks[23], (D_MODEL,), 0.02),
    }

def reference(x, c, ctx, c_ctx, w_mod, b_mod, norm1_g, norm2_g, w_in, ret_decay_logit,
              ret_norm_g, gqa_qnorm_g, gqa_knorm_g, hgrn_lb_logit, hgrn_norm_g, diff_lambda,
              diff_norm_g, w_out, router_w, router_bias, moe_w_gate, moe_w_up, moe_w_down,
              final_norm_g):
    n_tokens = x.shape[1]
    rows = n_tokens // GRID_W
    rope_hd = axial_rope(rows, HEAD_DIM)
    rope_diff = axial_rope(rows, DIFF_QK_DIM)
    sm = jax.nn.softmax(hgrn_lb_logit.astype(jnp.float32), axis=1)
    lower_bounds = jnp.cumsum(sm, axis=1) - sm[:, :1]
    xc = ctx
    for layer in range(DEPTH):
        x, xc = trunk_layer(
            layer, x, xc, c, c_ctx, rope_hd, rope_diff, w_mod[layer], b_mod[layer],
            norm1_g[layer], norm2_g[layer], w_in[layer], ret_decay_logit[layer],
            ret_norm_g[layer], gqa_qnorm_g[layer], gqa_knorm_g[layer], lower_bounds[:, layer],
            hgrn_norm_g[layer], diff_lambda[layer], diff_norm_g[layer], w_out[layer],
            router_w, router_bias, moe_w_gate[layer], moe_w_up[layer], moe_w_down[layer],
            layer < DEPTH - 1)
    return rms_norm(x, final_norm_g)


_drawn_inputs = setup_inputs


def setup_inputs(seed=0):
    import zlib

    import numpy as np

    out = dict(_drawn_inputs(seed))
    spreads = {}
    factors = {'ret_norm_g': 15.663,
     'gqa_qnorm_g': 23.992,
     'gqa_knorm_g': 24.734,
     'diff_norm_g': 8.0,
     'final_norm_g': 24.869,
     'hgrn_lb_logit': 4.116,
     'hgrn_norm_g': 32.292,
     'norm2_g': 2.996}
    for name, (base, spread) in spreads.items():
        noise = np.random.default_rng([zlib.crc32(name.encode()), seed]).standard_normal(out[name].shape)
        drawn = base * np.exp(spread * noise) if base else spread * noise
        out[name] = jnp.asarray(drawn.astype(out[name].dtype))
    for name, factor in factors.items():
        out[name] = (out[name] * factor).astype(out[name].dtype)
    return out
```

```python
import math
from contextlib import ExitStack

import concourse.bass as bass
import numpy as np
from concourse import mybir

F32 = mybir.dt.float32
I32 = mybir.dt.int32
U8 = mybir.dt.uint8
ALU = mybir.AluOpType
ACT = mybir.ActivationFunctionType
AX_X = mybir.AxisListType.X

P = 128
D = 1024
KD = D // P
LAYERS = 2
SEG = 256
TOK = 2 * SEG
HD = 64
HEADS = 4
GRID_W = 64
E = 32
G = 8
FF = 512
EPS = 1e-6
NF = 21
VW = 896
RING = 6
UNITS_MOD, UNITS_IN, UNITS_OUT = 24, 14, 4
UNITS_DENSE = UNITS_MOD + UNITS_IN + UNITS_OUT
LEVELS = [0, 1, 2, 4, 8, 16, 32, 64]
ROPED = [0, 1, 2, 3, 6, 7, 8, 17, 18, 19, 20]
TINY = 2.0 ** -63
RQ, RK, RG, GQ, GK, HQ, ZF, ZB, HG, DQ, DK = 0, 2, 4, 6, 8, 9, 11, 13, 15, 17, 19
VCOL = {"ret": 0, "gqa": 256, "hg": 384, "df": 640}
MIXERS = ["ret", "gqa", "hg", "df"]
MIXROW = {"ret": 0, "gqa": 2, "hg": 4, "df": 6}
PER_LAYER = dict(
    mod_rows=12, h_ready=8, h2_ready=8, feat_ready=21, v_ready=8, gsq=3, geps=3,
    groot=3, gnorm=3, osb=6, oeps=6, oroot=6, osq=6, W_ready=16,
    roped=11, mixed=8, gates=4, fgate=4, flog=4, fg_free=4, qk=20,
    qk_arg=18, qk_exp=18, dec=16, dec_free=8, h_read=1, mix_read=1, x_mixed=1,
    mask=1, dest=1, idx=1, table=1, list_f=1, scores=1, y_all=1,
    x_done=1)
assert UNITS_DENSE % RING == 0


def max_blocks(n_tokens):
    return E + (2 * n_tokens) // (P + 1)


def token_tiles(layer):
    return [0, 1, 2, 3] if layer < LAYERS - 1 else [2, 3]


def segments(layer):
    return [0, 1] if layer < LAYERS - 1 else [1]


def plan_jobs():
    jobs = []
    for L in range(LAYERS):
        segs, tts = segments(L), token_tiles(L)
        for u in range(12):
            jobs.append((L, "mod", u))
            if u:
                jobs.append((L, "modT", u - 1))
        jobs.append((L, "modT", 11))
        jobs.append((L, "ss1"))
        jobs += [(L, "feat", f) for f in range(NF)]
        jobs += [(L, "v", half, t) for half in range(2) for t in range(4)]
        jobs += [(L, "gss", i) for i in range(3)]
        jobs += [(L, "rope", f) for f in ROPED]
        for j in range(2):
            for hh in range(2):
                jobs += [(L, "rs", 2 * j + hh, part) for part in ([0] if 0 in segs else []) + [1, 2]]
            jobs += [(L, "pv", "ret", j), (L, "oss", "ret", j)]
        for j in range(2):
            for hh in range(2):
                for i in tts:
                    jobs += [(L, "gs", 2 * j + hh, i), (L, "gt", 2 * j + hh, i)]
            jobs += [(L, "pv", "gqa", j)]
        for j in range(2):
            for lev in range(len(LEVELS)):
                jobs += [(L, "hl", j, lev, hh) for hh in range(2)]
            jobs += [(L, "hx", j, hh) for hh in range(2)]
            jobs += [(L, "hc", j, hh) for hh in range(2)]
            jobs += [(L, "pv", "hg", j), (L, "oss", "hg", j)]
        for j in range(2):
            for hh in range(2):
                for i in tts:
                    jobs += [(L, "ds", 2 * j + hh, 0, i), (L, "ds", 2 * j + hh, 1, i), (L, "dt", 2 * j + hh, i)]
            jobs += [(L, "pv", "df", j), (L, "oss", "df", j)]
        jobs += [(L, "out", f) for f in range(KD)]
        jobs.append((L, "ss2"))
        jobs.append((L, "router"))
        for i in range(len(tts)):
            jobs += [(L, "h2t", i, half) for half in range(2)]
        jobs += [(L, "pos"), (L, "list")]
        for i in range(len(tts)):
            jobs += [(L, "yt", i, half) for half in range(2)]
    jobs.append((LAYERS, "ssf"))
    return jobs


class Steps:

    def __init__(self, eng, own):
        self.eng, self.own, self.counts, self.open = eng, own, {}, {}

    def did(self, ins, sem=None):
        sem = self.own if sem is None else sem
        ins.then_inc(sem, 1)
        self.counts[id(sem)] = self.counts.get(id(sem), 0) + 1
        self.open[id(sem)] = (sem, self.counts[id(sem)])

    def settle(self):
        for sem, n in self.open.values():
            self.eng.wait_ge(sem, n)
        self.open = {}


def build_program(nc, A):
    jobs = plan_jobs()
    job_number = {key: n for n, key in enumerate(jobs)}

    with ExitStack() as ctx:
        def sb(name, shape, dt=F32):
            return ctx.enter_context(nc.sbuf_tensor(name, shape, dt))

        named = {}

        def sem(*name):
            name = "_".join(map(str, name))
            if name not in named:
                named[name] = ctx.enter_context(nc.semaphore(name))
            return named[name]

        mats = sb("mats", [P, 7, P])
        IDENT, HEAD_MEAN, ALL_MEAN, BEFORE, ONES, ROT_HD, ROT_DF = (mats[:, i, :] for i in range(7))
        mod_sel = sb("mod_sel", [P, 2])
        rope = sb("rope", [P, 4, SEG])
        dist = sb("dist", [P, 3, 2, SEG])
        eye2 = sb("eye2", [P, 2, SEG])
        later = sb("later", [P, 2, SEG], U8)
        levels = sb("levels", [P, len(LEVELS), P], U8)
        iota_e = sb("iota_e", [P, 4, 4])
        g_rank = sb("g_rank", [P, G])
        blk_iota = sb("blk_iota", [1, 40])
        tok_id = sb("tok_id", [P, 4], I32)
        cc = sb("cc", [P, KD, 2])
        ccs = sb("ccs", [P, KD, 32])
        b_mod = sb("b_mod", [P, LAYERS, 48])
        norm1 = sb("norm1", [P, LAYERS, KD])
        norm2 = sb("norm2", [P, LAYERS, KD])
        normf = sb("normf", [P, KD])
        head_g = sb("head_g", [P, 5, LAYERS])
        decay_logit = sb("decay_logit", [P, LAYERS, 2, HEADS])
        log_decay = sb("log_decay", [P, LAYERS, 2, HEADS])
        lb_logit = sb("lb_logit", [P, 2, LAYERS, 2])
        lb_soft = sb("lb_soft", [P, 2, LAYERS, 2])
        lb = sb("lb", [P, 2, LAYERS, 2])
        one_m_lb = sb("one_m_lb", [P, 2, LAYERS, 2])
        lb_tmp = sb("lb_tmp", [P, 2, 2, 2])
        lam_in = sb("lam_in", [P, LAYERS, 4, 32])
        lam_pr = sb("lam_pr", [P, LAYERS, 2, 32])
        lam_ex = sb("lam_ex", [P, LAYERS, 2])
        neg_lam = sb("neg_lam", [P, LAYERS])
        router_w = sb("router_w", [P, KD, E])
        router_b = sb("router_b", [P, E])
        ring = sb("ring", [P, RING, 4, 512])
        xT = sb("xT", [P, KD, TOK])
        hT = sb("hT", [P, KD, TOK])
        featT = sb("featT", [P, NF, TOK])
        vtok = sb("vtok", [P, 4, VW])
        Wst = sb("Wst", [P, 2, 6, SEG])
        modT = sb("modT", [P, 48, 2])
        mod_rows = sb("mod_rows", [P, 2, 512])
        mscale = sb("mscale", [P, 2, KD, 2])
        sq = sb("sq", [P, 2, TOK])
        rs = sb("rs", [P, TOK])
        rot = sb("rot", [P, SEG])
        scratch = sb("scratch", [P, 8 * TOK])
        dec = scratch[:, 0:3 * TOK].rearrange("p (a b t) -> p a b t", a=3, b=2)
        prob = scratch[:, 0:2 * TOK].rearrange("p (a t) -> p a t", a=2)
        fg = scratch[:, 0:TOK]
        qk = scratch[:, TOK:5 * TOK].rearrange("p (b a t) -> p b a t", b=2, a=2)
        hn = scratch[:, 5 * TOK:7 * TOK].rearrange("p (a t) -> p a t", a=2)
        osb = scratch[:, 7 * TOK:8 * TOK]
        cum = sb("cum", [P, 2, 2, SEG + 1])
        stat = sb("stat", [P, 2, 4])
        def room(at, width, dt=F32):
            flat = featT[:, :, :].rearrange("p f t -> p (f t)")[:, at:at + width]
            return flat if dt == F32 else flat.bitcast(dt)
        h2tok = room(0, 1024)
        xg = room(1024, 1024)
        xgT = room(2048, 1024).rearrange("p (k t) -> p k t", k=KD)
        sg = room(3072, 512)
        hm = room(3584, 512)
        hmT = room(4096, 512).rearrange("p (k t) -> p k t", k=4)
        ysb = room(4608, 1024)
        y0 = room(5632, 1024)
        y1 = room(6656, 1024)
        sc = sb("sc", [P, 4, E])
        sel = sb("sel", [P, 4, E])
        cmp1 = room(7680, 512)
        cmp2 = room(8192, 512)
        gsc = sb("gsc", [P, 4, G])
        gbest = sb("gbest", [P, 4, 2])
        goh = sb("goh", [P, 4, G])
        mask = sb("mask", [P, 4, E])
        gate = sb("gate", [P, 4, E])
        gsum = sb("gsum", [P, 4, 2])
        posn = room(9984, 4 * E).rearrange("p (a e) -> p a e", e=E)
        cnt = sb("cnt", [P, E])
        nblk = room(10240, 4 * E).rearrange("p (a e) -> p a e", e=E)
        blk_end = sb("blk_end", [P, E])
        row0 = sb("row0", [P, E])
        dst = room(10112, 4 * E).rearrange("p (a e) -> p a e", e=E)
        dd = sb("dd", [P, 4, 2])
        gk = sb("gk", [P, 4, 2])
        be_cmp = room(8704, 40 * E)
        be = sb("be", [1, 48])
        be_i = sb("be_i", [1, 48], I32)
        lst_i = room(10368, P, I32)
        lst_f = room(10496, P)
        idx = sb("idx", [P, 40], I32)
        idx_now = sb("idx_now", [P, 1], I32)
        dti2 = [sb(f"rows_of_token_{L}", [P, 8], I32) for L in range(LAYERS)]
        zero_i = sb("zero_i", [40, P], I32)

        banks = [ctx.enter_context(nc.psum_tensor(f"bank{i}", [P, 512], F32)) for i in range(8)]
        dram = {}
        for L in range(LAYERS):
            nt = len(token_tiles(L)) * P
            nb = max_blocks(nt)
            dram[L] = dict(
                h2=nc.dram_tensor(f"h2_{L}", (nt, D), F32, kind="Internal").ap(),
                list=nc.dram_tensor(f"list_{L}", (nb * P, 1), I32, kind="Internal").ap(),
                y=nc.dram_tensor(f"y_{L}", (nb * P, D), F32, kind="Internal").ap(), nb=nb)

        unit0 = [0]
        for L in range(LAYERS):
            unit0.append(unit0[-1] + UNITS_DENSE + dram[L]["nb"] * 6)
        landed = [sem("landed", i) for i in range(RING)]
        used = [sem("used", i) for i in range(RING)]
        full = [sem("bank_full", i) for i in range(8)]
        free = [sem("bank_free", i) for i in range(8)]

        def bank(key):
            return banks[job_number[key] % 8]

        def wait_full(eng, key):
            n = job_number[key]
            eng.wait_ge(full[n % 8], n // 8 + 1)

        def free_sem(key):
            return free[job_number[key] % 8]

        def unit(n):
            return ring[:, n % RING, :, :]

        def wvalid(b, n):
            return b < n

        def load_dense(sp, L, u0, u1):
            for u in range(u0, u1):
                n = unit0[L] + u
                if u < UNITS_MOD:
                    src, c, k = A["w_mod"], u // 2, u % 2
                elif u < UNITS_MOD + UNITS_IN:
                    src, c, k = A["w_in"], (u - UNITS_MOD) // 2, u % 2
                else:
                    src, c, k = A["w_out"], (u - UNITS_MOD - UNITS_IN) // 2, u % 2
                if n >= RING:
                    sp.wait_ge(used[n % RING], n // RING)
                sp.dma_start(unit(n), src[L].rearrange("(k p) n -> p k n", p=P)[:, 4 * k:4 * k + 4, 512 * c:512 * c + 512]
                             ).then_inc(landed[n % RING], 16)

        def release_after(pe, key, units):
            wait_full(pe, key)
            for n in units:
                pe.sem_inc(used[n % RING], 1)

        block = ctx.enter_context(nc.Block())

        @block.sync
        def _(sp):
            small = [
                (mats[:, :, :], A["k_mats"]), (mod_sel[:, :], A["k_mod_sel"]), (rope[:, :, :], A["k_rope"]),
                (dist[:, :, :, :], A["k_dist"]), (eye2[:, :, :], A["k_eye2"]), (scratch[:, 0:TOK].bitcast(I32), A["k_later"]),
                (scratch[:, TOK:TOK + len(LEVELS) * P].bitcast(I32), A["k_levels"]), (iota_e[:, :, :], A["k_before4"]), (g_rank[:, :], A["k_grank"]),
                (blk_iota[:, :], A["k_blk"]), (tok_id[:, :], A["k_tok"]), (b_mod[:, :, :], A["b_mod"]),
                (norm1[:, :, :], A["norm1"]), (norm2[:, :, :], A["norm2"]), (normf[:, :], A["normf"]),
                (head_g[:, :, :], A["head_g"]),
                (decay_logit[:, :, :, :], A["decay"].partition_broadcast(P)),
                (lb_logit[:, :, :, :], A["lb_logit"]),
                (lam_in[:, :, :, :], A["lam"].partition_broadcast(P)),
                (router_w[:, :, :], A["router_w"]),
                (router_b[:, :], A["router_b"].partition_broadcast(P)),
                (zero_i[:, :], A["k_zero"]),
            ]
            sp.dma_start(cc[:, :, :], A["cc"]).then_inc(sem("cc_in"), 16)
            for n, src in enumerate(small):
                if n == 0:
                    load_dense(sp, 0, 0, 4)
                sp.dma_start(src[0], src[1]).then_inc(sem("small_in"), 16)
            sp.dma_start(xT[:, :, :], A["xT"]).then_inc(sem("x_in"), 16)
            sp.wait_ge(sem("small_in"), 16 * len(small))
            sp.sem_inc(sem("small_ready"), 1)
            for L in range(LAYERS):
                load_dense(sp, L, 4 if L == 0 else 0, UNITS_DENSE)
                d = dram[L]
                sp.wait_ge(sem("table"), L * PER_LAYER["table"] + 1)
                n = sp.value_load(be_i[0:1, 40:41], min_val=1, max_val=d["nb"])
                base = (unit0[L] + UNITS_DENSE) // RING
                with sp.Fori(0, d["nb"]) as b:
                    with sp.If(b < n):
                        e = sp.value_load(be_i[0:1, bass.ds(b, 1)], min_val=0, max_val=E - 1)
                        for i in range(6):
                            sp.wait_ge(used[i], b + base)
                            src = [A["w_gate"], A["w_up"], A["w_down"]][i // 2]
                            rows = src[L, bass.ds(e, 1), :, :].rearrange("o a b -> (o a) b")
                            if i < 4:
                                rows = rows.rearrange("(k p) n -> p k n", p=P)[:, 4 * (i % 2):4 * (i % 2) + 4, :]
                            else:
                                rows = rows.rearrange("(k p) n -> p k n", p=P)[:, :, 512 * (i % 2):512 * (i % 2) + 512]
                            sp.dma_start(ring[:, i, :, :], rows).then_inc(landed[i], 16)
                    with sp.Else():
                        for i in range(6):
                            sp.wait_ge(landed[i], (b + base) * 16)
                            sp.sem_inc(landed[i], 16)
            sp.wait_ge(sem("final"), KD)
            sp.dma_start(A["outT"], hT[:, :, SEG:TOK]).then_inc(sem("out_stored"), 16)
            sp.wait_ge(sem("out_stored"), 16)

        @block.tensor
        def _(pe):
            order = iter(jobs)

            def begin(*key):
                assert next(order) == key, key
                n = job_number[key]
                if n >= 8:
                    pe.wait_ge(free[n % 8], n // 8)
                return banks[n % 8]

            def end(ins, key):
                ins.then_inc(full[job_number[key] % 8], 1)

            def arrived(n):
                pe.wait_ge(landed[n % RING], 16 * (n // RING + 1))

            def mm(out, lhsT, rhs, start, stop, **kw):
                return pe.matmul(out, lhsT, rhs, start=start, stop=stop, skip_group_check=True, **kw)

            pe.wait_ge(sem("cc_silu"), 1)
            pe.wait_ge(sem("small_ready"), 1)
            for L in range(LAYERS):
                segs, tts = segments(L), token_tiles(L)
                lo = 0 if 0 in segs else SEG

                def mod_turn(u):
                    ps = begin(L, "modT", u)
                    pe.wait_ge(sem("mod_rows"), L * PER_LAYER["mod_rows"] + u + 1)
                    for q in range(4):
                        ins = mm(ps[:, 2 * q:2 * q + 2], mod_rows[:, u % 2, q * P:(q + 1) * P], mod_sel[:, :], True, True)
                    end(ins, (L, "modT", u))

                for u in range(12):
                    ps = begin(L, "mod", u)
                    n = unit0[L] + 2 * u
                    arrived(n)
                    arrived(n + 1)
                    for half in range(2):
                        for q in range(4):
                            ins = mm(ps[32 * q:32 * q + 32, :], ccs[:, 4 * half + q, :], unit(n + half)[:, q, :],
                                     half == 0, half == 1, tile_position=(0, 32 * q))
                        if half == 0:
                            ins.then_inc(used[n % RING], 1)
                    end(ins, (L, "mod", u))
                    pe.wait_ge(full[job_number[(L, "mod", u)] % 8], job_number[(L, "mod", u)] // 8 + 1)
                    pe.sem_inc(used[(n + 1) % RING], 1)
                    if u:
                        mod_turn(u - 1)
                mod_turn(11)

                def mean_squares(name, gain_of_sum, count):
                    ps = begin(L, name)
                    for k in range(KD):
                        pe.wait_ge(sem(name, "sq", L), k + 1)
                        ins = mm(ps[:, 0:TOK], ALL_MEAN, sq[:, k % 2, :], k == 0, k == KD - 1)
                        if k < KD - 1:
                            ins.then_inc(sem(name, "sq_read", L), 1)
                    end(ins, (L, name))

                if L == 0:
                    pe.wait_ge(sem("x_in"), 16)
                mean_squares("ss1", None, None)

                base = unit0[L] + UNITS_MOD
                pe.wait_ge(sem("h_ready"), L * PER_LAYER["h_ready"] + KD)
                for f in range(NF):
                    n = base + 2 * (f // 4)
                    ps = begin(L, "feat", f)
                    q_lo = lo if f in (RQ, RQ + 1, RG, RG + 1, GQ, GQ + 1, HQ, HQ + 1, HG, HG + 1, DQ, DQ + 1) else 0
                    if f % 4 == 0:
                        arrived(n)
                        arrived(n + 1)
                    for k in range(KD):
                        ins = mm(ps[:, q_lo:TOK], unit(n + k // 4)[:, k % 4, (f % 4) * P:(f % 4) * P + P], hT[:, k, q_lo:TOK],
                                 k == 0, k == KD - 1)
                    end(ins, (L, "feat", f))
                    if f % 4 == 3:
                        release_after(pe, (L, "feat", f), [n, n + 1])
                for half in range(2):
                    n = base + 10 + 2 * half
                    c0, w = (P, 384) if half == 0 else (0, 512)
                    if half == 1:
                        arrived(n)
                        arrived(n + 1)
                    for t in range(4):
                        ps = begin(L, "v", half, t)
                        for k in range(KD):
                            ins = mm(ps[:, 0:w], hT[:, k, t * P:(t + 1) * P], unit(n + k // 4)[:, k % 4, c0:c0 + w],
                                     k == 0, k == KD - 1)
                        end(ins, (L, "v", half, t))
                    release_after(pe, (L, "v", half, 3), [n, n + 1])
                pe.sem_inc(sem("h_read"), 1)

                for i in range(3):
                    ps = begin(L, "gss", i)
                    pe.wait_ge(sem("gsq"), L * PER_LAYER["gsq"] + i + 1)
                    end(mm(ps[:, :], HEAD_MEAN, sq[:, i % 2, :], True, True), (L, "gss", i))
                for f in ROPED:
                    ps = begin(L, "rope", f)
                    if f in (GQ, GQ + 1, GK):
                        pe.wait_ge(sem("gnorm"), L * PER_LAYER["gnorm"] + f - GQ + 1)
                    else:
                        pe.wait_ge(sem("feat_ready"), L * PER_LAYER["feat_ready"] + f + 1)
                    end(mm(ps[:, 0:SEG], ROT_HD if f < DQ else ROT_DF, featT[:, f, SEG:TOK], True, True), (L, "rope", f))

                def value_product(mixer, j):
                    ps = begin(L, "pv", mixer, j)
                    for hh in range(2):
                        pe.wait_ge(sem("W_ready"), L * PER_LAYER["W_ready"] + 1 + hh + 2 * j + 4 * MIXERS.index(mixer))
                        vh = j if mixer == "gqa" else 2 * j + hh
                        vc = VCOL[mixer] + HD * vh
                        for g in segs:
                            parts = [(0, 0), (1, 1)] if g == 0 else [(2, 0), (3, 1), (4, 2), (5, 3)]
                            for n, (w, t) in enumerate(parts):
                                ins = mm(ps[HD * hh:HD * hh + HD, g * SEG:(g + 1) * SEG], vtok[:, t, vc:vc + HD],
                                         Wst[:, hh, w, :], n == 0, n == len(parts) - 1, tile_position=(0, HD * hh))
                    end(ins, (L, "pv", mixer, j))

                def head_mean(mixer, j):
                    ps = begin(L, "oss", mixer, j)
                    pe.wait_ge(sem("osq"), L * PER_LAYER["osq"] + 1 + j + 2 * ["ret", "hg", "df"].index(mixer))
                    end(mm(ps[:, lo:TOK], HEAD_MEAN, sq[:, 0, lo:TOK], True, True), (L, "oss", mixer, j))

                pe.wait_ge(sem("roped"), L * PER_LAYER["roped"] + len(ROPED))
                for j in range(2):
                    for hh in range(2):
                        r = slice(HD * hh, HD * hh + HD)
                        for part in ([0] if 0 in segs else []) + [1, 2]:
                            ps = begin(L, "rs", 2 * j + hh, part)
                            t0 = 0 if part == 0 else SEG
                            s0 = SEG if part == 2 else 0
                            for s in range(2):
                                ins = mm(ps[:, s * SEG:(s + 1) * SEG], featT[r, RK + j, s0 + s * P:s0 + s * P + P],
                                         featT[r, RQ + j, t0:t0 + SEG], True, True)
                            end(ins, (L, "rs", 2 * j + hh, part))
                    value_product("ret", j)
                    head_mean("ret", j)
                for j in range(2):
                    for hh in range(2):
                        h = 2 * j + hh
                        r = slice(HD * j, HD * j + HD)
                        for i in tts:
                            keys = TOK if i >= 2 else SEG
                            ps = begin(L, "gs", h, i)
                            end(mm(ps[:, 0:keys], featT[r, GQ + hh, i * P:(i + 1) * P], featT[r, GK, 0:keys], True, True),
                                (L, "gs", h, i))
                            ps = begin(L, "gt", h, i)
                            pe.wait_ge(sem("prob", L), 1 + tts.index(i) + len(tts) * h)
                            for s in range(keys // P):
                                ins = pe.transpose(ps[:, s * P:(s + 1) * P], prob[:, 0, s * P:(s + 1) * P], IDENT)
                            end(ins, (L, "gt", h, i))
                    value_product("gqa", j)
                for j in range(2):
                    for lev in range(len(LEVELS)):
                        m = j * 10 + lev
                        pe.wait_ge(sem("qk"), L * PER_LAYER["qk"] + m + 1)
                        for hh in range(2):
                            r = slice(HD * hh, HD * hh + HD)
                            ps = begin(L, "hl", j, lev, hh)
                            for t in tts:
                                ins = mm(ps[:, t * P:(t + 1) * P], qk[r, m % 2, 1, t * P:(t + 1) * P],
                                         qk[r, m % 2, 0, t * P:(t + 1) * P], True, True)
                            end(ins, (L, "hl", j, lev, hh))
                    m = j * 10 + 8
                    pe.wait_ge(sem("qk"), L * PER_LAYER["qk"] + m + 1)
                    for hh in range(2):
                        r = slice(HD * hh, HD * hh + HD)
                        ps = begin(L, "hx", j, hh)
                        for t in tts:
                            s = t ^ 1
                            ins = mm(ps[:, t * P:(t + 1) * P], qk[r, m % 2, 1, s * P:(s + 1) * P],
                                     qk[r, m % 2, 0, t * P:(t + 1) * P], True, True)
                        end(ins, (L, "hx", j, hh))
                    m = j * 10 + 9
                    pe.wait_ge(sem("qk"), L * PER_LAYER["qk"] + m + 1)
                    for hh in range(2):
                        r = slice(HD * hh, HD * hh + HD)
                        ps = begin(L, "hc", j, hh)
                        for s in range(2):
                            for dr in range(2):
                                ins = mm(ps[:, s * SEG:(s + 1) * SEG],
                                         qk[r, m % 2, 1, dr * SEG + s * P:dr * SEG + s * P + P],
                                         qk[r, m % 2, 0, dr * SEG:(dr + 1) * SEG], dr == 0, dr == 1)
                        end(ins, (L, "hc", j, hh))
                    value_product("hg", j)
                    head_mean("hg", j)
                for j in range(2):
                    for hh in range(2):
                        h = 2 * j + hh
                        for i in tts:
                            keys = TOK if i >= 2 else SEG
                            for m in range(2):
                                r = slice(HD * hh + 32 * m, HD * hh + 32 * m + 32)
                                ps = begin(L, "ds", h, m, i)
                                end(mm(ps[:, 0:keys], featT[r, DQ + j, i * P:(i + 1) * P], featT[r, DK + j, 0:keys], True, True,
                                       tile_position=(HD * hh + 32 * m, 0)), (L, "ds", h, m, i))
                            ps = begin(L, "dt", h, i)
                            pe.wait_ge(sem("dprob", L), 1 + tts.index(i) + len(tts) * h)
                            for s in range(keys // P):
                                ins = pe.transpose(ps[:, s * P:(s + 1) * P], prob[:, 0, s * P:(s + 1) * P], IDENT)
                            end(ins, (L, "dt", h, i))
                    value_product("df", j)
                    head_mean("df", j)

                base = unit0[L] + UNITS_MOD + UNITS_IN
                pe.wait_ge(sem("mixed"), L * PER_LAYER["mixed"] + 8)
                for f in range(KD):
                    n = base + 2 * (f // 4)
                    if f % 4 == 0:
                        arrived(n)
                        arrived(n + 1)
                    ps = begin(L, "out", f)
                    for k in range(KD):
                        ins = mm(ps[:, lo:TOK], unit(n + k // 4)[:, k % 4, (f % 4) * P:(f % 4) * P + P], hT[:, k, lo:TOK],
                                 k == 0, k == KD - 1)
                    end(ins, (L, "out", f))
                    if f % 4 == 3:
                        release_after(pe, (L, "out", f), [n, n + 1])
                pe.sem_inc(sem("mix_read"), 1)
                mean_squares("ss2", None, None)

                pe.wait_ge(sem("h2_ready"), L * PER_LAYER["h2_ready"] + KD)
                ps = begin(L, "router")
                for i, t in enumerate(tts):
                    for k in range(KD):
                        ins = mm(ps[:, i * E:(i + 1) * E], hT[:, k, t * P:(t + 1) * P], router_w[:, k, :],
                                 k == 0, k == KD - 1)
                end(ins, (L, "router"))
                for i, t in enumerate(tts):
                    for half in range(2):
                        ps = begin(L, "h2t", i, half)
                        for q in range(4):
                            ins = pe.transpose(ps[:, q * P:(q + 1) * P], hT[:, 4 * half + q, t * P:(t + 1) * P], IDENT)
                        end(ins, (L, "h2t", i, half))
                ps = begin(L, "pos")
                pe.wait_ge(sem("mask"), L * PER_LAYER["mask"] + 1)
                for i in range(len(tts)):
                    for i2 in range(i + 1):
                        ins = mm(ps[:, i * E:(i + 1) * E], BEFORE if i2 == i else ONES, mask[:, i2, :], i2 == 0, i2 == i)
                for i2 in range(len(tts)):
                    ins = mm(ps[:, P:P + E], ONES, mask[:, i2, :], i2 == 0, i2 == len(tts) - 1)
                end(ins, (L, "pos"))
                ps = begin(L, "list")
                pe.wait_ge(sem("list_f"), L * PER_LAYER["list_f"] + 1)
                nb = dram[L]["nb"]
                end(pe.transpose(ps[:, 0:nb], lst_f[0:nb, :], IDENT[0:nb, 0:nb]), (L, "list"))

                for b in range(8):
                    done = sum(1 for x in range(job_number[(L, "list")] + 1) if x % 8 == b)
                    pe.wait_ge(free[b], done)
                pe.wait_ge(sem("table"), L * PER_LAYER["table"] + 1)
                n = pe.value_load(be_i[0:1, 40:41], min_val=1, max_val=nb)
                base = (unit0[L] + UNITS_DENSE) // RING

                def turn_rows(b):
                    pe.wait_ge(sem("gathered", L), (b + 1) * 16)
                    for k in range(KD):
                        ins = pe.transpose(banks[k // 4][:, (k % 4) * P:(k % 4) * P + P], xg[:, k * P:(k + 1) * P], IDENT)
                    ins.then_inc(sem("turned", L), 1)

                pe.sem_inc(sem("turned", L), 1)
                pe.sem_inc(sem("hm_turned", L), 1)
                turn_rows(0)
                with pe.Fori(0, nb) as b:
                    with pe.If(b < n):
                        pe.wait_ge(sem("xgT", L), b + 1)
                        pe.wait_ge(sem("xgT2", L), b + 1)
                        for w in range(2):
                            for half in range(2):
                                pe.wait_ge(landed[2 * w + half], (b + base) * 16 + 16)
                                for q in range(4):
                                    ins = mm(banks[2 + w][:, :], xgT[:, 4 * half + q, :], ring[:, 2 * w + half, q, :],
                                             half == 0 and q == 0, half == 1 and q == 3)
                                ins.then_inc(used[2 * w + half], 1)
                        with pe.If(b + 1 < n):
                            turn_rows(b + 1)
                        pe.wait_ge(sem("hm", L), b + 2)
                        if True:
                            for q in range(4):
                                ins = pe.transpose(banks[4][:, q * P:(q + 1) * P], hm[:, q * P:(q + 1) * P], IDENT)
                            ins.then_inc(sem("hm_turned", L), 1)
                        pe.wait_ge(sem("hmT", L), b + 1)
                        for c in range(2):
                            pe.wait_ge(landed[4 + c], (b + base) * 16 + 16)
                            pe.wait_ge(sem("y_read", c, L), b + 1)
                            for q in range(4):
                                ins = mm(banks[5 + c][:, :], hmT[:, q, :], ring[:, 4 + c, q, :], q == 0, q == 3)
                            ins.then_inc(used[4 + c], 1)
                    with pe.Else():
                        for i in range(6):
                            pe.wait_ge(used[i], b + base)
                            pe.sem_inc(used[i], 1)
                for i in range(len(tts)):
                    for half in range(2):
                        ps = begin(L, "yt", i, half)
                        pe.wait_ge(sem("y_tok", L), i + 1)
                        for q in range(4):
                            ins = pe.transpose(ps[:, q * P:(q + 1) * P], y0[:, (4 * half + q) * P:(4 * half + q + 1) * P], IDENT)
                        end(ins, (L, "yt", i, half))

            L = LAYERS
            ps = begin(L, "ssf")
            for k in range(KD):
                pe.wait_ge(sem("ssf", "sq", L), k + 1)
                ins = mm(ps[:, SEG:TOK], ALL_MEAN, sq[:, k % 2, SEG:TOK], k == 0, k == KD - 1)
                if k < KD - 1:
                    ins.then_inc(sem("ssf", "sq_read", L), 1)
            end(ins, (L, "ssf"))

        @block.scalar
        def _(act):
            st = Steps(act, sem("act_steps"))

            def evac(key, out, in_, func=ACT.Copy, done=None, **kw):
                wait_full(act, key)
                st.did(act.activation(out, in_, func, **kw), done)
                st.settle()
                act.sem_inc(free_sem(key), 1)

            act.wait_ge(sem("cc_in"), 16)
            act.wait_ge(sem("ccs_zero"), 1)
            st.did(act.activation(ccs[:, :, 0:2], cc[:, :, :], ACT.Silu), sem("cc_silu"))
            act.wait_ge(sem("small_ready"), 1)
            flat = lambda ap: ap.rearrange("p a b c -> p (a b c)")
            st.did(act.activation(flat(log_decay[:, :, :, :]), flat(decay_logit[:, :, :, :]), ACT.Sigmoid), sem("decay_sig"))
            act.wait_ge(sem("lb_sub"), 1)
            st.did(act.activation(flat(lb_soft[:, :, :, :]), flat(lb_soft[:, :, :, :]), ACT.Exp), sem("lb_exp"))
            act.wait_ge(sem("lam_sum"), 1)
            st.did(act.activation(lam_ex[:, :, :].rearrange("p a b -> p (a b)"),
                                  lam_ex[:, :, :].rearrange("p a b -> p (a b)"), ACT.Exp), sem("lam_exp"))
            act.wait_ge(sem("decay_max"), 1)
            st.did(act.activation(flat(log_decay[:, :, :, :]), flat(log_decay[:, :, :, :]), ACT.Ln), sem("decay_ready"))

            def squares(L, name, lo):
                for k in range(KD):
                    if k >= 2:
                        act.wait_ge(sem(name, "sq_read", L), k - 1)
                    st.did(act.activation(sq[:, k % 2, lo:TOK], xT[:, k, lo:TOK], ACT.Square), sem(name, "sq", L))

            def root(L, name, lo):
                act.wait_ge(sem(name, "eps", L), 1)
                st.did(act.activation(rs[:, lo:TOK], rs[:, lo:TOK], ACT.Sqrt), sem(name, "root", L))

            for L in range(LAYERS):
                segs, tts = segments(L), token_tiles(L)
                lo = 0 if 0 in segs else SEG
                for u in range(12):
                    if u >= 2:
                        wait_full(act, (L, "modT", u - 2))
                    elif L:
                        wait_full(act, (L - 1, "modT", 10 + u))
                    evac((L, "mod", u), mod_rows[:, u % 2, :], bank((L, "mod", u))[:, :], done=sem("mod_rows"))
                if L == 0:
                    act.wait_ge(sem("x_in"), 16)
                else:
                    act.wait_ge(sem("x_done"), (L - 1) * PER_LAYER["x_done"] + 1)
                squares(L, "ss1", 0)
                root(L, "ss1", 0)
                for f in range(NF):
                    q_lo = lo if f in (RQ, RQ + 1, RG, RG + 1, GQ, GQ + 1, HQ, HQ + 1, HG, HG + 1, DQ, DQ + 1) else 0
                    func = ACT.Silu if f in (RG, RG + 1, HG, HG + 1) else ACT.Copy
                    evac((L, "feat", f), featT[:, f, q_lo:TOK], bank((L, "feat", f))[:, q_lo:TOK], func, sem("feat_ready"))
                for half in range(2):
                    c0, w = (0, 384) if half == 0 else (384, 512)
                    for t in range(4):
                        evac((L, "v", half, t), vtok[:, t, c0:c0 + w], bank((L, "v", half, t))[:, 0:w], done=sem("v_ready"))
                for i in range(3):
                    q_lo = lo if i < 2 else 0
                    if i >= 2:
                        wait_full(act, (L, "gss", i - 2))
                    st.did(act.activation(sq[:, i % 2, :], featT[:, GQ + i, :], ACT.Square), sem("gsq"))
                for i in range(3):
                    act.wait_ge(sem("geps"), L * PER_LAYER["geps"] + i + 1)
                    st.did(act.activation(rs[:, :], rs[:, :], ACT.Sqrt), sem("groot"))

                def osquares(mixer, j):
                    act.wait_ge(sem("osb"), L * PER_LAYER["osb"] + 1 + j + 2 * ["ret", "hg", "df"].index(mixer))
                    st.did(act.activation(sq[:, 0, lo:TOK], osb[:, lo:TOK], ACT.Square), sem("osq"))
                    act.wait_ge(sem("oeps"), L * PER_LAYER["oeps"] + 1 + j + 2 * ["ret", "hg", "df"].index(mixer))
                    st.did(act.activation(rs[:, lo:TOK], rs[:, lo:TOK], ACT.Sqrt), sem("oroot"))

                if L == 0:
                    act.wait_ge(sem("decay_ready"), 1)
                for j in range(2):
                    for hh in range(2):
                        h = 2 * j + hh
                        act.wait_ge(sem("dec_free"), L * PER_LAYER["dec_free"] + 2 * h + 1)
                        for n, (dr, table) in enumerate([(0, 0), (1, 0)]):
                            st.did(act.activation(dec[:, n, :, :].rearrange("p b t -> p (b t)"),
                                                  dist[:, table, :, :].rearrange("p b t -> p (b t)"), ACT.Exp,
                                                  scale=log_decay[:, L, dr, h:h + 1]), sem("dec"))
                        act.wait_ge(sem("dec_free"), L * PER_LAYER["dec_free"] + 2 * h + 2)
                        for n, (dr, table) in enumerate([(0, 1), (1, 2)]):
                            st.did(act.activation(dec[:, 1 + n, :, :].rearrange("p b t -> p (b t)"),
                                                  dist[:, table, :, :].rearrange("p b t -> p (b t)"), ACT.Exp,
                                                  scale=log_decay[:, L, dr, h:h + 1]), sem("dec"))
                    osquares("ret", j)
                n = 0
                for h in range(HEADS):
                    for i in tts:
                        keys = TOK if i >= 2 else SEG
                        act.wait_ge(sem("gmax", L), n + 1)
                        if n:
                            act.wait_ge(sem("gt_copied", L), n)
                        st.did(act.activation(prob[:, 0, 0:keys], bank((L, "gs", h, i))[:, 0:keys], ACT.Exp,
                                              bias=stat[:, 0, 1:2], scale=HD ** -0.5, accum_out=stat[:, 0, 2:3]), sem("gexp", L))
                        st.settle()
                        act.sem_inc(free_sem((L, "gs", h, i)), 1)
                        n += 1
                for j in range(2):
                    for dr in range(2):
                        z = featT[:, (ZF, ZB)[dr] + j, :]
                        act.wait_ge(sem("fg_free"), L * PER_LAYER["fg_free"] + 2 * j + dr + 1)
                        st.did(act.activation(fg, z, ACT.Sigmoid))
                        st.settle()
                        st.did(act.activation(z, z, ACT.Sigmoid, scale=-1.0), sem("gates"))
                        act.wait_ge(sem("fgate"), L * PER_LAYER["fgate"] + 2 * j + dr + 1)
                        st.did(act.activation(fg, fg, ACT.Ln), sem("flog"))
                    for lev in range(1, 10):
                        m = j * 10 + lev
                        act.wait_ge(sem("qk_arg"), L * PER_LAYER["qk_arg"] + j * 9 + lev)
                        st.did(act.activation(qk[:, m % 2, :, :].rearrange("p a t -> p (a t)"),
                                              qk[:, m % 2, :, :].rearrange("p a t -> p (a t)"), ACT.Exp), sem("qk_exp"))
                    osquares("hg", j)
                n = 0
                for h in range(HEADS):
                    for i in tts:
                        keys = TOK if i >= 2 else SEG
                        for m in range(2):
                            act.wait_ge(sem("dmax", L), 2 * n + m + 1)
                            if n:
                                act.wait_ge(sem("dt_copied", L), n)
                            elif m == 0:
                                pass
                            st.did(act.activation(prob[:, m, 0:keys], bank((L, "ds", h, m, i))[:, 0:keys], ACT.Exp,
                                                  bias=stat[:, m, 1:2], scale=32 ** -0.5, accum_out=stat[:, m, 2:3]),
                                   sem("dexp", L))
                            st.settle()
                            act.sem_inc(free_sem((L, "ds", h, m, i)), 1)
                        n += 1
                    if h % 2:
                        osquares("df", h // 2)
                act.wait_ge(sem("x_mixed"), L * PER_LAYER["x_mixed"] + 1)
                squares(L, "ss2", lo)
                root(L, "ss2", lo)
                evac((L, "router"), sc[:, 0:len(tts), :].rearrange("p a e -> p (a e)"),
                     bank((L, "router"))[:, 0:len(tts) * E], ACT.Sigmoid, sem("scores"))
                for i in range(len(tts)):
                    if i:
                        act.wait_ge(sem("h2_stored", L), 16 * i)
                    for half in range(2):
                        evac((L, "h2t", i, half), h2tok[:, 512 * half:512 * half + 512], bank((L, "h2t", i, half))[:, :])
                    act.dma_start(dram[L]["h2"][i * P:(i + 1) * P, :], h2tok).then_inc(sem("h2_stored", L), 16)
                act.wait_ge(sem("table"), L * PER_LAYER["table"] + 1)
                nb = dram[L]["nb"]
                n = act.value_load(be_i[0:1, 40:41], min_val=1, max_val=nb)
                base = (unit0[L] + UNITS_DENSE) // RING

                def copy_rows(b, sems):
                    act.wait_ge(sem("turned", L), b + 2)
                    act.activation(xgT[:, 0:4, :].rearrange("p k t -> p (k t)"), banks[0][:, :], ACT.Copy
                                   ).then_inc(sem("xgT", L), 1)

                act.sem_inc(sem("y_read", 0, L), 1)
                act.sem_inc(sem("y_stored", L), 16)
                copy_rows(0, None)
                act.wait_ge(sem("h2_stored", L), 16 * len(tts))
                with act.Fori(0, nb) as b:
                    with act.If(b < n):
                        act.wait_ge(used[1], b + base + 1)
                        act.wait_ge(sem("hm", L), b + 1)
                        act.activation(sg, banks[2][:, :], ACT.Silu).then_inc(sem("sg", L), 1)
                        with act.If(b + 1 < n):
                            act.wait_ge(used[3], b + base + 1)
                            copy_rows(b + 1, None)
                        act.wait_ge(used[4], b + base + 1)
                        act.wait_ge(sem("y_stored", L), b * 16 + 16)
                        act.activation(ysb[:, 0:512], banks[5][:, :], ACT.Copy).then_inc(sem("y_read", 0, L), 1)
                        act.wait_ge(sem("y_read", 0, L), b + 2)
                        act.wait_ge(sem("y_read", 1, L), b + 2)
                        act.dma_start(dram[L]["y"][bass.ds(b * P, P), :], ysb).then_inc(sem("y_stored", L), 16)
                    with act.Else():
                        act.wait_ge(sem("y_stored", L), b * 16 + 16)
                        act.dma_start(dram[L]["y"][bass.ds(b * P, P), :], ysb).then_inc(sem("y_stored", L), 16)
                act.wait_ge(sem("y_stored", L), nb * 16 + 16)
                act.sem_inc(sem("y_all"), 1)
            L = LAYERS
            act.wait_ge(sem("x_done"), (L - 1) * PER_LAYER["x_done"] + 1)
            squares(L, "ssf", SEG)
            root(L, "ssf", SEG)

        @block.gpsimd
        def _(pool):
            pool.wait_ge(sem("small_ready"), 1)
            for L in range(LAYERS):
                d = dram[L]
                pool.dma_start(d["list"].rearrange("(b p) o -> b (p o)", p=P), zero_i[0:d["nb"], :]
                               ).then_inc(sem("list_zero", L), 16)
            for L in range(LAYERS):
                d, tts = dram[L], token_tiles(L)
                pool.wait_ge(sem("list_zero", L), 16)
                pool.wait_ge(sem("dest"), L * PER_LAYER["dest"] + 1)
                for i in range(len(tts)):
                    for k in range(2):
                        pool.indirect_dma_start(d["list"], bass.IndirectOffsetOnAxis(dti2[L][:, 2 * i + k:2 * i + k + 1], 0),
                                                tok_id[:, i:i + 1], None).then_inc(sem("listed", L), 16)
                pool.wait_ge(sem("listed", L), 32 * len(tts))
                pool.dma_start(lst_i[0:d["nb"], :], d["list"].rearrange("(b p) o -> b (p o)", p=P)
                               ).then_inc(sem("list_back", L), 16)
                pool.wait_ge(sem("h2_stored", L), 16 * len(tts))
                pool.wait_ge(sem("idx"), L * PER_LAYER["idx"] + 1)
                n = pool.value_load(be_i[0:1, 40:41], min_val=1, max_val=d["nb"])
                with pool.Fori(0, d["nb"]) as b:
                    with pool.If(b < n):
                        pool.wait_ge(sem("turned", L), b + 1)
                        pool.wait_ge(sem("idx_col", L), b + 1)
                        pool.sem_inc(sem("gather_turn"), 1)
                        pool.indirect_dma_start(xg, None, d["h2"], bass.IndirectOffsetOnAxis(idx_now[:, 0:1], 0)
                                                ).then_inc(sem("gathered", L), 16)
                pool.wait_ge(sem("y_all"), L * PER_LAYER["y_all"] + 1)
                for i in range(len(tts)):
                    if i:
                        pool.wait_ge(sem("y_tok_read", L), i)
                    for k, y in enumerate((y0, y1)):
                        pool.indirect_dma_start(y, None, d["y"], bass.IndirectOffsetOnAxis(dti2[L][:, 2 * i + k:2 * i + k + 1], 0)
                                                ).then_inc(sem("y_gathered", L), 16)

        @block.vector
        def _(dve):
            st = Steps(dve, sem("dve_steps"))
            did, settle = st.did, st.settle

            def release(key):
                settle()
                dve.sem_inc(free_sem(key), 1)

            did(dve.memset(ccs[:, :, :], 0.0), sem("ccs_zero"))
            did(dve.memset(cum[:, :, :, :], 0.0))
            did(dve.memset(featT[:, :, :], 0.0))
            dve.wait_ge(sem("small_ready"), 1)
            did(dve.tensor_copy(later[:, :, :].rearrange("p a t -> p (a t)"), scratch[:, 0:TOK].bitcast(I32)))
            did(dve.tensor_copy(levels[:, :, :].rearrange("p a t -> p (a t)"),
                                scratch[:, TOK:TOK + len(LEVELS) * P].bitcast(I32)))
            settle()
            l0, l1 = lb_logit[:, :, 0, :], lb_logit[:, :, 1, :]
            did(dve.tensor_tensor(lb_tmp[:, 0, :, :], l0, l1, ALU.max))
            settle()
            did(dve.tensor_tensor(lb_soft[:, :, 0, :], l0, lb_tmp[:, 0, :, :], ALU.subtract))
            did(dve.tensor_tensor(lb_soft[:, :, 1, :], l1, lb_tmp[:, 0, :, :], ALU.subtract))
            settle()
            dve.sem_inc(sem("lb_sub"), 1)
            did(dve.tensor_tensor(lam_pr[:, :, 0, :], lam_in[:, :, 0, :], lam_in[:, :, 1, :], ALU.mult))
            did(dve.tensor_tensor(lam_pr[:, :, 1, :], lam_in[:, :, 2, :], lam_in[:, :, 3, :], ALU.mult))
            settle()
            did(dve.tensor_reduce(lam_ex[:, :, :], lam_pr[:, :, :, :], AX_X, ALU.add), sem("lam_sum"))
            dve.wait_ge(sem("decay_sig"), 1)
            ld = log_decay[:, :, :, :].rearrange("p a b c -> p (a b c)")
            did(dve.tensor_scalar(ld, ld, TINY, None, ALU.max), sem("decay_max"))
            dve.wait_ge(sem("lb_exp"), 1)
            e0, e1 = lb_soft[:, :, 0, :], lb_soft[:, :, 1, :]
            did(dve.tensor_tensor(lb_tmp[:, 0, :, :], e0, e1, ALU.add))
            settle()
            did(dve.reciprocal(lb_tmp[:, 1, :, :], lb_tmp[:, 0, :, :]))
            settle()
            did(dve.tensor_tensor(e0, e0, lb_tmp[:, 1, :, :], ALU.mult))
            did(dve.tensor_tensor(e1, e1, lb_tmp[:, 1, :, :], ALU.mult))
            settle()
            did(dve.tensor_tensor(lb[:, :, 0, :], e0, e0, ALU.subtract))
            did(dve.tensor_tensor(lb_tmp[:, 0, :, :], e0, e1, ALU.add))
            settle()
            did(dve.tensor_tensor(lb[:, :, 1, :], lb_tmp[:, 0, :, :], e0, ALU.subtract))
            settle()
            did(dve.tensor_scalar(one_m_lb[:, :, :, :].rearrange("p a b c -> p (a b c)"),
                                  lb[:, :, :, :].rearrange("p a b c -> p (a b c)"), -1.0, 1.0, ALU.mult, ALU.add))
            dve.wait_ge(sem("lam_exp"), 1)
            did(dve.tensor_tensor(neg_lam[:, :], lam_ex[:, :, 1], lam_ex[:, :, 0], ALU.subtract))
            settle()
            for L in range(LAYERS):
                init = 0.8 - 0.6 * math.exp(-0.3 * L)
                did(dve.tensor_scalar(neg_lam[:, L:L + 1], neg_lam[:, L:L + 1], -init, None, ALU.add))
                did(dve.tensor_scalar(head_g[:, 4, L:L + 1], head_g[:, 4, L:L + 1], 1 - init, None, ALU.mult))
            settle()

            def inverse_root(L, name, lo):
                key = (L, name)
                wait_full(dve, key)
                did(dve.tensor_scalar(rs[:, lo:TOK], bank(key)[:, lo:TOK], EPS, None, ALU.add), sem(name, "eps", L))
                release(key)
                dve.wait_ge(sem(name, "root", L), 1)
                did(dve.reciprocal(rs[:, lo:TOK], rs[:, lo:TOK]))
                settle()

            def modulated(L, which, segs, lo, ready):
                for k in range(KD):
                    if k >= 2:
                        pass
                    did(dve.tensor_tensor(hn[:, k % 2, lo:TOK], xT[:, k, lo:TOK], rs[:, lo:TOK], ALU.mult))
                    settle()
                    for g in segs:
                        c = 1 - g
                        ins = dve.tensor_scalar(hT[:, k, g * SEG:(g + 1) * SEG], hn[:, k % 2, g * SEG:(g + 1) * SEG],
                                                mscale[:, which, k, c:c + 1], modT[:, 24 * which + k, c:c + 1], ALU.mult, ALU.add)
                        did(ins)
                    settle()
                    dve.sem_inc(ready, 1)

            for L in range(LAYERS):
                segs, tts = segments(L), token_tiles(L)
                lo = 0 if 0 in segs else SEG
                for u in range(12):
                    key = (L, "modT", u)
                    wait_full(dve, key)
                    did(dve.tensor_tensor(modT[:, 4 * u:4 * u + 4, :],
                                          bank(key)[:, 0:8].rearrange("p (a c) -> p a c", c=2),
                                          b_mod[:, L, 4 * u:4 * u + 4].unsqueeze(2).to_broadcast([P, 4, 2]), ALU.add))
                    release(key)
                for which, g_in in enumerate((norm1, norm2)):
                    did(dve.tensor_scalar(mscale[:, which, :, :].rearrange("p a b -> p (a b)"),
                                          modT[:, 24 * which + 8:24 * which + 16, :].rearrange("p a b -> p (a b)"),
                                          1.0, None, ALU.add))
                    settle()
                    did(dve.tensor_tensor(mscale[:, which, :, :], mscale[:, which, :, :],
                                          g_in[:, L, :].unsqueeze(2).to_broadcast([P, KD, 2]), ALU.mult))
                settle()
                inverse_root(L, "ss1", 0)
                modulated(L, 0, [0, 1], 0, sem("h_ready"))

                for i in range(3):
                    key = (L, "gss", i)
                    wait_full(dve, key)
                    dve.wait_ge(sem("feat_ready"), L * PER_LAYER["feat_ready"] + NF)
                    did(dve.tensor_scalar(rs[:, :], bank(key)[:, :], EPS, None, ALU.add), sem("geps"))
                    release(key)
                    dve.wait_ge(sem("groot"), L * PER_LAYER["groot"] + i + 1)
                    did(dve.reciprocal(rs[:, :], rs[:, :]))
                    settle()
                    f = featT[:, GQ + i, :]
                    did(dve.scalar_tensor_tensor(out=f, in0=f, scalar=head_g[:, 1 + i // 2, L:L + 1], in1=rs[:, :],
                                                 op0=ALU.mult, op1=ALU.mult), sem("gnorm"))
                    settle()
                for f in ROPED:
                    key = (L, "rope", f)
                    wait_full(dve, key)
                    cs = 0 if f < DQ else 2
                    x = featT[:, f, SEG:TOK]
                    did(dve.tensor_tensor(rot[:, :], bank(key)[:, 0:SEG], rope[:, cs + 1, :], ALU.mult))
                    did(dve.tensor_tensor(x, x, rope[:, cs, :], ALU.mult))
                    release(key)
                    did(dve.tensor_tensor(x, x, rot[:, :], ALU.add), sem("roped"))
                    settle()

                def readout(mixer, j):
                    key = (L, "pv", mixer, j)
                    out = hT[:, MIXROW[mixer] + j, lo:TOK]
                    wait_full(dve, key)
                    if mixer == "gqa":
                        did(dve.tensor_copy(out, bank(key)[:, lo:TOK]))
                        release(key)
                        dve.sem_inc(sem("mixed"), 1)
                        return
                    did(dve.tensor_copy(osb[:, lo:TOK], bank(key)[:, lo:TOK]), sem("osb"))
                    release(key)
                    key = (L, "oss", mixer, j)
                    n = 1 + j + 2 * ["ret", "hg", "df"].index(mixer)
                    wait_full(dve, key)
                    did(dve.tensor_scalar(rs[:, lo:TOK], bank(key)[:, lo:TOK], EPS, None, ALU.add), sem("oeps"))
                    release(key)
                    dve.wait_ge(sem("oroot"), L * PER_LAYER["oroot"] + n)
                    did(dve.reciprocal(rs[:, lo:TOK], rs[:, lo:TOK]))
                    settle()
                    g = head_g[:, {"ret": 0, "hg": 3, "df": 4}[mixer], L:L + 1]
                    did(dve.scalar_tensor_tensor(out=out, in0=osb[:, lo:TOK], scalar=g, in1=rs[:, lo:TOK],
                                                 op0=ALU.mult, op1=ALU.mult))
                    settle()
                    if mixer != "df":
                        silu_g = featT[:, {"ret": RG, "hg": HG}[mixer] + j, lo:TOK]
                        did(dve.tensor_tensor(out, out, silu_g, ALU.mult))
                        settle()
                    dve.sem_inc(sem("mixed"), 1)

                dve.wait_ge(sem("v_ready"), L * PER_LAYER["v_ready"] + 8)
                dve.wait_ge(sem("h_read"), L * PER_LAYER["h_read"] + 1)
                dve.sem_inc(sem("dec_free"), 1)
                for j in range(2):
                    for hh in range(2):
                        h = 2 * j + hh
                        dve.wait_ge(sem("dec"), L * PER_LAYER["dec"] + 4 * h + 2)
                        own = dec[:, 0, :, :]
                        did(dve.copy_predicated(own, later[:, :, :], dec[:, 1, :, :]))
                        settle()
                        did(dve.tensor_tensor(own, own, eye2[:, :, :], ALU.add))
                        settle()
                        dve.sem_inc(sem("dec_free"), 1)
                        for part in ([0] if 0 in segs else []) + [2]:
                            key = (L, "rs", h, part)
                            if part == 2:
                                cross = (L, "rs", h, 1)
                                dve.wait_ge(sem("dec"), L * PER_LAYER["dec"] + 4 * h + 4)
                                did(dve.tensor_tensor(dec[:, 1, :, :], dec[:, 1, :, :], dec[:, 2, :, :], ALU.add))
                                settle()
                                wait_full(dve, cross)
                                did(dve.scalar_tensor_tensor(out=Wst[:, hh, 2:4, :],
                                                             in0=bank(cross)[:, :].rearrange("p (a t) -> p a t", a=2),
                                                             scalar=HD ** -0.5, in1=dec[:, 1, :, :], op0=ALU.mult, op1=ALU.mult))
                                release(cross)
                            wait_full(dve, key)
                            w = 0 if part == 0 else 4
                            did(dve.scalar_tensor_tensor(out=Wst[:, hh, w:w + 2, :],
                                                         in0=bank(key)[:, :].rearrange("p (a t) -> p a t", a=2),
                                                         scalar=HD ** -0.5, in1=own, op0=ALU.mult, op1=ALU.mult))
                            release(key)
                        dve.sem_inc(sem("W_ready"), 1)
                        if h < 3:
                            dve.sem_inc(sem("dec_free"), 1)
                    readout("ret", j)

                def softmax_stats(key, m, keys, scale, done):
                    wait_full(dve, key)
                    did(dve.tensor_reduce(stat[:, m, 0:1], bank(key)[:, 0:keys], AX_X, ALU.max))
                    settle()
                    did(dve.tensor_scalar(stat[:, m, 1:2], stat[:, m, 0:1], -scale, None, ALU.mult), done)

                def store_turned(key, hh, i, copied):
                    wait_full(dve, key)
                    w0, ns = (0, 2) if i < 2 else (2, 4)
                    c0 = (i % 2) * P
                    did(dve.tensor_copy(Wst[:, hh, w0:w0 + ns, c0:c0 + P],
                                        bank(key)[:, 0:ns * P].rearrange("p (a t) -> p a t", a=ns)), copied)
                    release(key)

                n = 0
                for h in range(HEADS):
                    for i in tts:
                        keys = TOK if i >= 2 else SEG
                        softmax_stats((L, "gs", h, i), 0, keys, HD ** -0.5, sem("gmax", L))
                        dve.wait_ge(sem("gexp", L), n + 1)
                        did(dve.reciprocal(stat[:, 0, 3:4], stat[:, 0, 2:3]))
                        settle()
                        did(dve.tensor_scalar(prob[:, 0, 0:keys], prob[:, 0, 0:keys], stat[:, 0, 3:4], None, ALU.mult),
                            sem("prob", L))
                        if i == tts[0] and h % 2 == 0 and h:
                            pass
                        store_turned((L, "gt", h, i), h % 2, i, sem("gt_copied", L))
                        n += 1
                    dve.sem_inc(sem("W_ready"), 1)
                    if h % 2:
                        readout("gqa", h // 2)

                for j in range(2):
                    q = featT[:, HQ + j, :]
                    kf, kb = featT[:, ZF + j, :], featT[:, ZB + j, :]
                    for dr in range(2):
                        z = (kf, kb)[dr]
                        dve.sem_inc(sem("fg_free"), 1)
                        dve.wait_ge(sem("gates"), L * PER_LAYER["gates"] + 2 * j + dr + 1)
                        did(dve.tensor_scalar(z, z, one_m_lb[:, dr, L, j:j + 1], None, ALU.mult))
                        did(dve.tensor_scalar(fg, fg, one_m_lb[:, dr, L, j:j + 1], lb[:, dr, L, j:j + 1], ALU.mult, ALU.add))
                        settle()
                        did(dve.tensor_scalar(fg, fg, TINY, None, ALU.max), sem("fgate"))
                        dve.wait_ge(sem("flog"), L * PER_LAYER["flog"] + 2 * j + dr + 1)
                        for g in range(2):
                            did(dve.tensor_tensor_scan(cum[:, dr, g, 1:SEG + 1], fg[:, g * SEG:(g + 1) * SEG],
                                                       fg[:, g * SEG:(g + 1) * SEG], 0.0, ALU.add, ALU.bypass))
                        settle()

                    def pieces(ap, h):
                        return ap.rearrange("p (b two h) -> p b two h", two=2, h=h)

                    def halves(m, h):
                        return pieces(qk[:, m % 2, 0, :], h), pieces(qk[:, m % 2, 1, :], h)

                    for lev in range(10):
                        m = j * 10 + lev
                        if m >= 2:
                            jj, ll = divmod(m - 2, 10)
                            for hh in range(2):
                                wait_full(dve, (L, "hl", jj, ll, hh) if ll < 8 else (L, ("hx", "hc")[ll - 8], jj, hh))
                        Q, K = qk[:, m % 2, 0, :], qk[:, m % 2, 1, :]
                        if lev == 0:
                            did(dve.tensor_copy(Q, q))
                            did(dve.tensor_tensor(K, kf, kb, ALU.add))
                        elif lev < 9:
                            h = LEVELS[lev] if lev < 8 else P
                            nb2 = SEG // (2 * h)
                            for g in range(2):
                                Qv = pieces(Q[:, g * SEG:(g + 1) * SEG], h)
                                Kv = pieces(K[:, g * SEG:(g + 1) * SEG], h)
                                incF = pieces(cum[:, 0, g, 1:SEG + 1], h)
                                excF = pieces(cum[:, 0, g, 0:SEG], h)
                                excB = pieces(cum[:, 1, g, 0:SEG], h)
                                midF = excF[:, :, 1, 0:1].to_broadcast([P, nb2, h])
                                midB = excB[:, :, 1, 0:1].to_broadcast([P, nb2, h])
                                did(dve.tensor_tensor(Qv[:, :, 1, :], incF[:, :, 1, :], midF, ALU.subtract))
                                did(dve.tensor_tensor(Kv[:, :, 0, :], midF, incF[:, :, 0, :], ALU.subtract))
                                did(dve.tensor_tensor(Qv[:, :, 0, :], midB, excB[:, :, 0, :], ALU.subtract))
                                did(dve.tensor_tensor(Kv[:, :, 1, :], excB[:, :, 1, :], midB, ALU.subtract))
                        else:
                            did(dve.tensor_copy(Q[:, 0:SEG], cum[:, 0, 1, 1:SEG + 1]))
                            did(dve.tensor_tensor(Q[:, SEG:TOK], cum[:, 1, 1, SEG:SEG + 1].to_broadcast([P, SEG]),
                                                  cum[:, 1, 1, 0:SEG], ALU.subtract))
                            did(dve.tensor_tensor(K[:, 0:SEG], cum[:, 0, 0, SEG:SEG + 1].to_broadcast([P, SEG]),
                                                  cum[:, 0, 0, 1:SEG + 1], ALU.subtract))
                            did(dve.tensor_copy(K[:, SEG:TOK], cum[:, 1, 0, 0:SEG]))
                        if lev:
                            settle()
                            dve.sem_inc(sem("qk_arg"), 1)
                            dve.wait_ge(sem("qk_exp"), L * PER_LAYER["qk_exp"] + j * 9 + lev)
                            if lev < 9:
                                h = LEVELS[lev] if lev < 8 else P
                                did(dve.tensor_tensor(Q, Q, q, ALU.mult))
                                Kv, kfv, kbv = pieces(K, h), pieces(kf, h), pieces(kb, h)
                                did(dve.tensor_tensor(Kv[:, :, 0, :], Kv[:, :, 0, :], kfv[:, :, 0, :], ALU.mult))
                                did(dve.tensor_tensor(Kv[:, :, 1, :], Kv[:, :, 1, :], kbv[:, :, 1, :], ALU.mult))
                            else:
                                did(dve.tensor_tensor(Q[:, 0:SEG], Q[:, 0:SEG], q[:, SEG:TOK], ALU.mult))
                                did(dve.tensor_tensor(Q[:, SEG:TOK], Q[:, SEG:TOK], q[:, SEG:TOK], ALU.mult))
                                did(dve.tensor_tensor(K[:, 0:SEG], K[:, 0:SEG], kf[:, 0:SEG], ALU.mult))
                                did(dve.tensor_tensor(K[:, SEG:TOK], K[:, SEG:TOK], kb[:, 0:SEG], ALU.mult))
                        settle()
                        dve.sem_inc(sem("qk"), 1)
                        for hh in range(2):
                            key = (L, "hl", j, lev, hh) if lev < 8 else (L, ("hx", "hc")[lev - 8], j, hh)
                            wait_full(dve, key)
                            ps = bank(key)
                            if lev < 8:
                                for t in tts:
                                    w = (0 if t < 2 else 4) + t % 2
                                    c0 = (t % 2) * P
                                    own = Wst[:, hh, w, c0:c0 + P]
                                    if lev == 0:
                                        did(dve.tensor_copy(own, ps[:, t * P:(t + 1) * P]))
                                    else:
                                        did(dve.copy_predicated(own, levels[:, lev, :], ps[:, t * P:(t + 1) * P]))
                            elif lev == 8:
                                for t in tts:
                                    w = (0 if t < 2 else 4) + (t ^ 1) % 2
                                    c0 = (t % 2) * P
                                    did(dve.tensor_copy(Wst[:, hh, w, c0:c0 + P], ps[:, t * P:(t + 1) * P]))
                            else:
                                did(dve.tensor_copy(Wst[:, hh, 2:4, :], ps[:, :].rearrange("p (a t) -> p a t", a=2)))
                            release(key)
                    dve.sem_inc(sem("W_ready"), 2)
                    readout("hg", j)

                n = 0
                for h in range(HEADS):
                    for i in tts:
                        keys = TOK if i >= 2 else SEG
                        for m in range(2):
                            softmax_stats((L, "ds", h, m, i), m, keys, 32 ** -0.5, sem("dmax", L))
                        dve.wait_ge(sem("dexp", L), 2 * n + 2)
                        for m in range(2):
                            did(dve.reciprocal(stat[:, m, 3:4], stat[:, m, 2:3]))
                        settle()
                        did(dve.tensor_scalar(stat[:, 1, 3:4], stat[:, 1, 3:4], neg_lam[:, L:L + 1], None, ALU.mult))
                        did(dve.tensor_scalar(prob[:, 0, 0:keys], prob[:, 0, 0:keys], stat[:, 0, 3:4], None, ALU.mult))
                        settle()
                        did(dve.scalar_tensor_tensor(out=prob[:, 0, 0:keys], in0=prob[:, 1, 0:keys], scalar=stat[:, 1, 3:4],
                                                     in1=prob[:, 0, 0:keys], op0=ALU.mult, op1=ALU.add), sem("dprob", L))
                        store_turned((L, "dt", h, i), h % 2, i, sem("dt_copied", L))
                        n += 1
                    dve.sem_inc(sem("W_ready"), 1)
                    if h % 2:
                        readout("df", h // 2)

                for f in range(KD):
                    key = (L, "out", f)
                    wait_full(dve, key)
                    for g in segs:
                        x = xT[:, f, g * SEG:(g + 1) * SEG]
                        did(dve.scalar_tensor_tensor(out=x, in0=bank(key)[:, g * SEG:(g + 1) * SEG],
                                                     scalar=modT[:, 16 + f, 1 - g:2 - g], in1=x, op0=ALU.mult, op1=ALU.add))
                    release(key)
                dve.sem_inc(sem("x_mixed"), 1)
                inverse_root(L, "ss2", lo)
                dve.wait_ge(sem("mix_read"), L * PER_LAYER["mix_read"] + 1)
                modulated(L, 1, segs, lo, sem("h2_ready"))

                nt, nb = len(tts), dram[L]["nb"]
                dve.wait_ge(sem("scores"), L * PER_LAYER["scores"] + 1)
                did(dve.tensor_tensor(sel[:, 0:nt, :], sc[:, 0:nt, :], router_b[:, :].unsqueeze(1).to_broadcast([P, nt, E]), ALU.add))
                settle()
                for i in range(nt):
                    s4 = sel[:, i, :].rearrange("p (g e) -> p g e", e=4)
                    of_j = s4.unsqueeze(2).to_broadcast([P, G, 4, 4])
                    of_e = s4.unsqueeze(3).to_broadcast([P, G, 4, 4])
                    c1 = cmp1[:, 0:P].rearrange("p (g e j) -> p g e j", e=4, j=4)
                    c2 = cmp1[:, P:2 * P].rearrange("p (g e j) -> p g e j", e=4, j=4)
                    did(dve.tensor_tensor(c1, of_j, of_e, ALU.is_gt))
                    did(dve.tensor_tensor(c2, of_j, of_e, ALU.is_equal))
                    settle()
                    did(dve.tensor_tensor(c2, c2, iota_e[:, :, :].unsqueeze(1).to_broadcast([P, G, 4, 4]), ALU.mult))
                    settle()
                    did(dve.tensor_tensor(c1, c1, c2, ALU.add))
                    settle()
                    m4 = mask[:, i, :].rearrange("p (g e) -> p g e", e=4)
                    did(dve.tensor_reduce(m4, c1, AX_X, ALU.add))
                    settle()
                    did(dve.tensor_scalar(mask[:, i, :], mask[:, i, :], 2.0, None, ALU.is_lt))
                    settle()
                    t4 = cmp2[:, 0:E].rearrange("p (g e) -> p g e", e=4)
                    did(dve.tensor_tensor(cmp2[:, 0:E], mask[:, i, :], sel[:, i, :], ALU.mult))
                    settle()
                    did(dve.tensor_reduce(gsc[:, i, :], t4, AX_X, ALU.add))
                    settle()
                    did(dve.tensor_reduce(gbest[:, i, 0:1], gsc[:, i, :], AX_X, ALU.max))
                    settle()
                    did(dve.scalar_tensor_tensor(out=goh[:, i, :], in0=gsc[:, i, :], scalar=gbest[:, i, 0:1], in1=g_rank[:, :],
                                                 op0=ALU.is_equal, op1=ALU.mult))
                    settle()
                    did(dve.tensor_reduce(gbest[:, i, 1:2], goh[:, i, :], AX_X, ALU.max))
                    settle()
                    did(dve.tensor_scalar(goh[:, i, :], goh[:, i, :], gbest[:, i, 1:2], None, ALU.is_equal))
                    settle()
                    did(dve.tensor_tensor(m4, m4, goh[:, i, :].unsqueeze(2).to_broadcast([P, G, 4]), ALU.mult))
                    settle()
                    did(dve.tensor_tensor(gate[:, i, :], sc[:, i, :], mask[:, i, :], ALU.mult))
                    settle()
                    did(dve.tensor_reduce(gsum[:, i, 0:1], gate[:, i, :], AX_X, ALU.add))
                    settle()
                    did(dve.reciprocal(gsum[:, i, 1:2], gsum[:, i, 0:1]))
                    settle()
                    did(dve.tensor_scalar(gate[:, i, :], gate[:, i, :], gsum[:, i, 1:2], None, ALU.mult))
                settle()
                dve.sem_inc(sem("mask"), 1)
                key = (L, "pos")
                wait_full(dve, key)
                did(dve.tensor_copy(posn[:, 0:nt, :].rearrange("p a e -> p (a e)"), bank(key)[:, 0:nt * E]))
                did(dve.tensor_copy(cnt[:, :], bank(key)[:, P:P + E]))
                release(key)
                for q in range(4):
                    did(dve.tensor_scalar(nblk[:, q, :], cnt[:, :], float(q * P), None, ALU.is_gt))
                settle()
                for q in range(1, 4):
                    did(dve.tensor_tensor(nblk[:, 0, :], nblk[:, 0, :], nblk[:, q, :], ALU.add))
                    settle()
                did(dve.tensor_tensor_scan(blk_end[:, :], nblk[:, 0, :], nblk[:, 0, :], 0.0, ALU.add, ALU.bypass))
                settle()
                did(dve.tensor_tensor(row0[:, :], blk_end[:, :], nblk[:, 0, :], ALU.subtract))
                cmpb = be_cmp[0:1, 0:nb * E].rearrange("p (b e) -> p b e", e=E)
                did(dve.tensor_tensor(cmpb, blk_end[0:1, :].unsqueeze(1).to_broadcast([1, nb, E]),
                                      blk_iota[0:1, 0:nb].unsqueeze(2).to_broadcast([1, nb, E]), ALU.is_le))
                settle()
                did(dve.tensor_reduce(be[0:1, 0:nb], cmpb, AX_X, ALU.add))
                settle()
                did(dve.tensor_scalar(be[0:1, 0:nb], be[0:1, 0:nb], float(E - 1), None, ALU.min))
                did(dve.tensor_copy(be[0:1, 40:41], blk_end[0:1, E - 1:E]))
                settle()
                did(dve.tensor_copy(be_i[0:1, 0:nb], be[0:1, 0:nb]))
                did(dve.tensor_copy(be_i[0:1, 40:41], be[0:1, 40:41]))
                settle()
                dve.sem_inc(sem("table"), 1)
                did(dve.tensor_scalar(row0[:, :], row0[:, :], float(P), 1.0, ALU.mult, ALU.add))
                settle()
                d_ = dst[:, 0:nt, :]
                did(dve.tensor_tensor(d_, posn[:, 0:nt, :], row0[:, :].unsqueeze(1).to_broadcast([P, nt, E]), ALU.add))
                settle()
                did(dve.tensor_tensor(d_, d_, mask[:, 0:nt, :], ALU.mult))
                settle()
                did(dve.tensor_reduce(dd[:, 0:nt, 1:2].rearrange("p a o -> p (a o)"), d_, AX_X, ALU.max))
                did(dve.tensor_reduce(dd[:, 0:nt, 0:1].rearrange("p a o -> p (a o)"), d_, AX_X, ALU.add))
                settle()
                did(dve.tensor_tensor(dd[:, 0:nt, 0:1], dd[:, 0:nt, 0:1], dd[:, 0:nt, 1:2], ALU.subtract))
                settle()
                for i in range(nt):
                    for k in range(2):
                        did(dve.scalar_tensor_tensor(out=cmp2[:, 0:E], in0=dst[:, i, :], scalar=dd[:, i, k:k + 1],
                                                     in1=gate[:, i, :], op0=ALU.is_equal, op1=ALU.mult))
                        settle()
                        did(dve.tensor_reduce(gk[:, i, k:k + 1], cmp2[:, 0:E], AX_X, ALU.add))
                        settle()
                did(dve.tensor_scalar(dd[:, 0:nt, :].rearrange("p a k -> p (a k)"), dd[:, 0:nt, :].rearrange("p a k -> p (a k)"),
                                      -1.0, None, ALU.add))
                settle()
                did(dve.tensor_copy(dti2[L][:, 0:2 * nt], dd[:, 0:nt, :].rearrange("p a k -> p (a k)")))
                settle()
                dve.sem_inc(sem("dest"), 1)
                dve.wait_ge(sem("list_back", L), 16)
                did(dve.tensor_copy(lst_f[0:nb, :], lst_i[0:nb, :]), sem("list_f"))
                key = (L, "list")
                wait_full(dve, key)
                did(dve.tensor_copy(idx[:, 0:nb], bank(key)[:, 0:nb]))
                release(key)
                dve.sem_inc(sem("idx"), 1)

                n = dve.value_load(be_i[0:1, 40:41], min_val=1, max_val=nb)
                base = (unit0[L] + UNITS_DENSE) // RING

                def copy_rows(b):
                    dve.wait_ge(sem("turned", L), b + 2)
                    dve.tensor_copy(xgT[:, 4:8, :].rearrange("p k t -> p (k t)"), banks[1][:, :]).then_inc(sem("xgT2", L), 1)

                def index_column(b):
                    dve.tensor_copy(idx_now[:, 0:1], idx[:, bass.ds(b, 1)]).then_inc(sem("idx_col", L), 1)

                dve.sem_inc(sem("hm", L), 1)
                dve.sem_inc(sem("y_read", 1, L), 1)
                index_column(0)
                copy_rows(0)
                with dve.Fori(0, nb) as b:
                    with dve.If(b < n):
                        with dve.If(b + 1 < n):
                            dve.wait_ge(sem("gathered", L), (b + 1) * 16)
                            index_column(b + 1)
                        dve.wait_ge(sem("sg", L), b + 1)
                        dve.wait_ge(used[3], b + base + 1)
                        dve.wait_ge(sem("hm_turned", L), b + 1)
                        dve.tensor_tensor(hm, sg, banks[3][:, :], ALU.mult).then_inc(sem("hm", L), 1)
                        dve.wait_ge(sem("hm_turned", L), b + 2)
                        dve.wait_ge(used[5], b + base)
                        dve.tensor_copy(hmT.rearrange("p k t -> p (k t)"), banks[4][:, :]).then_inc(sem("hmT", L), 1)
                        with dve.If(b + 1 < n):
                            copy_rows(b + 1)
                        dve.wait_ge(used[5], b + base + 1)
                        dve.wait_ge(sem("y_stored", L), b * 16 + 16)
                        dve.tensor_copy(ysb[:, 512:1024], banks[6][:, :]).then_inc(sem("y_read", 1, L), 1)
                for i, t in enumerate(tts):
                    dve.wait_ge(sem("y_gathered", L), 32 * (i + 1))
                    did(dve.tensor_scalar(y1, y1, gk[:, i, 1:2], None, ALU.mult))
                    settle()
                    did(dve.scalar_tensor_tensor(out=y0, in0=y0, scalar=gk[:, i, 0:1], in1=y1, op0=ALU.mult, op1=ALU.add),
                        sem("y_tok", L))
                    for half in range(2):
                        key = (L, "yt", i, half)
                        wait_full(dve, key)
                        for q in range(4):
                            k = 4 * half + q
                            x = xT[:, k, t * P:(t + 1) * P]
                            g = t // 2
                            did(dve.scalar_tensor_tensor(out=x, in0=bank(key)[:, q * P:(q + 1) * P],
                                                         scalar=modT[:, 40 + k, 1 - g:2 - g], in1=x, op0=ALU.mult, op1=ALU.add))
                        release(key)
                    dve.sem_inc(sem("y_tok_read", L), 1)
                dve.sem_inc(sem("x_done"), 1)
            L = LAYERS
            inverse_root(L, "ssf", SEG)
            for k in range(KD):
                did(dve.scalar_tensor_tensor(out=hT[:, k, SEG:TOK], in0=xT[:, k, SEG:TOK], scalar=normf[:, k:k + 1],
                                             in1=rs[:, SEG:TOK], op0=ALU.mult, op1=ALU.mult), sem("final"))


def constants():
    f = np.float32
    p = np.arange(P)
    same_head = (p[:, None] // HD == p[None, :] // HD).astype(f) / HD

    def rotation(d):
        r = np.zeros((P, P), f)
        for m in range(P):
            base, o = m // d * d, m % d
            if o < d // 2:
                r[base + o + d // 2, m] = -1
            else:
                r[base + o - d // 2, m] = 1
        return r

    mats = np.stack([np.eye(P, dtype=f), same_head, np.full((P, P), 1 / D, f),
                     (p[:, None] < p[None, :]).astype(f), np.ones((P, P), f), rotation(HD), rotation(HD // 2)], 1)

    def axial(d):
        n = d // 4
        inv = (np.float32(10000.0) ** (-np.arange(n, dtype=f) / f(n))).astype(f)
        t = np.arange(SEG)
        ang = np.concatenate([(t // GRID_W).astype(f)[:, None] * inv, (t % GRID_W).astype(f)[:, None] * inv], 1).astype(f)
        c = np.tile(np.cos(ang).astype(f).T, (2 * P // d, 1))
        s = np.tile(np.sin(ang).astype(f).T, (2 * P // d, 1))
        return c, s

    rope = np.stack([*axial(HD), *axial(HD // 2)], 1)
    s = (np.arange(2)[None, :, None] * P + p[:, None, None])
    t = np.arange(SEG)[None, None, :]
    dist = np.stack([np.abs(t - s), SEG + t - s, SEG - t + s], 1).astype(f)
    lev = np.zeros((P, len(LEVELS), P), np.uint8)
    for n, h in enumerate(LEVELS):
        if h:
            a, b = p[:, None], p[None, :]
            lev[:, n, :] = (a // (2 * h) == b // (2 * h)) & (a // h != b // h)
    return {
        "k_mats": mats, "k_mod_sel": (p[:, None] % 32 == np.arange(2)[None]).astype(f), "k_rope": rope.astype(f),
        "k_dist": dist, "k_eye2": (t == s).astype(f), "k_later": (s > t).astype(np.int32).reshape(P, TOK), "k_levels": lev.astype(np.int32).reshape(P, -1),
        "k_before4": np.broadcast_to((np.arange(4)[None, :] < np.arange(4)[:, None]).astype(f), (P, 4, 4)),
        "k_grank": np.broadcast_to((G - np.arange(G)).astype(f), (P, G)),
        "k_blk": np.arange(40, dtype=f)[None], "k_tok": (p[:, None] + P * np.arange(4)[None]).astype(np.int32),
        "k_zero": np.zeros((40, P), np.int32),
    }


def kernel(**inputs):
    import concourse.bacc as bacc
    from concourse.bass_utils import run_bass_kernel_spmd

    a = {k: np.asarray(v) for k, v in inputs.items()}

    def feature_major(v):
        return np.moveaxis(v.reshape(*v.shape[:-1], v.shape[-1] // P, P), -1, 0)

    w = a["w_in"]
    col = lambda i, n: w[:, :, i:i + n]
    gq = w[:, :, 1024:1280].reshape(LAYERS, D, 4, HD)[:, :, [0, 2, 1, 3], :].reshape(LAYERS, D, 256)
    w_in = np.concatenate([
        col(0, 256), col(256, 256), col(768, 256), gq, col(1280, 128),
        col(1536, 256), col(1792, 256), col(2048, 256), col(2560, 256), col(2816, 256), col(3072, 256),
        col(512, 256), col(1408, 128), col(2304, 256), col(3328, 256)], axis=2)
    both = np.concatenate([a["ctx"][0], a["x"][0]], 0)
    twice = lambda g: np.concatenate([g, g], 1).T
    arrays = {
        "xT": np.moveaxis(both.reshape(TOK, KD, P), -1, 0).transpose(0, 2, 1),
        "cc": np.stack([a["c"][0], a["c_ctx"]], -1).reshape(KD, P, 2).transpose(1, 0, 2),
        "w_mod": a["w_mod"], "w_in": w_in, "w_out": a["w_out"],
        "b_mod": feature_major(a["b_mod"]), "norm1": feature_major(a["norm1_g"]), "norm2": feature_major(a["norm2_g"]),
        "normf": feature_major(a["final_norm_g"]),
        "head_g": np.stack([twice(a[k]) for k in ("ret_norm_g", "gqa_qnorm_g", "gqa_knorm_g", "hgrn_norm_g", "diff_norm_g")], 1),
        "decay": a["ret_decay_logit"], "lb_logit": feature_major(a["hgrn_lb_logit"]), "lam": a["diff_lambda"],
        "router_w": a["router_w"].reshape(KD, P, E).transpose(1, 0, 2), "router_b": a["router_bias"],
        "w_gate": a["moe_w_gate"], "w_up": a["moe_w_up"], "w_down": a["moe_w_down"], **constants(),
    }
    arrays = {k: np.ascontiguousarray(v) for k, v in arrays.items()}
    nc = bacc.Bacc("TRN2", target_bir_lowering=False, num_devices=1)
    A = {k: nc.dram_tensor(f"in_{k}", v.shape, mybir.dt.from_np(v.dtype), kind="ExternalInput").ap() for k, v in arrays.items()}
    A["outT"] = nc.dram_tensor("out_T", (P, KD, SEG), F32, kind="ExternalOutput").ap()
    build_program(nc, A)
    r = run_bass_kernel_spmd(nc, [{f"in_{k}": v for k, v in arrays.items()}], core_ids=[0])
    out = r.results[0]["out_T"]
    return np.ascontiguousarray(out.transpose(2, 1, 0).reshape(1, SEG, D))
```

```python
import math
from contextlib import ExitStack

import concourse.bass as bass
import numpy as np
from concourse import mybir

F32 = mybir.dt.float32
I32 = mybir.dt.int32
U8 = mybir.dt.uint8
ALU = mybir.AluOpType
ACT = mybir.ActivationFunctionType
AX_X = mybir.AxisListType.X

P = 128
D = 1024
KD = D // P
LAYERS = 2
SEG = 256
TOK = 2 * SEG
HD = 64
HEADS = 4
GRID_W = 64
E = 32
G = 8
FF = 512
ROWS = 64
MAXB = 48
EPS = 1e-6
NF = 21
VW = 896
RING = 6
MOD_FIRST = 4
MOD_LATER = [(0, u) for u in range(MOD_FIRST, 12)] + [(1, u) for u in range(12)]
DENSE = [
    [("mod", 0, u) for u in range(MOD_FIRST)] + [("in", 0, i) for i in range(7)] + [("mod", *lu) for lu in MOD_LATER]
    + [("out", 0, i) for i in range(2)],
    [("in", 1, i) for i in range(7)] + [("out", 1, i) for i in range(2)],
]
LEVELS = [0, 1, 2, 4, 8, 16, 32, 64]
ROPED_FIRST, ROPED_LAST = [0, 1, 2, 3, 6, 7, 8], [17, 18, 19, 20]
ROPED = ROPED_FIRST + ROPED_LAST
TINY = 2.0 ** -63
RQ, RK, RG, GQ, GK, HQ, ZF, ZB, HG, DQ, DK = 0, 2, 4, 6, 8, 9, 11, 13, 15, 17, 19
QUERY_TILES = (RQ, RQ + 1, RG, RG + 1, GQ, GQ + 1, HQ, HQ + 1, HG, HG + 1, DQ, DQ + 1)
VCOL = {"ret": 0, "gqa": 256, "hg": 384, "df": 640}
MIXERS = ["ret", "gqa", "hg", "df"]
MAPS = {"gqa": 1, "df": 2}
LEVELS_ALL = 10
NORMED = [("ret", 0), ("ret", 1), ("hg", 0), ("hg", 1), ("df", 0), ("df", 1)]
MIXTILE = {"ret": RQ, "gqa": RK, "hg": HQ, "df": DQ}
PER_LAYER = dict(
    h_ready=8, h2_ready=8, feat_ready=21, v_ready=8, gsq=3, geps=3,
    groot=3, gnorm=3, osb=6, oeps=6, oroot=6, osq=6, W_ready=16,
    roped=11, mixed=8, gates=4, fgate=4, flog=4, fg_free=4, qk=20,
    qk_arg=18, qk_exp=18, dec=16, dec_free=8, mix_read=1, x_mixed=1,
    mask=1, dest=1, idx=1, table=1,  scores=1, y_all=1,
    x_done=1, one_hots=1, normed=6)
assert all(2 * len(d) % RING == 0 for d in DENSE)


def max_blocks(n_tokens):
    return E + (2 * n_tokens) // (ROWS + 1)


def token_tiles(layer):
    return [0, 1, 2, 3] if layer < LAYERS - 1 else [2, 3]


def segments(layer):
    return [0, 1] if layer < LAYERS - 1 else [1]


PROJ_FIRST = [("feat", f) for f in range(9)] + [("v", 0, t) for t in range(4)]
PROJ_BESIDE = [("feat", f) for f in range(9, 17)] + [("v", 1, t) for t in range(4)] + [("feat", f) for f in range(17, 21)]


def chunk_of(item):
    if item[0] == "v":
        return (2, P, 384) if item[1] == 0 else (5, 0, 512)
    f = item[1]
    if f < 9:
        return f // 4, f % 4 * P, P
    return (3 + (f - 9) // 4, (f - 9) % 4 * P, P) if f < 17 else (6, (f - 17) * P, P)


def last_of_chunk(item):
    items = PROJ_FIRST + PROJ_BESIDE
    at = items.index(item)
    return at + 1 == len(items) or chunk_of(items[at + 1])[0] != chunk_of(item)[0]


def first_of_chunk(item):
    items = PROJ_FIRST + PROJ_BESIDE
    at = items.index(item)
    return at == 0 or chunk_of(items[at - 1])[0] != chunk_of(item)[0]


def proj_beside(layer, hook):
    hooks = 4 + HEADS * len(token_tiles(layer)) + 2
    n = len(PROJ_BESIDE)
    return [x for k, x in enumerate(PROJ_BESIDE) if k * hooks // n == hook]


def mod_later(layer, step):
    if layer:
        return []
    jobs = [(MOD_LATER[step][0], "mod", MOD_LATER[step][1])]
    if step:
        jobs.append((MOD_LATER[step - 1][0], "modT", MOD_LATER[step - 1][1]))
    if step == len(MOD_LATER) - 1:
        jobs.append((MOD_LATER[step][0], "modT", MOD_LATER[step][1]))
    return jobs


def softmax_steps(L, name):
    pairs = HEADS * len(token_tiles(L))
    per = pairs // 2
    for n in range(pairs + 2):
        yield (n if n < pairs else None, n - 1 if 1 <= n <= pairs else None, n - 2 if n >= 2 else None,
               (n - 2) // per if n >= 2 and (n - 2) % per == per - 1 else None)


def softmax_pair(L, n):
    tts = token_tiles(L)
    return n // len(tts), tts[n % len(tts)]


def softmax_jobs(L, name):
    jobs = []
    for step, (made, _, turned, j) in enumerate(softmax_steps(L, name)):
        if made is not None:
            jobs += [(L, "s", name, m, made) for m in range(MAPS[name])]
        if turned is not None:
            jobs.append((L, "t", name, turned))
        if j is not None:
            jobs.append((L, "pv", name, j))
        if name == "gqa":
            jobs += [(L, *x) for x in proj_beside(L, 4 + step)]
    return jobs


def plan_jobs():
    jobs = []
    for L in range(LAYERS):
        segs, tts = segments(L), token_tiles(L)
        if L == 0:
            for u in range(MOD_FIRST):
                jobs += [(0, "mod", u), (0, "modT", u)]
        jobs.append((L, "ss1"))
        jobs += [(L, *x) for x in PROJ_FIRST]
        jobs += [(L, "gss", i) for i in range(3)]
        jobs += [(L, "rope", f) for f in ROPED_FIRST]
        for j in range(2):
            for hh in range(2):
                jobs += [(L, "rs", 2 * j + hh, part) for part in ([0] if 0 in segs else []) + [1, 2]]
                jobs += [(L, *x) for x in proj_beside(L, 2 * j + hh)]
            jobs += [(L, "pv", "ret", j)]
        jobs += softmax_jobs(L, "gqa")
        for j in range(2):
            for lev in range(LEVELS_ALL + 1):
                if lev < LEVELS_ALL:
                    jobs += [(L, "hl", j, lev, hh) for hh in range(2)] + mod_later(L, j * LEVELS_ALL + lev)
            jobs += [(L, "pv", "hg", j)]
        jobs += [(L, "rope", f) for f in ROPED_LAST]
        jobs += softmax_jobs(L, "df")
        jobs += [(L, "oss", x) for x in range(len(NORMED))]
        jobs += [(L, "out", f) for f in range(KD)]
        jobs.append((L, "ss2"))
        jobs.append((L, "router"))
        for i in range(len(tts)):
            jobs += [(L, "h2t", i, half) for half in range(2)]
        jobs += [(L, "pos"), (L, "idx")]
        for i in range(len(tts)):
            jobs += [(L, "yt", i, half) for half in range(2)]
    jobs.append((LAYERS, "ssf"))
    return jobs


class Steps:

    def __init__(self, eng, own):
        self.eng, self.own, self.counts, self.open = eng, own, {}, {}

    def did(self, ins, sem=None):
        sem = self.own if sem is None else sem
        ins.then_inc(sem, 1)
        self.counts[id(sem)] = self.counts.get(id(sem), 0) + 1
        self.open[id(sem)] = (sem, self.counts[id(sem)])

    def settle(self):
        for sem, n in self.open.values():
            self.eng.wait_ge(sem, n)
        self.open = {}


def build_program(nc, A):
    jobs = plan_jobs()
    job_number = {key: n for n, key in enumerate(jobs)}

    with ExitStack() as ctx:
        def sb(name, shape, dt=F32):
            return ctx.enter_context(nc.sbuf_tensor(name, shape, dt))

        named = {}

        def sem(*name):
            name = "_".join(map(str, name))
            if name not in named:
                named[name] = ctx.enter_context(nc.semaphore(name))
            return named[name]

        mats = sb("mats", [P, 7, P])
        IDENT, HEAD_MEAN, ALL_MEAN, BEFORE, ONES, ROT_HD, ROT_DF = (mats[:, i, :] for i in range(7))
        mod_sel = sb("mod_sel", [P, 2])
        rope = sb("rope", [P, 4, SEG])
        dist = sb("dist", [P, 3, 2, SEG])
        later = sb("later", [P, 2, SEG], U8)
        levels = sb("levels", [P, len(LEVELS), P], U8)
        iota_e = sb("iota_e", [P, 4, 4])
        g_rank = sb("g_rank", [P, G])
        row_iota = sb("row_iota", [P, MAXB + 1 + ROWS])
        tok_id = sb("tok_id", [P, 4])
        cc = sb("cc", [P, KD, 2])
        ccs = sb("ccs", [P, KD, 32])
        b_mod = sb("b_mod", [P, LAYERS, 48])
        norm1 = sb("norm1", [P, LAYERS, KD])
        norm2 = sb("norm2", [P, LAYERS, KD])
        normf = sb("normf", [P, KD])
        head_g = sb("head_g", [P, 5, LAYERS])
        decay_logit = sb("decay_logit", [P, LAYERS, 2, HEADS])
        log_decay = sb("log_decay", [P, LAYERS, 2, HEADS])
        lb_logit = sb("lb_logit", [P, 2, LAYERS, 2])
        lb_soft = sb("lb_soft", [P, 2, LAYERS, 2])
        lb = sb("lb", [P, 2, LAYERS, 2])
        one_m_lb = sb("one_m_lb", [P, 2, LAYERS, 2])
        lb_tmp = sb("lb_tmp", [P, 2, 2, 2])
        lam_in = sb("lam_in", [P, LAYERS, 4, 32])
        lam_pr = sb("lam_pr", [P, LAYERS, 2, 32])
        lam_ex = sb("lam_ex", [P, LAYERS, 2])
        neg_lam = sb("neg_lam", [P, LAYERS])
        router_w = sb("router_w", [P, KD, E])
        router_b = sb("router_b", [P, E])
        ring = sb("ring", [P, RING, 4, 512])
        xT = sb("xT", [P, KD, TOK])
        hT = sb("hT", [P, KD, TOK])
        featT = sb("featT", [P, NF, TOK])
        vtok = sb("vtok", [P, 4, VW])
        Wst = sb("Wst", [P, 2, 6, SEG])
        modT = sb("modT", [P, LAYERS, 48, 2])
        mod_rows = sb("mod_rows", [P, 2, 512])
        mscale = sb("mscale", [P, 2, KD, 2])
        sq = sb("sq", [P, 2, TOK])
        rs2 = sb("rs2", [P, 2, TOK])
        rs = rs2[:, 0, :]
        eps = sb("eps", [P, 1])
        rot = sb("rot", [P, 2, SEG])
        scratch = sb("scratch", [P, 7 * TOK])
        dec = scratch[:, 0:3 * TOK].rearrange("p (a b t) -> p a b t", a=3, b=2)
        prob = scratch[:, 0:6 * TOK].rearrange("p (b m t) -> p b m t", b=3, m=2)
        fg = scratch[:, 0:TOK]
        qk = scratch[:, TOK:7 * TOK].rearrange("p (b a t) -> p b a t", b=3, a=2)
        hn = scratch[:, 5 * TOK:7 * TOK].rearrange("p (a t) -> p a t", a=2)
        cum = sb("cum", [P, 2, 2, SEG + 1])
        stat = sb("stat", [P, 6, 4])
        def room(at, width, dt=F32):
            flat = featT[:, :, :].rearrange("p f t -> p (f t)")[:, at:at + width]
            return flat if dt == F32 else flat.bitcast(dt)
        h2tok = room(0, 1024)
        xg = room(1024, 1024)[0:ROWS, :]
        xgT = room(2048, 512).rearrange("p (k t) -> p k t", k=KD)
        sg = room(2560, 256)
        hm = room(2816, 256)
        hmT = room(3072, 256).rearrange("p (c t) -> p c t", c=2)
        ysb = room(3328, 512)
        ytok = room(3840, 4096).rearrange("p (b k d) -> p b k d", b=2, k=2)
        sc = sb("sc", [P, 4, E])
        sel = sb("sel", [P, 4, E])
        cmp1 = room(3840, 512)
        cmp2 = room(4352, 512)
        past = room(4864, 8 * (MAXB + 1)).rearrange("p (a b) -> p a b", b=MAXB + 1)
        in_block = room(5376, 8 * MAXB).rearrange("p (a b) -> p a b", b=MAXB)
        in_slot = room(5888, 8 * ROWS).rearrange("p (a s) -> p a s", s=ROWS)
        gsc = sb("gsc", [P, 4, G])
        gbest = sb("gbest", [P, 4, 2])
        goh = sb("goh", [P, 4, G])
        mask = sb("mask", [P, 4, E])
        gate = sb("gate", [P, 4, E])
        gsum = sb("gsum", [P, 4, 2])
        posn = room(9984, 4 * E).rearrange("p (a e) -> p a e", e=E)
        cnt = sb("cnt", [P, E])
        nblk = room(10240, 2 * E).rearrange("p (a e) -> p a e", e=E)
        tok2 = sb("tok2", [P, 8])
        row_of = sb("row_of", [P, 8])
        slot_of = sb("slot_of", [P, 8])
        zeros = sb("zeros", [P, 256])
        blk_end = sb("blk_end", [P, E])
        row0 = sb("row0", [P, E])
        end_row = sb("end_row", [1, E])
        dst = room(10112, 4 * E).rearrange("p (a e) -> p a e", e=E)
        dd = sb("dd", [P, 4, 2])
        gk = sb("gk", [P, 4, 2])
        be_cmp = room(7936, MAXB * E)
        be = sb("be", [1, MAXB + 1])
        be_i = sb("be_i", [1, MAXB + 1], I32)
        idx = sb("idx", [ROWS, MAXB], I32)
        idx_now = sb("idx_now", [ROWS, 1], I32)
        dti2 = [sb(f"rows_of_token_{L}", [P, 8], I32) for L in range(LAYERS)]

        banks = [ctx.enter_context(nc.psum_tensor(f"bank{i}", [P, 512], F32)) for i in range(8)]
        dram = {}
        for L in range(LAYERS):
            nt = len(token_tiles(L)) * P
            nb = max_blocks(nt)
            dram[L] = dict(
                h2=nc.dram_tensor(f"h2_{L}", (nt, D), F32, kind="Internal").ap(),
                nb=nb)
        y_dram = nc.dram_tensor("y_rows", (MAXB * ROWS, D), F32, kind="Internal").ap()

        unit0 = [0]
        for L in range(LAYERS):
            unit0.append(unit0[-1] + 2 * len(DENSE[L]) + dram[L]["nb"] * 6)
        first_unit = {what: unit0[L] + 2 * n for L in range(LAYERS) for n, what in enumerate(DENSE[L])}
        landed = [sem("landed", i) for i in range(RING)]
        used = [sem("used", i) for i in range(RING)]
        full = [sem("bank_full", i) for i in range(8)]
        free = [sem("bank_free", i) for i in range(8)]

        def bank(key):
            return banks[job_number[key] % 8]

        def wait_full(eng, key):
            n = job_number[key]
            eng.wait_ge(full[n % 8], n // 8 + 1)

        def free_sem(key):
            return free[job_number[key] % 8]

        def unit(n):
            return ring[:, n % RING, :, :]

        def down_unit(i):
            return ring[:, i, :, :].rearrange("p a n -> p (a n)").rearrange("p (k n) -> p k n", k=2)

        def load_dense(sp, L, n0, n1):
            for m in range(n0, n1):
                what, lw, c = DENSE[L][m // 2]
                n, k = unit0[L] + m, m % 2
                src = A["w_" + what][lw].rearrange("(k p) n -> p k n", p=P)[:, 4 * k:4 * k + 4, 512 * c:512 * c + 512]
                if n >= RING:
                    sp.wait_ge(used[n % RING], n // RING)
                sp.dma_start(unit(n), src).then_inc(landed[n % RING], 16)

        def release_after(pe, key, units):
            wait_full(pe, key)
            for n in units:
                pe.sem_inc(used[n % RING], 1)

        block = ctx.enter_context(nc.Block())

        @block.sync
        def _(sp):
            small = [
                (mats[:, :, :], A["k_mats"]), (mod_sel[:, :], A["k_mod_sel"]), (rope[:, :, :], A["k_rope"]),
                (dist[:, :, :, :], A["k_dist"]), (scratch[:, 0:TOK].bitcast(I32), A["k_later"]),
                (scratch[:, TOK:TOK + len(LEVELS) * P].bitcast(I32), A["k_levels"]), (iota_e[:, :, :], A["k_before4"]), (g_rank[:, :], A["k_grank"]),
                (row_iota[:, :], A["k_rows"]), (tok_id[:, :], A["k_tok"]), (b_mod[:, :, :], A["b_mod"]),
                (norm1[:, :, :], A["norm1"]), (norm2[:, :, :], A["norm2"]), (normf[:, :], A["normf"]),
                (head_g[:, :, :], A["head_g"]),
                (decay_logit[:, :, :, :], A["decay"].partition_broadcast(P)),
                (lb_logit[:, :, :, :], A["lb_logit"]),
                (lam_in[:, :, :, :], A["lam"].partition_broadcast(P)),
                (router_w[:, :, :], A["router_w"]),
                (router_b[:, :], A["router_b"].partition_broadcast(P)),
            ]
            sp.dma_start(cc[:, :, :], A["cc"]).then_inc(sem("cc_in"), 16)
            for n, src in enumerate(small):
                if n == 0:
                    load_dense(sp, 0, 0, 4)
                sp.dma_start(src[0], src[1]).then_inc(sem("small_in"), 16)
            sp.dma_start(xT[:, :, :], A["xT"]).then_inc(sem("x_in"), 16)
            sp.wait_ge(sem("small_in"), 16 * len(small))
            sp.sem_inc(sem("small_ready"), 1)
            for L in range(LAYERS):
                if L:
                    sp.wait_ge(sem("y_all_gathered"), 1)
                load_dense(sp, L, 4 if L == 0 else 0, 2 * len(DENSE[L]))
                d = dram[L]
                sp.wait_ge(sem("table"), L * PER_LAYER["table"] + 1)
                n = sp.value_load(be_i[0:1, MAXB:MAXB + 1], min_val=1, max_val=d["nb"])
                base = (unit0[L] + 2 * len(DENSE[L])) // RING
                with sp.Fori(0, d["nb"]) as b:
                    with sp.If(b < n):
                        e = sp.value_load(be_i[0:1, bass.ds(b, 1)], min_val=0, max_val=E - 1)
                        for i in range(6):
                            sp.wait_ge(used[i], b + base)
                            src = [A["w_gate"], A["w_up"], A["w_down"]][i // 2]
                            rows = src[L, bass.ds(e, 1), :, :].rearrange("o a b -> (o a) b")
                            if i < 4:
                                rows = rows.rearrange("(k p) n -> p k n", p=P)[:, 4 * (i % 2):4 * (i % 2) + 4, :]
                            else:
                                rows = rows.rearrange("(k p) n -> p k n", p=P)[:, 2 * (i % 2):2 * (i % 2) + 2, :]
                            slot = ring[:, i, :, :] if i < 4 else down_unit(i)
                            sp.dma_start(slot, rows).then_inc(landed[i], 16)
                    with sp.Else():
                        for i in range(6):
                            sp.wait_ge(landed[i], (b + base) * 16)
                            sp.sem_inc(landed[i], 16)
            sp.wait_ge(sem("final"), KD)
            sp.dma_start(A["outT"], hT[:, :, SEG:TOK]).then_inc(sem("out_stored"), 16)
            sp.wait_ge(sem("out_stored"), 16)

        @block.tensor
        def _(pe):
            order = iter(jobs)

            def begin(*key):
                assert next(order) == key, key
                n = job_number[key]
                if n >= 8:
                    pe.wait_ge(free[n % 8], n // 8)
                return banks[n % 8]

            def end(ins, key):
                ins.then_inc(full[job_number[key] % 8], 1)

            def arrived(n):
                pe.wait_ge(landed[n % RING], 16 * (n // RING + 1))

            def mm(out, lhsT, rhs, start, stop, **kw):
                return pe.matmul(out, lhsT, rhs, start=start, stop=stop, skip_group_check=True, **kw)

            pe.wait_ge(sem("cc_silu"), 1)
            for L in range(LAYERS):
                segs, tts = segments(L), token_tiles(L)
                lo = 0 if 0 in segs else SEG

                def modulation(lm, u):
                    ps = begin(lm, "mod", u)
                    n = first_unit[("mod", lm, u)]
                    arrived(n)
                    arrived(n + 1)
                    for half in range(2):
                        for q in range(4):
                            ins = mm(ps[32 * q:32 * q + 32, :], ccs[:, 4 * half + q, :], unit(n + half)[:, q, :],
                                     half == 0, half == 1, tile_position=(0, 32 * q))
                    end(ins, (lm, "mod", u))
                    release_after(pe, (lm, "mod", u), [n, n + 1])

                def mod_turn(lm, u):
                    ps = begin(lm, "modT", u)
                    m = 12 * lm + u
                    pe.wait_ge(sem("mod_rows"), m + 1)
                    for q in range(4):
                        ins = mm(ps[:, 2 * q:2 * q + 2], mod_rows[:, m % 2, q * P:(q + 1) * P], mod_sel[:, :], True, True)
                    end(ins, (lm, "modT", u))

                if L == 0:
                    for u in range(MOD_FIRST):
                        modulation(0, u)
                        if u == 0:
                            pe.wait_ge(sem("small_ready"), 1)
                        mod_turn(0, u)

                def mean_squares(name, gain_of_sum, count):
                    ps = begin(L, name)
                    for k in range(KD):
                        pe.wait_ge(sem(name, "sq", L), k + 1)
                        ins = mm(ps[:, 0:TOK], ALL_MEAN, sq[:, k % 2, :], k == 0, k == KD - 1)
                        if k < KD - 1:
                            ins.then_inc(sem(name, "sq_read", L), 1)
                    end(ins, (L, name))

                if L == 0:
                    pe.wait_ge(sem("x_in"), 16)
                mean_squares("ss1", None, None)

                base = first_unit[("in", L, 0)]
                pe.wait_ge(sem("h_ready"), L * PER_LAYER["h_ready"] + KD)

                def project(item):
                    c, c0, w = chunk_of(item)
                    n = base + 2 * c
                    ps = begin(L, *item)
                    if first_of_chunk(item):
                        arrived(n)
                        arrived(n + 1)
                    for k in range(KD):
                        weights = unit(n + k // 4)[:, k % 4, c0:c0 + w]
                        if item[0] == "feat":
                            q_lo = lo if item[1] in QUERY_TILES else 0
                            ins = mm(ps[:, q_lo:TOK], weights, hT[:, k, q_lo:TOK], k == 0, k == KD - 1)
                        else:
                            t = item[2]
                            ins = mm(ps[:, 0:w], hT[:, k, t * P:(t + 1) * P], weights, k == 0, k == KD - 1)
                    end(ins, (L, *item))
                    if last_of_chunk(item):
                        release_after(pe, (L, *item), [n, n + 1])

                for item in PROJ_FIRST:
                    project(item)

                for i in range(3):
                    ps = begin(L, "gss", i)
                    pe.wait_ge(sem("gsq"), L * PER_LAYER["gsq"] + i + 1)
                    end(mm(ps[:, :], HEAD_MEAN, sq[:, i % 2, :], True, True), (L, "gss", i))
                def rotate(tiles):
                    for f in tiles:
                        ps = begin(L, "rope", f)
                        if f in (GQ, GQ + 1, GK):
                            pe.wait_ge(sem("gnorm"), L * PER_LAYER["gnorm"] + f - GQ + 1)
                        else:
                            pe.wait_ge(sem("feat_ready"), L * PER_LAYER["feat_ready"] + f + 1)
                        end(mm(ps[:, 0:SEG], ROT_HD if f < DQ else ROT_DF, featT[:, f, SEG:TOK], True, True), (L, "rope", f))

                rotate(ROPED_FIRST)

                def value_product(mixer, j):
                    ps = begin(L, "pv", mixer, j)
                    pe.wait_ge(sem("v_ready"), L * PER_LAYER["v_ready"] + (4 if mixer in ("ret", "gqa") else 8))
                    for hh in range(2):
                        pe.wait_ge(sem("W_ready", mixer), L * HEADS + 2 * j + hh + 1)
                        vh = j if mixer == "gqa" else 2 * j + hh
                        vc = VCOL[mixer] + HD * vh
                        for g in segs:
                            parts = [(0, 0), (1, 1)] if g == 0 else [(4, 0), (5, 1), (2, 2), (3, 3)]
                            for n, (w, t) in enumerate(parts):
                                ins = mm(ps[HD * hh:HD * hh + HD, g * SEG:(g + 1) * SEG], vtok[:, t, vc:vc + HD],
                                         Wst[:, hh, w, :], n == 0, n == len(parts) - 1, tile_position=(0, HD * hh))
                    end(ins, (L, "pv", mixer, j))

                def attention(mixer):
                    for step, (made, _, turned, j) in enumerate(softmax_steps(L, mixer)):
                        if made is not None:
                            h, i = softmax_pair(L, made)
                            keys = TOK if i >= 2 else SEG
                            for m in range(MAPS[mixer]):
                                if mixer == "gqa":
                                    r0, width, fq, fk = HD * (h // 2), HD, GQ + h % 2, GK
                                else:
                                    r0, width, fq, fk = HD * (h % 2) + 32 * m, 32, DQ + h // 2, DK + h // 2
                                r = slice(r0, r0 + width)
                                ps = begin(L, "s", mixer, m, made)
                                end(mm(ps[:, 0:keys], featT[r, fq, i * P:(i + 1) * P], featT[r, fk, 0:keys], True, True,
                                       tile_position=(r0, 0)), (L, "s", mixer, m, made))
                        if turned is not None:
                            h, i = softmax_pair(L, turned)
                            ps = begin(L, "t", mixer, turned)
                            pe.wait_ge(sem("prob", mixer, L), turned + 1)
                            for n, s in enumerate([0, 1] if i < 2 else [2, 3, 0, 1]):
                                ins = pe.transpose(ps[:, n * P:(n + 1) * P], prob[:, turned % 3, 0, s * P:(s + 1) * P], IDENT)
                            end(ins, (L, "t", mixer, turned))
                        if j is not None:
                            value_product(mixer, j)
                        if mixer == "gqa":
                            for item in proj_beside(L, 4 + step):
                                project(item)

                pe.wait_ge(sem("roped"), L * PER_LAYER["roped"] + len(ROPED_FIRST))
                for j in range(2):
                    for hh in range(2):
                        r = slice(HD * hh, HD * hh + HD)
                        for part in ([0] if 0 in segs else []) + [1, 2]:
                            ps = begin(L, "rs", 2 * j + hh, part)
                            t0 = 0 if part == 0 else SEG
                            s0 = SEG if part == 2 else 0
                            for s in range(2):
                                ins = mm(ps[:, s * SEG:(s + 1) * SEG], featT[r, RK + j, s0 + s * P:s0 + s * P + P],
                                         featT[r, RQ + j, t0:t0 + SEG], True, True)
                            end(ins, (L, "rs", 2 * j + hh, part))
                        for item in proj_beside(L, 2 * j + hh):
                            project(item)
                    value_product("ret", j)
                attention("gqa")
                for j in range(2):
                    for lev in range(LEVELS_ALL):
                        m = j * LEVELS_ALL + lev
                        pe.wait_ge(sem("qk"), L * PER_LAYER["qk"] + m + 1)
                        for hh in range(2):
                            r = slice(HD * hh, HD * hh + HD)
                            Q, K = qk[r, m % 3, 0, :], qk[r, m % 3, 1, :]
                            ps = begin(L, "hl", j, lev, hh)
                            if lev < 9:
                                for t in tts:
                                    tq, tk = (t, t) if lev < 8 else (t ^ 1, t)
                                    ins = mm(ps[:, t * P:(t + 1) * P], K[:, tk * P:(tk + 1) * P], Q[:, tq * P:(tq + 1) * P],
                                             True, True)
                            else:
                                for s in range(2):
                                    for dr in range(2):
                                        ins = mm(ps[:, s * SEG:(s + 1) * SEG], K[:, dr * SEG + s * P:dr * SEG + s * P + P],
                                                 Q[:, dr * SEG:(dr + 1) * SEG], dr == 0, dr == 1)
                            end(ins, (L, "hl", j, lev, hh))
                        if L == 0:
                            modulation(*MOD_LATER[m])
                            if m:
                                mod_turn(*MOD_LATER[m - 1])
                            if m == len(MOD_LATER) - 1:
                                mod_turn(*MOD_LATER[m])
                    value_product("hg", j)
                rotate(ROPED_LAST)
                pe.wait_ge(sem("roped"), L * PER_LAYER["roped"] + len(ROPED))
                attention("df")
                for x in range(len(NORMED)):
                    ps = begin(L, "oss", x)
                    pe.wait_ge(sem("osq"), L * PER_LAYER["osq"] + x + 1)
                    end(mm(ps[:, lo:TOK], HEAD_MEAN, sq[:, x % 2, lo:TOK], True, True), (L, "oss", x))

                base = first_unit[("out", L, 0)]
                pe.wait_ge(sem("normed"), L * PER_LAYER["normed"] + len(NORMED))
                for f in range(KD):
                    n = base + 2 * (f // 4)
                    if f % 4 == 0:
                        arrived(n)
                        arrived(n + 1)
                    ps = begin(L, "out", f)
                    for k in range(KD):
                        mix = featT[:, MIXTILE[MIXERS[k // 2]] + k % 2, lo:TOK]
                        ins = mm(ps[:, lo:TOK], unit(n + k // 4)[:, k % 4, (f % 4) * P:(f % 4) * P + P], mix,
                                 k == 0, k == KD - 1)
                    end(ins, (L, "out", f))
                    if f % 4 == 3:
                        release_after(pe, (L, "out", f), [n, n + 1])
                pe.sem_inc(sem("mix_read"), 1)
                mean_squares("ss2", None, None)

                pe.wait_ge(sem("h2_ready"), L * PER_LAYER["h2_ready"] + KD)
                ps = begin(L, "router")
                for i, t in enumerate(tts):
                    for k in range(KD):
                        ins = mm(ps[:, i * E:(i + 1) * E], hT[:, k, t * P:(t + 1) * P], router_w[:, k, :],
                                 k == 0, k == KD - 1)
                end(ins, (L, "router"))
                for i, t in enumerate(tts):
                    for half in range(2):
                        ps = begin(L, "h2t", i, half)
                        for q in range(4):
                            ins = pe.transpose(ps[:, q * P:(q + 1) * P], hT[:, 4 * half + q, t * P:(t + 1) * P], IDENT)
                        end(ins, (L, "h2t", i, half))
                ps = begin(L, "pos")
                pe.wait_ge(sem("mask"), L * PER_LAYER["mask"] + 1)
                for i in range(len(tts)):
                    for i2 in range(i + 1):
                        ins = mm(ps[:, i * E:(i + 1) * E], BEFORE if i2 == i else ONES, mask[:, i2, :], i2 == 0, i2 == i)
                for i2 in range(len(tts)):
                    ins = mm(ps[:, P:P + E], ONES, mask[:, i2, :], i2 == 0, i2 == len(tts) - 1)
                end(ins, (L, "pos"))
                ps = begin(L, "idx")
                pe.wait_ge(sem("one_hots"), L * PER_LAYER["one_hots"] + 1)
                nb = dram[L]["nb"]
                for a in range(2 * len(tts)):
                    ins = mm(ps[0:ROWS, 0:MAXB], in_slot[:, a, :], in_block[:, a, :], a == 0, a == 2 * len(tts) - 1)
                end(ins, (L, "idx"))

                for b in range(8):
                    done = sum(1 for x in range(job_number[(L, "idx")] + 1) if x % 8 == b)
                    pe.wait_ge(free[b], done)
                pe.wait_ge(sem("table"), L * PER_LAYER["table"] + 1)
                n = pe.value_load(be_i[0:1, MAXB:MAXB + 1], min_val=1, max_val=nb)
                base = (unit0[L] + 2 * len(DENSE[L])) // RING

                def turn_rows(b):
                    pe.wait_ge(sem("gathered", L), (b + 1) * 16)
                    pe.sem_inc(sem("turn"), 1)
                    for k in range(KD):
                        ins = pe.transpose(banks[0][:, k * ROWS:(k + 1) * ROWS], xg[:, k * P:(k + 1) * P],
                                           IDENT[0:ROWS, 0:ROWS])
                    ins.then_inc(sem("turned", L), 1)

                pe.sem_inc(sem("turned", L), 1)
                pe.sem_inc(sem("hm_turned", L), 1)
                turn_rows(0)
                with pe.Fori(0, nb) as b:
                    with pe.If(b < n):
                        pe.wait_ge(sem("xgT", L), b + 1)
                        for w in range(2):
                            for half in range(2):
                                i = 2 * w + half
                                pe.wait_ge(landed[i], (b + base) * 16 + 16)
                                for q in range(4):
                                    for c in range(2):
                                        ins = mm(banks[2 + w][ROWS * c:ROWS * c + ROWS, 0:256], xgT[:, 4 * half + q, :],
                                                 ring[:, i, q, 256 * c:256 * c + 256],
                                                 half == 0 and q == 0, half == 1 and q == 3, tile_position=(0, ROWS * c))
                                ins.then_inc(used[i], 1)
                        with pe.If(b + 1 < n):
                            turn_rows(b + 1)
                        pe.wait_ge(sem("hm", L), b + 2)
                        for c in range(2):
                            ins = pe.transpose(banks[4][:, c * P:(c + 1) * P], hm[:, c * P:(c + 1) * P], IDENT)
                        ins.then_inc(sem("hm_turned", L), 1)
                        pe.wait_ge(sem("hmT", L), b + 1)
                        pe.wait_ge(sem("y_read", L), b + 1)
                        for q in range(4):
                            i = 4 + q // 2
                            if q % 2 == 0:
                                pe.wait_ge(landed[i], (b + base) * 16 + 16)
                            for c in range(2):
                                ins = mm(banks[5][ROWS * c:ROWS * c + ROWS, :], hmT[:, q % 2, ROWS * (q // 2):ROWS * (q // 2) + ROWS],
                                         down_unit(i)[:, q % 2, 512 * c:512 * c + 512], q == 0, q == 3,
                                         tile_position=(0, ROWS * c))
                            if q % 2 == 1:
                                ins.then_inc(used[i], 1)
                    with pe.Else():
                        for i in range(6):
                            pe.wait_ge(used[i], b + base)
                            pe.sem_inc(used[i], 1)
                for i in range(len(tts)):
                    for half in range(2):
                        ps = begin(L, "yt", i, half)
                        pe.wait_ge(sem("y_tok", L), i + 1)
                        for q in range(4):
                            ins = pe.transpose(ps[:, q * P:(q + 1) * P], ytok[:, i % 2, 0, (4 * half + q) * P:(4 * half + q + 1) * P], IDENT)
                        end(ins, (L, "yt", i, half))

            L = LAYERS
            ps = begin(L, "ssf")
            for k in range(KD):
                pe.wait_ge(sem("ssf", "sq", L), k + 1)
                ins = mm(ps[:, SEG:TOK], ALL_MEAN, sq[:, k % 2, SEG:TOK], k == 0, k == KD - 1)
                if k < KD - 1:
                    ins.then_inc(sem("ssf", "sq_read", L), 1)
            end(ins, (L, "ssf"))

        @block.scalar
        def _(act):
            st = Steps(act, sem("act_steps"))

            def evac(key, out, in_, func=ACT.Copy, done=None, **kw):
                wait_full(act, key)
                st.did(act.activation(out, in_, func, **kw), done)
                st.settle()
                act.sem_inc(free_sem(key), 1)

            act.wait_ge(sem("cc_in"), 16)
            act.wait_ge(sem("ccs_zero"), 1)
            st.did(act.activation(ccs[:, :, 0:2], cc[:, :, :], ACT.Silu), sem("cc_silu"))
            act.wait_ge(sem("small_ready"), 1)
            flat = lambda ap: ap.rearrange("p a b c -> p (a b c)")
            st.did(act.activation(flat(log_decay[:, :, :, :]), flat(decay_logit[:, :, :, :]), ACT.Sigmoid), sem("decay_sig"))
            act.wait_ge(sem("lb_sub"), 1)
            st.did(act.activation(flat(lb_soft[:, :, :, :]), flat(lb_soft[:, :, :, :]), ACT.Exp), sem("lb_exp"))
            act.wait_ge(sem("lam_sum"), 1)
            st.did(act.activation(lam_ex[:, :, :].rearrange("p a b -> p (a b)"),
                                  lam_ex[:, :, :].rearrange("p a b -> p (a b)"), ACT.Exp), sem("lam_exp"))
            act.wait_ge(sem("decay_max"), 1)
            st.did(act.activation(flat(log_decay[:, :, :, :]), flat(log_decay[:, :, :, :]), ACT.Ln), sem("decay_ready"))

            def squares(L, name, lo):
                for k in range(KD):
                    if k >= 2:
                        act.wait_ge(sem(name, "sq_read", L), k - 1)
                    st.did(act.activation(sq[:, k % 2, lo:TOK], xT[:, k, lo:TOK], ACT.Square), sem(name, "sq", L))

            def root(key, out, lo, done):
                evac(key, out[:, lo:TOK], bank(key)[:, lo:TOK], ACT.Sqrt, done, bias=eps[:, 0:1])

            def modulate(L, which, segs, ready):
                for k in range(KD):
                    act.wait_ge(sem("hn"), 2 * L * KD + which * KD + k + 1)
                    for n, g in enumerate(segs):
                        c = 1 - g
                        st.did(act.activation(hT[:, k, g * SEG:(g + 1) * SEG], hn[:, k % 2, g * SEG:(g + 1) * SEG], ACT.Identity,
                                              scale=mscale[:, which, k, c:c + 1], bias=modT[:, L, 24 * which + k, c:c + 1]),
                               ready if n == len(segs) - 1 else None)

            for L in range(LAYERS):
                segs, tts = segments(L), token_tiles(L)
                lo = 0 if 0 in segs else SEG
                def mod_copy(lm, u):
                    m = 12 * lm + u
                    if m >= 2:
                        wait_full(act, ((m - 2) // 12, "modT", (m - 2) % 12))
                    evac((lm, "mod", u), mod_rows[:, m % 2, :], bank((lm, "mod", u))[:, :], done=sem("mod_rows"))

                if L == 0:
                    for u in range(MOD_FIRST):
                        mod_copy(0, u)
                if L == 0:
                    act.wait_ge(sem("x_in"), 16)
                else:
                    act.wait_ge(sem("x_done"), (L - 1) * PER_LAYER["x_done"] + 1)
                squares(L, "ss1", 0)
                root((L, "ss1"), rs, 0, sem("root"))
                if L:
                    act.wait_ge(sem("h_ready"), L * PER_LAYER["h_ready"])
                modulate(L, 0, [0, 1], sem("h_ready"))

                def copy_projected(item):
                    if item[0] == "feat":
                        f = item[1]
                        q_lo = lo if f in QUERY_TILES else 0
                        func = ACT.Silu if f in (RG, RG + 1, HG, HG + 1) else ACT.Copy
                        evac((L, *item), featT[:, f, q_lo:TOK], bank((L, *item))[:, q_lo:TOK], func, sem("feat_ready"))
                    else:
                        c0, w = (0, 384) if item[1] == 0 else (384, 512)
                        evac((L, *item), vtok[:, item[2], c0:c0 + w], bank((L, *item))[:, 0:w], done=sem("v_ready"))

                for item in PROJ_FIRST:
                    copy_projected(item)
                for i in range(3):
                    q_lo = lo if i < 2 else 0
                    if i >= 2:
                        wait_full(act, (L, "gss", i - 2))
                    st.did(act.activation(sq[:, i % 2, :], featT[:, GQ + i, :], ACT.Square), sem("gsq"))
                for i in range(3):
                    if i >= 2:
                        act.wait_ge(sem("gnorm"), L * PER_LAYER["gnorm"] + i - 1)
                    root((L, "gss", i), rs2[:, i % 2, :], 0, sem("groot"))

                def attention(mixer):
                    d = HD if mixer == "gqa" else 32
                    for step, (made, _, turned, j) in enumerate(softmax_steps(L, mixer)):
                        if made is not None:
                            h, i = softmax_pair(L, made)
                            keys = TOK if i >= 2 else SEG
                            for m in range(MAPS[mixer]):
                                key = (L, "s", mixer, m, made)
                                s4 = 2 * (made % 3) + m
                                act.wait_ge(sem("max", mixer, L), MAPS[mixer] * made + m + 1)
                                if made >= 3 and m == 0:
                                    wait_full(act, (L, "t", mixer, made - 3))
                                st.did(act.activation(prob[:, made % 3, m, 0:keys], bank(key)[:, 0:keys], ACT.Exp,
                                                      bias=stat[:, s4, 1:2], scale=d ** -0.5, accum_out=stat[:, s4, 2:3]),
                                       sem("exp", mixer, L))
                                st.settle()
                                act.sem_inc(free_sem(key), 1)
                        if turned is not None:
                            h, i = softmax_pair(L, turned)
                            key = (L, "t", mixer, turned)
                            if i == tts[0] and h % 2 == 0:
                                wait_full(act, (L, "pv", mixer, 0) if h else (L, "pv", {"gqa": "ret", "df": "hg"}[mixer], 1))
                            w0, ns = (0, 2) if i < 2 else (2, 4)
                            c0 = (i % 2) * P
                            last = i == tts[-1]
                            evac(key, Wst[:, h % 2, w0:w0 + ns, c0:c0 + P],
                                 bank(key)[:, 0:ns * P].rearrange("p (a t) -> p a t", a=ns),
                                 done=sem("W_ready", mixer) if last else None)
                        if mixer == "gqa":
                            for item in proj_beside(L, 4 + step):
                                copy_projected(item)

                if L == 0:
                    act.wait_ge(sem("decay_ready"), 1)
                for j in range(2):
                    for hh in range(2):
                        h = 2 * j + hh
                        act.wait_ge(sem("dec_free"), L * PER_LAYER["dec_free"] + 2 * h + 1)
                        for n, (dr, table) in enumerate([(0, 0), (1, 0)]):
                            st.did(act.activation(dec[:, n, :, :].rearrange("p b t -> p (b t)"),
                                                  dist[:, table, :, :].rearrange("p b t -> p (b t)"), ACT.Exp,
                                                  scale=log_decay[:, L, dr, h:h + 1]), sem("dec"))
                        act.wait_ge(sem("dec_free"), L * PER_LAYER["dec_free"] + 2 * h + 2)
                        for n, (dr, table) in enumerate([(0, 1), (1, 2)]):
                            st.did(act.activation(dec[:, 1 + n, :, :].rearrange("p b t -> p (b t)"),
                                                  dist[:, table, :, :].rearrange("p b t -> p (b t)"), ACT.Exp,
                                                  scale=log_decay[:, L, dr, h:h + 1]), sem("dec"))
                        for item in proj_beside(L, h):
                            copy_projected(item)
                attention("gqa")
                for j in range(2):
                    for dr in range(2):
                        z = featT[:, (ZF, ZB)[dr] + j, :]
                        act.wait_ge(sem("fg_free"), L * PER_LAYER["fg_free"] + 2 * j + dr + 1)
                        st.did(act.activation(fg, z, ACT.Sigmoid))
                        st.settle()
                        st.did(act.activation(z, z, ACT.Sigmoid, scale=-1.0), sem("gates"))
                        act.wait_ge(sem("fgate"), L * PER_LAYER["fgate"] + 2 * j + dr + 1)
                        st.did(act.activation(fg, fg, ACT.Ln), sem("flog"))
                    for lev in range(LEVELS_ALL):
                        m = j * LEVELS_ALL + lev
                        if lev == 0:
                            if L == 0 and m:
                                mod_copy(*MOD_LATER[m - 1])
                            continue
                        act.wait_ge(sem("qk_arg"), L * PER_LAYER["qk_arg"] + j * 9 + lev)
                        st.did(act.activation(qk[:, m % 3, :, :].rearrange("p a t -> p (a t)"),
                                              qk[:, m % 3, :, :].rearrange("p a t -> p (a t)"), ACT.Exp), sem("qk_exp"))
                        if L == 0:
                            mod_copy(*MOD_LATER[m - 1])
                if L == 0:
                    mod_copy(*MOD_LATER[-1])
                attention("df")
                for x in range(len(NORMED) + 1):
                    if x < len(NORMED):
                        mixer, j = NORMED[x]
                        act.wait_ge(sem("mixed"), L * PER_LAYER["mixed"] + len(MIXERS) * 2)
                        if x >= 2:
                            wait_full(act, (L, "oss", x - 2))
                        st.did(act.activation(sq[:, x % 2, lo:TOK], featT[:, MIXTILE[mixer] + j, lo:TOK], ACT.Square), sem("osq"))
                    if x:
                        if x >= 3:
                            act.wait_ge(sem("normed"), L * PER_LAYER["normed"] + x - 2)
                        root((L, "oss", x - 1), rs2[:, (x - 1) % 2, :], lo, sem("oroot"))
                act.wait_ge(sem("x_mixed"), L * PER_LAYER["x_mixed"] + 1)
                squares(L, "ss2", lo)
                root((L, "ss2"), rs, lo, sem("root"))
                act.wait_ge(sem("mix_read"), L + 1)
                modulate(L, 1, segs, sem("h2_ready"))
                evac((L, "router"), sc[:, 0:len(tts), :].rearrange("p a e -> p (a e)"),
                     bank((L, "router"))[:, 0:len(tts) * E], ACT.Sigmoid, sem("scores"))
                for i in range(len(tts)):
                    if i:
                        act.wait_ge(sem("h2_stored", L), 16 * i)
                    for half in range(2):
                        evac((L, "h2t", i, half), h2tok[:, 512 * half:512 * half + 512], bank((L, "h2t", i, half))[:, :])
                    act.dma_start(dram[L]["h2"][i * P:(i + 1) * P, :], h2tok).then_inc(sem("h2_stored", L), 16)
                act.wait_ge(sem("table"), L * PER_LAYER["table"] + 1)
                nb = dram[L]["nb"]
                n = act.value_load(be_i[0:1, MAXB:MAXB + 1], min_val=1, max_val=nb)
                base = (unit0[L] + 2 * len(DENSE[L])) // RING

                act.sem_inc(sem("y_read", L), 1)
                act.sem_inc(sem("y_stored", L), 32)
                if L == 0:
                    act.wait_ge(sem("y_may_store"), 1)
                act.wait_ge(sem("h2_stored", L), 16 * len(tts))
                with act.Fori(0, nb) as b:
                    with act.If(b < n):
                        act.wait_ge(used[1], b + base + 1)
                        act.wait_ge(sem("hm", L), b + 1)
                        act.activation(sg, banks[2][:, 0:256], ACT.Silu).then_inc(sem("sg", L), 1)
                        act.wait_ge(used[5], b + base + 1)
                        act.wait_ge(sem("y_stored", L), b * 32 + 32)
                        act.activation(ysb, banks[5][:, :], ACT.Copy).then_inc(sem("y_read", L), 1)
                        act.wait_ge(sem("y_read", L), b + 2)
                        for c in range(2):
                            act.dma_start(y_dram[bass.ds(b * ROWS, ROWS), 512 * c:512 * c + 512], ysb[ROWS * c:ROWS * c + ROWS, :]
                                          ).then_inc(sem("y_stored", L), 16)
                act.wait_ge(sem("y_stored", L), n * 32 + 32)
                act.sem_inc(sem("y_all"), 1)
                for i in range(len(tts)):
                    y1 = ytok[:, i % 2, 1, :]
                    act.wait_ge(sem("y_gathered", i % 2), 32 * (i // 2 + 1 + 2 * L))
                    st.did(act.activation(y1, y1, ACT.Copy, scale=gk[:, i, 1:2]), sem("y1_scaled"))
            L = LAYERS
            act.wait_ge(sem("x_done"), (L - 1) * PER_LAYER["x_done"] + 1)
            squares(L, "ssf", SEG)
            root((L, "ssf"), rs, SEG, sem("root"))

        @block.gpsimd
        def _(pool):
            pool.wait_ge(sem("small_ready"), 1)
            pool.wait_ge(sem("zeros_set"), 1)
            pool.wait_ge(sem("h_ready"), KD)
            pool.dma_start(y_dram.rearrange("(p r) (c n) -> p (r c) n", p=P, n=256),
                           zeros[:, :].unsqueeze(1).to_broadcast([P, MAXB * ROWS * 4 // P, 256])).then_inc(sem("y_zeroed"), 16)
            for L in range(LAYERS):
                d, tts = dram[L], token_tiles(L)
                pool.wait_ge(sem("h2_stored", L), 16 * len(tts))
                pool.wait_ge(sem("idx"), L * PER_LAYER["idx"] + 1)
                if L == 0:
                    pool.wait_ge(sem("y_zeroed"), 16)
                    pool.sem_inc(sem("y_may_store"), 1)
                n = pool.value_load(be_i[0:1, MAXB:MAXB + 1], min_val=1, max_val=d["nb"])
                with pool.Fori(0, d["nb"]) as b:
                    with pool.If(b < n):
                        pool.wait_ge(sem("turned", L), b + 1)
                        pool.wait_ge(sem("idx_col", L), b + 1)
                        pool.sem_inc(sem("gather_turn"), 1)
                        pool.indirect_dma_start(xg, None, d["h2"], bass.IndirectOffsetOnAxis(idx_now[:, 0:1], 0)
                                                ).then_inc(sem("gathered", L), 16)
                pool.wait_ge(sem("y_all"), L * PER_LAYER["y_all"] + 1)
                for i in range(len(tts)):
                    if i >= 2:
                        pool.wait_ge(sem("y_tok_read", L), i - 1)
                    for k in range(2):
                        pool.indirect_dma_start(ytok[:, i % 2, k, :], None, y_dram, bass.IndirectOffsetOnAxis(dti2[L][:, 2 * i + k:2 * i + k + 1], 0)
                                                ).then_inc(sem("y_gathered", i % 2), 16)
                if L == 0:
                    for i in range(2):
                        pool.wait_ge(sem("y_gathered", i), 32 * len(tts) // 2)
                    pool.sem_inc(sem("y_all_gathered"), 1)

        @block.vector
        def _(dve):
            st = Steps(dve, sem("dve_steps"))
            did, settle = st.did, st.settle

            def release(key):
                settle()
                dve.sem_inc(free_sem(key), 1)

            did(dve.memset(ccs[:, :, :], 0.0), sem("ccs_zero"))
            did(dve.memset(cum[:, :, :, :], 0.0))
            did(dve.memset(featT[:, :, :], 0.0))
            did(dve.memset(zeros[:, :], 0.0), sem("zeros_set"))
            did(dve.memset(eps[:, :], EPS))
            dve.wait_ge(sem("small_ready"), 1)
            did(dve.tensor_copy(later[:, :, :].rearrange("p a t -> p (a t)"), scratch[:, 0:TOK].bitcast(I32)))
            did(dve.tensor_copy(levels[:, :, :].rearrange("p a t -> p (a t)"),
                                scratch[:, TOK:TOK + len(LEVELS) * P].bitcast(I32)))
            settle()
            for k in range(2):
                did(dve.tensor_copy(tok2[:, :].rearrange("p (a k) -> p a k", k=2)[:, :, k], tok_id[:, :]))
            l0, l1 = lb_logit[:, :, 0, :], lb_logit[:, :, 1, :]
            did(dve.tensor_tensor(lb_tmp[:, 0, :, :], l0, l1, ALU.max))
            settle()
            did(dve.tensor_tensor(lb_soft[:, :, 0, :], l0, lb_tmp[:, 0, :, :], ALU.subtract))
            did(dve.tensor_tensor(lb_soft[:, :, 1, :], l1, lb_tmp[:, 0, :, :], ALU.subtract))
            settle()
            dve.sem_inc(sem("lb_sub"), 1)
            did(dve.tensor_tensor(lam_pr[:, :, 0, :], lam_in[:, :, 0, :], lam_in[:, :, 1, :], ALU.mult))
            did(dve.tensor_tensor(lam_pr[:, :, 1, :], lam_in[:, :, 2, :], lam_in[:, :, 3, :], ALU.mult))
            settle()
            did(dve.tensor_reduce(lam_ex[:, :, :], lam_pr[:, :, :, :], AX_X, ALU.add), sem("lam_sum"))
            dve.wait_ge(sem("decay_sig"), 1)
            ld = log_decay[:, :, :, :].rearrange("p a b c -> p (a b c)")
            did(dve.tensor_scalar(ld, ld, TINY, None, ALU.max), sem("decay_max"))
            dve.wait_ge(sem("lb_exp"), 1)
            e0, e1 = lb_soft[:, :, 0, :], lb_soft[:, :, 1, :]
            did(dve.tensor_tensor(lb_tmp[:, 0, :, :], e0, e1, ALU.add))
            settle()
            did(dve.reciprocal(lb_tmp[:, 1, :, :], lb_tmp[:, 0, :, :]))
            settle()
            did(dve.tensor_tensor(e0, e0, lb_tmp[:, 1, :, :], ALU.mult))
            did(dve.tensor_tensor(e1, e1, lb_tmp[:, 1, :, :], ALU.mult))
            settle()
            did(dve.tensor_tensor(lb[:, :, 0, :], e0, e0, ALU.subtract))
            did(dve.tensor_tensor(lb_tmp[:, 0, :, :], e0, e1, ALU.add))
            settle()
            did(dve.tensor_tensor(lb[:, :, 1, :], lb_tmp[:, 0, :, :], e0, ALU.subtract))
            settle()
            did(dve.tensor_scalar(one_m_lb[:, :, :, :].rearrange("p a b c -> p (a b c)"),
                                  lb[:, :, :, :].rearrange("p a b c -> p (a b c)"), -1.0, 1.0, ALU.mult, ALU.add))
            dve.wait_ge(sem("lam_exp"), 1)
            did(dve.tensor_tensor(neg_lam[:, :], lam_ex[:, :, 1], lam_ex[:, :, 0], ALU.subtract))
            settle()
            for L in range(LAYERS):
                init = 0.8 - 0.6 * math.exp(-0.3 * L)
                did(dve.tensor_scalar(neg_lam[:, L:L + 1], neg_lam[:, L:L + 1], -init, None, ALU.add))
                did(dve.tensor_scalar(head_g[:, 4, L:L + 1], head_g[:, 4, L:L + 1], 1 - init, None, ALU.mult))
            settle()

            def inverse_root(n, lo):
                dve.wait_ge(sem("root"), n + 1)
                did(dve.reciprocal(rs[:, lo:TOK], rs[:, lo:TOK]))
                settle()

            def normalized(n, lo, ready, per_layer):
                for k in range(KD):
                    if k >= 2:
                        dve.wait_ge(ready, per_layer + k - 1)
                    did(dve.tensor_tensor(hn[:, k % 2, lo:TOK], xT[:, k, lo:TOK], rs[:, lo:TOK], ALU.mult), sem("hn"))

            for L in range(LAYERS):
                segs, tts = segments(L), token_tiles(L)
                lo = 0 if 0 in segs else SEG
                def mod_add(lm, u):
                    key = (lm, "modT", u)
                    wait_full(dve, key)
                    did(dve.tensor_tensor(modT[:, lm, 4 * u:4 * u + 4, :],
                                          bank(key)[:, 0:8].rearrange("p (a c) -> p a c", c=2),
                                          b_mod[:, lm, 4 * u:4 * u + 4].unsqueeze(2).to_broadcast([P, 4, 2]), ALU.add))
                    release(key)

                def mod_scale(which):
                    g_in = (norm1, norm2)[which]
                    did(dve.tensor_scalar(mscale[:, which, :, :].rearrange("p a b -> p (a b)"),
                                          modT[:, L, 24 * which + 8:24 * which + 16, :].rearrange("p a b -> p (a b)"),
                                          1.0, None, ALU.add))
                    settle()
                    did(dve.tensor_tensor(mscale[:, which, :, :], mscale[:, which, :, :],
                                          g_in[:, L, :].unsqueeze(2).to_broadcast([P, KD, 2]), ALU.mult))
                    settle()

                if L == 0:
                    for u in range(MOD_FIRST):
                        mod_add(0, u)
                mod_scale(0)
                inverse_root(2 * L, 0)
                normalized(2 * L, 0, sem("h_ready"), L * PER_LAYER["h_ready"])

                for i in range(3):
                    dve.wait_ge(sem("groot"), L * PER_LAYER["groot"] + i + 1)
                    root_i = rs2[:, i % 2, :]
                    did(dve.reciprocal(root_i, root_i))
                    settle()
                    f = featT[:, GQ + i, :]
                    did(dve.scalar_tensor_tensor(out=f, in0=f, scalar=head_g[:, 1 + i // 2, L:L + 1], in1=root_i,
                                                 op0=ALU.mult, op1=ALU.mult), sem("gnorm"))
                    settle()
                def rotary(tiles):
                    for n, f in enumerate(tiles + [None]):
                        settle()
                        if f is not None:
                            key = (L, "rope", f)
                            wait_full(dve, key)
                            cs = 0 if f < DQ else 2
                            x = featT[:, f, SEG:TOK]
                            did(dve.tensor_tensor(rot[:, n % 2, :], bank(key)[:, 0:SEG], rope[:, cs + 1, :], ALU.mult))
                            did(dve.tensor_tensor(x, x, rope[:, cs, :], ALU.mult))
                        if n:
                            x = featT[:, tiles[n - 1], SEG:TOK]
                            did(dve.tensor_tensor(x, x, rot[:, (n - 1) % 2, :], ALU.add), sem("roped"))
                        if f is not None:
                            release(key)

                rotary(ROPED_FIRST)

                def readout(mixer, j):
                    key = (L, "pv", mixer, j)
                    wait_full(dve, key)
                    did(dve.tensor_copy(featT[:, MIXTILE[mixer] + j, lo:TOK], bank(key)[:, lo:TOK]))
                    release(key)
                    dve.sem_inc(sem("mixed"), 1)

                dve.sem_inc(sem("dec_free"), 1)
                for j in range(2):
                    for hh in range(2):
                        h = 2 * j + hh
                        dve.wait_ge(sem("dec"), L * PER_LAYER["dec"] + 4 * h + 2)
                        own = dec[:, 0, :, :]
                        did(dve.copy_predicated(own, later[:, :, :], dec[:, 1, :, :]))
                        settle()
                        for c in range(2):
                            diag = own[:, c, c * P:(c + 1) * P]
                            did(dve.tensor_tensor(diag, diag, IDENT, ALU.add))
                        settle()
                        dve.sem_inc(sem("dec_free"), 1)
                        for part in ([0] if 0 in segs else []) + [2]:
                            key = (L, "rs", h, part)
                            if part == 2:
                                cross = (L, "rs", h, 1)
                                dve.wait_ge(sem("dec"), L * PER_LAYER["dec"] + 4 * h + 4)
                                did(dve.tensor_tensor(dec[:, 1, :, :], dec[:, 1, :, :], dec[:, 2, :, :], ALU.add))
                                settle()
                                wait_full(dve, cross)
                                did(dve.scalar_tensor_tensor(out=Wst[:, hh, 4:6, :],
                                                             in0=bank(cross)[:, :].rearrange("p (a t) -> p a t", a=2),
                                                             scalar=HD ** -0.5, in1=dec[:, 1, :, :], op0=ALU.mult, op1=ALU.mult))
                                release(cross)
                            wait_full(dve, key)
                            w = 0 if part == 0 else 2
                            did(dve.scalar_tensor_tensor(out=Wst[:, hh, w:w + 2, :],
                                                         in0=bank(key)[:, :].rearrange("p (a t) -> p a t", a=2),
                                                         scalar=HD ** -0.5, in1=own, op0=ALU.mult, op1=ALU.mult))
                            release(key)
                        dve.sem_inc(sem("W_ready", "ret"), 1)
                        if h < 3:
                            dve.sem_inc(sem("dec_free"), 1)
                    readout("ret", j)

                def attention(mixer):
                    scale = (HD if mixer == "gqa" else 32) ** -0.5
                    for made, turned, _, j in softmax_steps(L, mixer):
                        if made is not None:
                            h, i = softmax_pair(L, made)
                            keys = TOK if i >= 2 else SEG
                            for m in range(MAPS[mixer]):
                                key = (L, "s", mixer, m, made)
                                s4 = 2 * (made % 3) + m
                                wait_full(dve, key)
                                did(dve.tensor_reduce(stat[:, s4, 0:1], bank(key)[:, 0:keys], AX_X, ALU.max))
                                settle()
                                did(dve.tensor_scalar(stat[:, s4, 1:2], stat[:, s4, 0:1], -scale, None, ALU.mult),
                                    sem("max", mixer, L))
                        if turned is not None:
                            h, i = softmax_pair(L, turned)
                            keys = TOK if i >= 2 else SEG
                            s4 = 2 * (turned % 3)
                            p0, p1 = prob[:, turned % 3, 0, 0:keys], prob[:, turned % 3, 1, 0:keys]
                            dve.wait_ge(sem("exp", mixer, L), MAPS[mixer] * (turned + 1))
                            did(dve.reciprocal(stat[:, s4:s4 + MAPS[mixer], 3], stat[:, s4:s4 + MAPS[mixer], 2]))
                            settle()
                            if mixer == "gqa":
                                did(dve.tensor_scalar(p0, p0, stat[:, s4, 3:4], None, ALU.mult), sem("prob", mixer, L))
                            else:
                                did(dve.tensor_scalar(p0, p0, stat[:, s4, 3:4], None, ALU.mult))
                                did(dve.tensor_scalar(stat[:, s4 + 1, 3:4], stat[:, s4 + 1, 3:4], neg_lam[:, L:L + 1], None, ALU.mult))
                                settle()
                                did(dve.scalar_tensor_tensor(out=p0, in0=p1, scalar=stat[:, s4 + 1, 3:4], in1=p0,
                                                             op0=ALU.mult, op1=ALU.add), sem("prob", mixer, L))
                        if j is not None:
                            readout(mixer, j)

                attention("gqa")
                dve.wait_ge(sem("feat_ready"), L * PER_LAYER["feat_ready"] + HG + 2)
                for j in range(2):
                    q = featT[:, HQ + j, :]
                    kf, kb = featT[:, ZF + j, :], featT[:, ZB + j, :]
                    for dr in range(2):
                        z = (kf, kb)[dr]
                        dve.sem_inc(sem("fg_free"), 1)
                        dve.wait_ge(sem("gates"), L * PER_LAYER["gates"] + 2 * j + dr + 1)
                        did(dve.tensor_scalar(z, z, one_m_lb[:, dr, L, j:j + 1], None, ALU.mult))
                        did(dve.tensor_scalar(fg, fg, one_m_lb[:, dr, L, j:j + 1], lb[:, dr, L, j:j + 1], ALU.mult, ALU.add))
                        settle()
                        did(dve.tensor_scalar(fg, fg, TINY, None, ALU.max), sem("fgate"))
                        dve.wait_ge(sem("flog"), L * PER_LAYER["flog"] + 2 * j + dr + 1)
                        for g in range(2):
                            did(dve.tensor_tensor_scan(cum[:, dr, g, 1:SEG + 1], fg[:, g * SEG:(g + 1) * SEG],
                                                       fg[:, g * SEG:(g + 1) * SEG], 0.0, ALU.add, ALU.bypass))
                        settle()

                    def pieces(ap, h):
                        return ap.rearrange("p s (b two h) -> p s b two h", two=2, h=h)

                    def level_arguments(lev):
                        m = j * LEVELS_ALL + lev
                        if m >= 3:
                            jj, ll = divmod(m - 3, LEVELS_ALL)
                            for hh in range(2):
                                wait_full(dve, (L, "hl", jj, ll, hh))
                        Q, K = qk[:, m % 3, 0, :], qk[:, m % 3, 1, :]
                        if lev == 0:
                            return
                        if lev < 9:
                            h = LEVELS[lev] if lev < 8 else P
                            nb2 = SEG // (2 * h)
                            Qv = pieces(Q.rearrange("p (s t) -> p s t", s=2), h)
                            Kv = pieces(K.rearrange("p (s t) -> p s t", s=2), h)
                            incF = pieces(cum[:, 0, :, 1:SEG + 1], h)
                            excF = pieces(cum[:, 0, :, 0:SEG], h)
                            excB = pieces(cum[:, 1, :, 0:SEG], h)
                            for g in range(2):
                                midF = excF[:, g, :, 1, 0:1].to_broadcast([P, nb2, h])
                                midB = excB[:, g, :, 1, 0:1].to_broadcast([P, nb2, h])
                                did(dve.tensor_tensor(Qv[:, g, :, 1, :], incF[:, g, :, 1, :], midF, ALU.subtract))
                                did(dve.tensor_tensor(Kv[:, g, :, 0, :], midF, incF[:, g, :, 0, :], ALU.subtract))
                                did(dve.tensor_tensor(Qv[:, g, :, 0, :], midB, excB[:, g, :, 0, :], ALU.subtract))
                                did(dve.tensor_tensor(Kv[:, g, :, 1, :], excB[:, g, :, 1, :], midB, ALU.subtract))
                        else:
                            did(dve.tensor_copy(Q[:, 0:SEG], cum[:, 0, 1, 1:SEG + 1]))
                            did(dve.tensor_tensor(Q[:, SEG:TOK], cum[:, 1, 1, SEG:SEG + 1].to_broadcast([P, SEG]),
                                                  cum[:, 1, 1, 0:SEG], ALU.subtract))
                            did(dve.tensor_tensor(K[:, 0:SEG], cum[:, 0, 0, SEG:SEG + 1].to_broadcast([P, SEG]),
                                                  cum[:, 0, 0, 1:SEG + 1], ALU.subtract))
                            did(dve.tensor_copy(K[:, SEG:TOK], cum[:, 1, 0, 0:SEG]))
                        settle()
                        dve.sem_inc(sem("qk_arg"), 1)

                    def level_factors(lev):
                        m = j * LEVELS_ALL + lev
                        Q, K = qk[:, m % 3, 0, :], qk[:, m % 3, 1, :]
                        if lev == 0:
                            did(dve.tensor_copy(Q, q))
                            did(dve.tensor_tensor(K, kf, kb, ALU.add))
                        else:
                            dve.wait_ge(sem("qk_exp"), L * PER_LAYER["qk_exp"] + j * 9 + lev)
                            if lev < 9:
                                h = LEVELS[lev] if lev < 8 else P
                                did(dve.tensor_tensor(Q, Q, q, ALU.mult))
                                Kv, kfv, kbv = (x.rearrange("p (b two h) -> p b two h", two=2, h=h) for x in (K, kf, kb))
                                did(dve.tensor_tensor(Kv[:, :, 0, :], Kv[:, :, 0, :], kfv[:, :, 0, :], ALU.mult))
                                did(dve.tensor_tensor(Kv[:, :, 1, :], Kv[:, :, 1, :], kbv[:, :, 1, :], ALU.mult))
                            else:
                                did(dve.tensor_tensor(Q[:, 0:SEG], Q[:, 0:SEG], q[:, SEG:TOK], ALU.mult))
                                did(dve.tensor_tensor(Q[:, SEG:TOK], Q[:, SEG:TOK], q[:, SEG:TOK], ALU.mult))
                                did(dve.tensor_tensor(K[:, 0:SEG], K[:, 0:SEG], kf[:, 0:SEG], ALU.mult))
                                did(dve.tensor_tensor(K[:, SEG:TOK], K[:, SEG:TOK], kb[:, 0:SEG], ALU.mult))
                        settle()
                        dve.sem_inc(sem("qk"), 1)

                    def level_weights(lev):
                        for hh in range(2):
                            key = (L, "hl", j, lev, hh)
                            wait_full(dve, key)
                            ps = bank(key)
                            flat = Wst[:, hh, :, :].rearrange("p w t -> p (w t)")
                            if lev < 9:
                                for g in segs:
                                    src = ps[:, g * SEG:(g + 1) * SEG].rearrange("p (b t) -> p b t", b=2)
                                    if lev < 8:
                                        own = flat[:, 2 * g * SEG:2 * g * SEG + 6 * P].rearrange("p (b x) -> p b x", x=3 * P)[:, :, 0:P]
                                    else:
                                        own = flat[:, 2 * g * SEG + P:2 * g * SEG + 3 * P].rearrange("p (b x) -> p b x", x=P)
                                    if 0 < lev < 8:
                                        did(dve.copy_predicated(own, levels[:, lev, :].unsqueeze(1).to_broadcast([P, 2, P]), src))
                                    else:
                                        did(dve.tensor_copy(own, src))
                            else:
                                did(dve.tensor_copy(Wst[:, hh, 4:6, :], ps[:, :].rearrange("p (a t) -> p a t", a=2)))
                            release(key)
                        m = j * LEVELS_ALL + lev
                        if L == 0 and m:
                            mod_add(*MOD_LATER[m - 1])
                        if L == 0 and m == len(MOD_LATER) - 1:
                            mod_add(*MOD_LATER[m])

                    if j == 0:
                        wait_full(dve, (L, "pv", "gqa", 1))
                    for lev in range(-1, LEVELS_ALL + 1):
                        if lev + 1 < LEVELS_ALL:
                            level_arguments(lev + 1)
                        if 0 <= lev < LEVELS_ALL:
                            level_factors(lev)
                        if lev >= 1:
                            level_weights(lev - 1)
                    dve.sem_inc(sem("W_ready", "hg"), 2)
                    readout("hg", j)

                rotary(ROPED_LAST)
                attention("df")
                for x, (mixer, j) in enumerate(NORMED):
                    out = featT[:, MIXTILE[mixer] + j, lo:TOK]
                    root_x = rs2[:, x % 2, lo:TOK]
                    dve.wait_ge(sem("oroot"), L * PER_LAYER["oroot"] + x + 1)
                    did(dve.reciprocal(root_x, root_x))
                    settle()
                    g = head_g[:, {"ret": 0, "hg": 3, "df": 4}[mixer], L:L + 1]
                    did(dve.scalar_tensor_tensor(out=out, in0=out, scalar=g, in1=root_x, op0=ALU.mult, op1=ALU.mult))
                    settle()
                    if mixer != "df":
                        did(dve.tensor_tensor(out, out, featT[:, {"ret": RG, "hg": HG}[mixer] + j, lo:TOK], ALU.mult))
                        settle()
                    dve.sem_inc(sem("normed"), 1)

                for f in range(KD):
                    key = (L, "out", f)
                    wait_full(dve, key)
                    for g in segs:
                        x = xT[:, f, g * SEG:(g + 1) * SEG]
                        did(dve.scalar_tensor_tensor(out=x, in0=bank(key)[:, g * SEG:(g + 1) * SEG],
                                                     scalar=modT[:, L, 16 + f, 1 - g:2 - g], in1=x, op0=ALU.mult, op1=ALU.add))
                    release(key)
                dve.sem_inc(sem("x_mixed"), 1)
                mod_scale(1)
                inverse_root(2 * L + 1, lo)
                normalized(2 * L + 1, lo, sem("h2_ready"), L * PER_LAYER["h2_ready"])

                nt, nb = len(tts), dram[L]["nb"]
                dve.wait_ge(sem("scores"), L * PER_LAYER["scores"] + 1)
                did(dve.tensor_tensor(sel[:, 0:nt, :], sc[:, 0:nt, :], router_b[:, :].unsqueeze(1).to_broadcast([P, nt, E]), ALU.add))
                settle()
                ng = nt * G
                flat3 = lambda ap: ap.rearrange("p a e -> p (a e)")
                s4 = flat3(sel[:, 0:nt, :]).rearrange("p (g e) -> p g e", e=4)
                of_j = s4.unsqueeze(2).to_broadcast([P, ng, 4, 4])
                of_e = s4.unsqueeze(3).to_broadcast([P, ng, 4, 4])
                c1 = cmp1[:, 0:16 * ng].rearrange("p (g e j) -> p g e j", e=4, j=4)
                c2 = cmp2[:, 0:16 * ng].rearrange("p (g e j) -> p g e j", e=4, j=4)
                did(dve.tensor_tensor(c1, of_j, of_e, ALU.is_gt))
                did(dve.tensor_tensor(c2, of_j, of_e, ALU.is_equal))
                settle()
                did(dve.tensor_tensor(c2, c2, iota_e[:, :, :].unsqueeze(1).to_broadcast([P, ng, 4, 4]), ALU.mult))
                settle()
                did(dve.tensor_tensor(c1, c1, c2, ALU.add))
                settle()
                mflat = flat3(mask[:, 0:nt, :])
                m4 = mflat.rearrange("p (g e) -> p g e", e=4)
                did(dve.tensor_reduce(m4, c1, AX_X, ALU.add))
                settle()
                did(dve.tensor_scalar(mflat, mflat, 2.0, None, ALU.is_lt))
                settle()
                t4 = cmp1[:, 0:nt * E].rearrange("p (g e) -> p g e", e=4)
                did(dve.tensor_tensor(cmp1[:, 0:nt * E], mflat, flat3(sel[:, 0:nt, :]), ALU.mult))
                settle()
                did(dve.tensor_reduce(flat3(gsc[:, 0:nt, :]), t4, AX_X, ALU.add))
                settle()
                did(dve.tensor_reduce(gbest[:, 0:nt, 0], gsc[:, 0:nt, :], AX_X, ALU.max))
                settle()
                did(dve.tensor_tensor(goh[:, 0:nt, :], gsc[:, 0:nt, :], gbest[:, 0:nt, 0:1].to_broadcast([P, nt, G]), ALU.is_equal))
                settle()
                did(dve.tensor_tensor(goh[:, 0:nt, :], goh[:, 0:nt, :], g_rank[:, :].unsqueeze(1).to_broadcast([P, nt, G]), ALU.mult))
                settle()
                did(dve.tensor_reduce(gbest[:, 0:nt, 1], goh[:, 0:nt, :], AX_X, ALU.max))
                settle()
                did(dve.tensor_tensor(goh[:, 0:nt, :], goh[:, 0:nt, :], gbest[:, 0:nt, 1:2].to_broadcast([P, nt, G]), ALU.is_equal))
                settle()
                did(dve.tensor_tensor(m4, m4, flat3(goh[:, 0:nt, :]).unsqueeze(2).to_broadcast([P, ng, 4]), ALU.mult))
                settle()
                dve.sem_inc(sem("mask"), 1)
                key = (L, "pos")
                wait_full(dve, key)
                did(dve.tensor_copy(posn[:, 0:nt, :].rearrange("p a e -> p (a e)"), bank(key)[:, 0:nt * E]))
                did(dve.tensor_copy(cnt[:, :], bank(key)[:, P:P + E]))
                release(key)
                did(dve.tensor_scalar(nblk[:, 0, :], cnt[:, :], 0.0, None, ALU.is_gt))
                for q in range(1, nt * P // ROWS):
                    settle()
                    did(dve.scalar_tensor_tensor(out=nblk[:, q % 2, :], in0=cnt[:, :], scalar=float(q * ROWS),
                                                 in1=nblk[:, (q - 1) % 2, :], op0=ALU.is_gt, op1=ALU.add))
                n_blk = nblk[:, (nt * P // ROWS - 1) % 2, :]
                settle()
                did(dve.tensor_tensor_scan(blk_end[:, :], n_blk, n_blk, 0.0, ALU.add, ALU.bypass))
                settle()
                did(dve.tensor_tensor(row0[:, :], blk_end[:, :], n_blk, ALU.subtract))
                cmpb = be_cmp[0:1, 0:nb * E].rearrange("p (b e) -> p b e", e=E)
                did(dve.tensor_scalar(end_row[0:1, :], blk_end[0:1, :], float(ROWS), None, ALU.mult))
                settle()
                did(dve.tensor_tensor(cmpb, end_row[0:1, :].unsqueeze(1).to_broadcast([1, nb, E]),
                                      row_iota[0:1, 0:nb].unsqueeze(2).to_broadcast([1, nb, E]), ALU.is_le))
                settle()
                did(dve.tensor_reduce(be[0:1, 0:nb], cmpb, AX_X, ALU.add))
                settle()
                did(dve.tensor_scalar(be[0:1, 0:nb], be[0:1, 0:nb], float(E - 1), None, ALU.min))
                did(dve.tensor_copy(be_i[0:1, MAXB:MAXB + 1], blk_end[0:1, E - 1:E]))
                settle()
                did(dve.tensor_copy(be_i[0:1, 0:nb], be[0:1, 0:nb]))
                settle()
                dve.sem_inc(sem("table"), 1)
                did(dve.tensor_scalar(row0[:, :], row0[:, :], float(ROWS), 1.0, ALU.mult, ALU.add))
                settle()
                d_ = dst[:, 0:nt, :]
                did(dve.tensor_tensor(d_, posn[:, 0:nt, :], row0[:, :].unsqueeze(1).to_broadcast([P, nt, E]), ALU.add))
                settle()
                did(dve.tensor_tensor(d_, d_, mask[:, 0:nt, :], ALU.mult))
                settle()
                did(dve.tensor_reduce(dd[:, 0:nt, 1:2].rearrange("p a o -> p (a o)"), d_, AX_X, ALU.max))
                did(dve.tensor_reduce(dd[:, 0:nt, 0:1].rearrange("p a o -> p (a o)"), d_, AX_X, ALU.add))
                settle()
                did(dve.tensor_tensor(dd[:, 0:nt, 0:1], dd[:, 0:nt, 0:1], dd[:, 0:nt, 1:2], ALU.subtract))
                settle()
                did(dve.tensor_scalar(row_of[:, 0:2 * nt], dd[:, 0:nt, :].rearrange("p a k -> p (a k)"), -1.0, None, ALU.add))
                settle()
                did(dve.tensor_copy(dti2[L][:, 0:2 * nt], row_of[:, 0:2 * nt]))
                row_b = row_of[:, 0:2 * nt].unsqueeze(2)
                did(dve.tensor_tensor(past[:, 0:2 * nt, :], row_b.to_broadcast([P, 2 * nt, MAXB + 1]),
                                      row_iota[:, 0:MAXB + 1].unsqueeze(1).to_broadcast([P, 2 * nt, MAXB + 1]), ALU.is_ge))
                settle()
                did(dve.tensor_reduce(slot_of[:, 0:2 * nt], past[:, 0:2 * nt, :], AX_X, ALU.add))
                did(dve.tensor_tensor(in_block[:, 0:2 * nt, :], past[:, 0:2 * nt, 0:MAXB], past[:, 0:2 * nt, 1:MAXB + 1], ALU.subtract))
                settle()
                did(dve.scalar_tensor_tensor(out=slot_of[:, 0:2 * nt], in0=slot_of[:, 0:2 * nt], scalar=-float(ROWS),
                                             in1=row_of[:, 0:2 * nt], op0=ALU.mult, op1=ALU.add))
                did(dve.tensor_tensor(in_block[:, 0:2 * nt, :], in_block[:, 0:2 * nt, :],
                                      tok2[:, 0:2 * nt].unsqueeze(2).to_broadcast([P, 2 * nt, MAXB]), ALU.mult))
                settle()
                did(dve.tensor_scalar(slot_of[:, 0:2 * nt], slot_of[:, 0:2 * nt], float(ROWS), None, ALU.add))
                settle()
                did(dve.tensor_tensor(in_slot[:, 0:2 * nt, :], slot_of[:, 0:2 * nt].unsqueeze(2).to_broadcast([P, 2 * nt, ROWS]),
                                      row_iota[:, MAXB + 1:].unsqueeze(1).to_broadcast([P, 2 * nt, ROWS]), ALU.is_equal))
                settle()
                dve.sem_inc(sem("one_hots"), 1)
                key = (L, "idx")
                wait_full(dve, key)
                did(dve.tensor_copy(idx[:, 0:nb], bank(key)[0:ROWS, 0:nb]))
                release(key)
                dve.sem_inc(sem("idx"), 1)
                did(dve.tensor_tensor(gate[:, 0:nt, :], sc[:, 0:nt, :], mask[:, 0:nt, :], ALU.mult))
                settle()
                did(dve.tensor_reduce(gsum[:, 0:nt, 0], gate[:, 0:nt, :], AX_X, ALU.add))
                settle()
                did(dve.reciprocal(gsum[:, 0:nt, 1], gsum[:, 0:nt, 0]))
                settle()
                did(dve.tensor_tensor(gate[:, 0:nt, :], gate[:, 0:nt, :], gsum[:, 0:nt, 1:2].to_broadcast([P, nt, E]), ALU.mult))
                for k in range(2):
                    pick = cmp1[:, 0:nt * E].rearrange("p (a e) -> p a e", e=E)
                    did(dve.tensor_tensor(pick, d_, dd[:, 0:nt, k:k + 1].to_broadcast([P, nt, E]), ALU.is_equal))
                    settle()
                    did(dve.tensor_tensor(pick, pick, gate[:, 0:nt, :], ALU.mult))
                    settle()
                    did(dve.tensor_reduce(gk[:, 0:nt, k], pick, AX_X, ALU.add))
                    settle()

                n = dve.value_load(be_i[0:1, MAXB:MAXB + 1], min_val=1, max_val=nb)
                base = (unit0[L] + 2 * len(DENSE[L])) // RING

                def copy_rows(b):
                    dve.wait_ge(sem("turned", L), b + 2)
                    dve.tensor_copy(xgT.rearrange("p k t -> p (k t)"), banks[0][:, :]).then_inc(sem("xgT", L), 1)

                def index_column(b):
                    dve.tensor_copy(idx_now[:, 0:1], idx[:, bass.ds(b, 1)]).then_inc(sem("idx_col", L), 1)

                dve.sem_inc(sem("hm", L), 1)
                index_column(0)
                copy_rows(0)
                with dve.Fori(0, nb) as b:
                    with dve.If(b < n):
                        with dve.If(b + 1 < n):
                            dve.wait_ge(sem("gathered", L), (b + 1) * 16)
                            index_column(b + 1)
                        dve.wait_ge(sem("sg", L), b + 1)
                        dve.wait_ge(used[3], b + base + 1)
                        dve.wait_ge(sem("hm_turned", L), b + 1)
                        dve.tensor_tensor(hm, sg, banks[3][:, 0:256], ALU.mult).then_inc(sem("hm", L), 1)
                        with dve.If(b + 1 < n):
                            copy_rows(b + 1)
                        dve.wait_ge(sem("hm_turned", L), b + 2)
                        dve.wait_ge(used[5], b + base)
                        dve.tensor_copy(hmT.rearrange("p c t -> p (c t)"), banks[4][:, 0:256]).then_inc(sem("hmT", L), 1)
                def weigh(i):
                    y0, y1 = ytok[:, i % 2, 0, :], ytok[:, i % 2, 1, :]
                    dve.wait_ge(sem("y_gathered", i % 2), 32 * (i // 2 + 1 + 2 * L))
                    dve.wait_ge(sem("y1_scaled"), i + 1 + 4 * L)
                    did(dve.scalar_tensor_tensor(out=y0, in0=y0, scalar=gk[:, i, 0:1], in1=y1, op0=ALU.mult, op1=ALU.add),
                        sem("y_tok", L))

                weigh(0)
                for i, t in enumerate(tts):
                    if i + 1 < len(tts):
                        weigh(i + 1)
                    for half in range(2):
                        key = (L, "yt", i, half)
                        wait_full(dve, key)
                        for q in range(4):
                            k = 4 * half + q
                            x = xT[:, k, t * P:(t + 1) * P]
                            g = t // 2
                            did(dve.scalar_tensor_tensor(out=x, in0=bank(key)[:, q * P:(q + 1) * P],
                                                         scalar=modT[:, L, 40 + k, 1 - g:2 - g], in1=x, op0=ALU.mult, op1=ALU.add))
                        release(key)
                    dve.sem_inc(sem("y_tok_read", L), 1)
                dve.sem_inc(sem("x_done"), 1)
            L = LAYERS
            inverse_root(2 * L, SEG)
            for k in range(KD):
                did(dve.scalar_tensor_tensor(out=hT[:, k, SEG:TOK], in0=xT[:, k, SEG:TOK], scalar=normf[:, k:k + 1],
                                             in1=rs[:, SEG:TOK], op0=ALU.mult, op1=ALU.mult), sem("final"))


def constants():
    f = np.float32
    p = np.arange(P)
    same_head = (p[:, None] // HD == p[None, :] // HD).astype(f) / HD

    def rotation(d):
        r = np.zeros((P, P), f)
        for m in range(P):
            base, o = m // d * d, m % d
            if o < d // 2:
                r[base + o + d // 2, m] = -1
            else:
                r[base + o - d // 2, m] = 1
        return r

    mats = np.stack([np.eye(P, dtype=f), same_head, np.full((P, P), 1 / D, f),
                     (p[:, None] < p[None, :]).astype(f), np.ones((P, P), f), rotation(HD), rotation(HD // 2)], 1)

    def axial(d):
        n = d // 4
        inv = (np.float32(10000.0) ** (-np.arange(n, dtype=f) / f(n))).astype(f)
        t = np.arange(SEG)
        ang = np.concatenate([(t // GRID_W).astype(f)[:, None] * inv, (t % GRID_W).astype(f)[:, None] * inv], 1).astype(f)
        c = np.tile(np.cos(ang).astype(f).T, (2 * P // d, 1))
        s = np.tile(np.sin(ang).astype(f).T, (2 * P // d, 1))
        return c, s

    rope = np.stack([*axial(HD), *axial(HD // 2)], 1)
    s = (np.arange(2)[None, :, None] * P + p[:, None, None])
    t = np.arange(SEG)[None, None, :]
    dist = np.stack([np.abs(t - s), SEG + t - s, SEG - t + s], 1).astype(f)
    lev = np.zeros((P, len(LEVELS), P), np.uint8)
    for n, h in enumerate(LEVELS):
        if h:
            a, b = p[:, None], p[None, :]
            lev[:, n, :] = (a // (2 * h) == b // (2 * h)) & (a // h != b // h)
    return {
        "k_mats": mats, "k_mod_sel": (p[:, None] % 32 == np.arange(2)[None]).astype(f), "k_rope": rope.astype(f),
        "k_dist": dist, "k_later": (s > t).astype(np.int32).reshape(P, TOK), "k_levels": lev.astype(np.int32).reshape(P, -1),
        "k_before4": np.broadcast_to((np.arange(4)[None, :] < np.arange(4)[:, None]).astype(f), (P, 4, 4)),
        "k_grank": np.broadcast_to((G - np.arange(G)).astype(f), (P, G)),
        "k_rows": np.broadcast_to(np.concatenate([ROWS * np.arange(MAXB + 1), np.arange(ROWS)]).astype(f), (P, MAXB + 1 + ROWS)),
        "k_tok": (p[:, None] + P * np.arange(4)[None]).astype(f),
    }


def kernel(**inputs):
    import concourse.bacc as bacc
    from concourse.bass_utils import run_bass_kernel_spmd

    a = {k: np.asarray(v) for k, v in inputs.items()}

    def feature_major(v):
        return np.moveaxis(v.reshape(*v.shape[:-1], v.shape[-1] // P, P), -1, 0)

    w = a["w_in"]
    col = lambda i, n: w[:, :, i:i + n]
    gq = w[:, :, 1024:1280].reshape(LAYERS, D, 4, HD)[:, :, [0, 2, 1, 3], :].reshape(LAYERS, D, 256)
    w_in = np.concatenate([
        col(0, 256), col(256, 256), col(768, 256), gq, col(1280, 128), col(512, 256), col(1408, 128),
        col(1536, 256), col(1792, 256), col(2048, 256), col(2560, 256), col(2304, 256), col(3328, 256),
        col(2816, 256), col(3072, 256)], axis=2)
    both = np.concatenate([a["ctx"][0], a["x"][0]], 0)
    twice = lambda g: np.concatenate([g, g], 1).T
    arrays = {
        "xT": np.moveaxis(both.reshape(TOK, KD, P), -1, 0).transpose(0, 2, 1),
        "cc": np.stack([a["c"][0], a["c_ctx"]], -1).reshape(KD, P, 2).transpose(1, 0, 2),
        "w_mod": a["w_mod"], "w_in": w_in, "w_out": a["w_out"],
        "b_mod": feature_major(a["b_mod"]), "norm1": feature_major(a["norm1_g"]), "norm2": feature_major(a["norm2_g"]),
        "normf": feature_major(a["final_norm_g"]),
        "head_g": np.stack([twice(a[k]) for k in ("ret_norm_g", "gqa_qnorm_g", "gqa_knorm_g", "hgrn_norm_g", "diff_norm_g")], 1),
        "decay": a["ret_decay_logit"], "lb_logit": feature_major(a["hgrn_lb_logit"]), "lam": a["diff_lambda"],
        "router_w": a["router_w"].reshape(KD, P, E).transpose(1, 0, 2), "router_b": a["router_bias"],
        "w_gate": a["moe_w_gate"], "w_up": a["moe_w_up"], "w_down": a["moe_w_down"], **constants(),
    }
    arrays = {k: np.ascontiguousarray(v) for k, v in arrays.items()}
    nc = bacc.Bacc("TRN2", target_bir_lowering=False, num_devices=1)
    A = {k: nc.dram_tensor(f"in_{k}", v.shape, mybir.dt.from_np(v.dtype), kind="ExternalInput").ap() for k, v in arrays.items()}
    A["outT"] = nc.dram_tensor("out_T", (P, KD, SEG), F32, kind="ExternalOutput").ap()
    build_program(nc, A)
    r = run_bass_kernel_spmd(nc, [{f"in_{k}": v for k, v in arrays.items()}], core_ids=[0])
    out = r.results[0]["out_T"]
    return np.ascontiguousarray(out.transpose(2, 1, 0).reshape(1, SEG, D))
```

```python
import math
from contextlib import ExitStack

import concourse.bass as bass
import numpy as np
from concourse import mybir

F32 = mybir.dt.float32
I32 = mybir.dt.int32
U8 = mybir.dt.uint8
ALU = mybir.AluOpType
ACT = mybir.ActivationFunctionType
AX_X = mybir.AxisListType.X

P = 128
D = 1024
KD = D // P
LAYERS = 2
SEG = 256
TOK = 2 * SEG
HD = 64
HEADS = 4
GRID_W = 64
E = 32
G = 8
FF = 512
ROWS = 64
MAXB = 48
EPS = 1e-6
NF = 21
VW = 896
RING = 6
MOD_FIRST = 4
MOD_LATER = [(0, u) for u in range(MOD_FIRST, 12)] + [(1, u) for u in range(12)]
DENSE = [
    [("mod", 0, u) for u in range(MOD_FIRST)] + [("in", 0, i) for i in range(7)] + [("mod", *lu) for lu in MOD_LATER]
    + [("out", 0, i) for i in range(2)],
    [("in", 1, i) for i in range(7)] + [("out", 1, i) for i in range(2)],
]
LEVELS = [0, 1, 2, 4, 8, 16, 32, 64]
ROPED_FIRST, ROPED_LAST = [0, 1, 2, 3, 6, 7, 8], [17, 18, 19, 20]
ROPED = ROPED_FIRST + ROPED_LAST
TINY = 2.0 ** -63
RQ, RK, RG, GQ, GK, HQ, ZF, ZB, HG, DQ, DK = 0, 2, 4, 6, 8, 9, 11, 13, 15, 17, 19
QUERY_TILES = (RQ, RQ + 1, RG, RG + 1, GQ, GQ + 1, HQ, HQ + 1, HG, HG + 1, DQ, DQ + 1)
VCOL = {"ret": 0, "gqa": 256, "hg": 384, "df": 640}
MIXERS = ["ret", "gqa", "hg", "df"]
MAPS = {"gqa": 1, "df": 2}
LEVELS_ALL = 10
NORMED = [("ret", 0), ("ret", 1), ("hg", 0), ("hg", 1), ("df", 0), ("df", 1)]
MIXTILE = {"ret": RQ, "gqa": RK, "hg": HQ, "df": DQ}
PER_LAYER = dict(
    h_ready=8, h2_ready=8, feat_ready=21, v_ready=8, gsq=3,
    groot=3, gnorm=3, oroot=6, osq=6,
    roped=11, mixed=8, gates=4, fgate=4, flog=4, qk=20,
    qk_arg=18, qk_exp=18, dec=16, dec_free=8, mix_read=1, x_mixed=1,
    mask=1, idx=1, table=1, scores=1, scores_T=1, y_all=1,
    x_done=1, one_hots=1, normed=6)
assert all(2 * len(d) % RING == 0 for d in DENSE)


def max_blocks(n_tokens):
    most = E + (2 * n_tokens) // (ROWS + 1)
    return most + most % 2


def usual_rows(layer):
    return 2 * len(token_tiles(layer)) * P // E + 8


def token_tiles(layer):
    return [0, 1, 2, 3] if layer < LAYERS - 1 else [2, 3]


def segments(layer):
    return [0, 1] if layer < LAYERS - 1 else [1]


PROJ_FIRST = [("feat", f) for f in range(9)] + [("v", 0, t) for t in range(4)]
PROJ_BESIDE = [("feat", f) for f in range(9, 17)] + [("v", 1, t) for t in range(4)] + [("feat", f) for f in range(17, 21)]


def chunk_of(item):
    if item[0] == "v":
        return (2, P, 384) if item[1] == 0 else (5, 0, 512)
    f = item[1]
    if f < 9:
        return f // 4, f % 4 * P, P
    return (3 + (f - 9) // 4, (f - 9) % 4 * P, P) if f < 17 else (6, (f - 17) * P, P)


def last_of_chunk(item):
    items = PROJ_FIRST + PROJ_BESIDE
    at = items.index(item)
    return at + 1 == len(items) or chunk_of(items[at + 1])[0] != chunk_of(item)[0]


def first_of_chunk(item):
    items = PROJ_FIRST + PROJ_BESIDE
    at = items.index(item)
    return at == 0 or chunk_of(items[at - 1])[0] != chunk_of(item)[0]


def norms_beside(layer, step):
    return [x for x in range(4) if step == 1 + 2 * x]


def proj_beside(layer, hook):
    hooks = 4 + HEADS * len(token_tiles(layer)) + 2
    n = len(PROJ_BESIDE)
    return [x for k, x in enumerate(PROJ_BESIDE) if k * hooks // n == hook]


def mod_later(layer, step):
    if layer:
        return []
    jobs = [(MOD_LATER[step][0], "mod", MOD_LATER[step][1])]
    if step:
        jobs.append((MOD_LATER[step - 1][0], "modT", MOD_LATER[step - 1][1]))
    if step == len(MOD_LATER) - 1:
        jobs.append((MOD_LATER[step][0], "modT", MOD_LATER[step][1]))
    return jobs


def softmax_steps(L, name):
    pairs = HEADS * len(token_tiles(L))
    per = pairs // 2
    for n in range(pairs + 2):
        yield (n if n < pairs else None, n - 1 if 1 <= n <= pairs else None, n - 2 if n >= 2 else None,
               (n - 2) // per if n >= 2 and (n - 2) % per == per - 1 else None)


def softmax_pair(L, n):
    tts = token_tiles(L)
    return n // len(tts), tts[n % len(tts)]


def softmax_jobs(L, name):
    jobs = []
    for step, (made, _, turned, j) in enumerate(softmax_steps(L, name)):
        if made is not None:
            jobs += [(L, "s", name, m, made) for m in range(MAPS[name])]
        if turned is not None:
            jobs.append((L, "t", name, turned))
        if j is not None:
            jobs.append((L, "pv", name, j))
        if name == "gqa":
            jobs += [(L, *x) for x in proj_beside(L, 4 + step)]
        else:
            jobs += [(L, "oss", x) for x in norms_beside(L, step)]
    return jobs


def plan_jobs():
    jobs = []
    for L in range(LAYERS):
        segs, tts = segments(L), token_tiles(L)
        jobs.append((L, "ss1"))
        if L == 0:
            for u in range(MOD_FIRST):
                jobs += [(0, "mod", u)] + ([(0, "modT", u - 1)] if u else [])
            jobs.append((0, "modT", MOD_FIRST - 1))
        jobs += [(L, *x) for x in PROJ_FIRST]
        jobs += [(L, "gss", i) for i in range(3)]
        jobs += [(L, "rope", f) for f in ROPED_FIRST]
        for j in range(2):
            for hh in range(2):
                jobs += [(L, "rs", 2 * j + hh, part) for part in ([0] if 0 in segs else []) + [1, 2]]
                jobs += [(L, *x) for x in proj_beside(L, 2 * j + hh)]
            jobs += [(L, "pv", "ret", j)]
        jobs += softmax_jobs(L, "gqa")
        for j in range(2):
            for lev in range(LEVELS_ALL + 1):
                if lev < LEVELS_ALL:
                    jobs += [(L, "hl", j, lev, hh) for hh in range(2)] + mod_later(L, j * LEVELS_ALL + lev)
            jobs += [(L, "pv", "hg", j)]
        jobs += [(L, "rope", f) for f in ROPED_LAST]
        jobs += softmax_jobs(L, "df")
        jobs += [(L, "oss", x) for x in range(4, len(NORMED))]
        jobs += [(L, "out", f) for f in range(KD)]
        jobs.append((L, "ss2"))
        jobs += [(L, "router"), (L, "routerT")]
        for i in range(len(tts)):
            jobs += [(L, "h2t", i, half) for half in range(2)]
        jobs += [(L, "pos"), (L, "idx")]
        for i in range(len(tts)):
            jobs += [(L, "yt", i, half) for half in range(2)]
    jobs.append((LAYERS, "ssf"))
    return jobs


class Steps:

    def __init__(self, eng, own):
        self.eng, self.own, self.counts, self.open = eng, own, {}, {}

    def did(self, ins, sem=None):
        sem = self.own if sem is None else sem
        ins.then_inc(sem, 1)
        self.counts[id(sem)] = self.counts.get(id(sem), 0) + 1
        self.open[id(sem)] = (sem, self.counts[id(sem)])

    def settle(self):
        for sem, n in self.open.values():
            self.eng.wait_ge(sem, n)
        self.open = {}


def build_program(nc, A):
    jobs = plan_jobs()
    job_number = {key: n for n, key in enumerate(jobs)}

    with ExitStack() as ctx:
        def sb(name, shape, dt=F32):
            return ctx.enter_context(nc.sbuf_tensor(name, shape, dt))

        named = {}

        def sem(*name):
            name = "_".join(map(str, name))
            if name not in named:
                named[name] = ctx.enter_context(nc.semaphore(name))
            return named[name]

        mats = sb("mats", [P, 7, P])
        IDENT, HEAD_MEAN, ALL_MEAN, BEFORE, ONES, ROT_HD, ROT_DF = (mats[:, i, :] for i in range(7))
        mod_sel = sb("mod_sel", [P, 2])
        rope = sb("rope", [P, 4, SEG])
        dist = sb("dist", [P, 2, 2, SEG])
        later = sb("later", [P, 2, SEG], U8)
        levels = sb("levels", [P, len(LEVELS), P], U8)
        iota_e = sb("iota_e", [P, 4, 4])
        g_rank = sb("g_rank", [P, G])
        row_iota = sb("row_iota", [P, MAXB + 1 + ROWS])
        tok_id = sb("tok_id", [P, 4])
        cc = sb("cc", [P, KD, 2])
        ccs = sb("ccs", [P, KD, 32])
        b_mod = sb("b_mod", [P, LAYERS, 48])
        norm1 = sb("norm1", [P, LAYERS, KD])
        norm2 = sb("norm2", [P, LAYERS, KD])
        normf = sb("normf", [P, KD])
        head_g = sb("head_g", [P, 5, LAYERS])
        decay_logit = sb("decay_logit", [P, LAYERS, 2, HEADS])
        log_decay = sb("log_decay", [P, LAYERS, 2, HEADS])
        back_decay = sb("back_decay", [P, LAYERS, 2, HEADS])
        seg_decay = sb("seg_decay", [P, LAYERS, 2, HEADS])
        lb_logit = sb("lb_logit", [P, 2, LAYERS, 2])
        lb_soft = sb("lb_soft", [P, 2, LAYERS, 2])
        lb = sb("lb", [P, 2, LAYERS, 2])
        one_m_lb = sb("one_m_lb", [P, 2, LAYERS, 2])
        lb_tmp = sb("lb_tmp", [P, 2, 2, 2])
        lam_in = sb("lam_in", [P, LAYERS, 4, 32])
        lam_pr = sb("lam_pr", [P, LAYERS, 2, 32])
        lam_ex = sb("lam_ex", [P, LAYERS, 2])
        neg_lam = sb("neg_lam", [P, LAYERS])
        router_w = sb("router_w", [P, KD, E])
        router_b = sb("router_b", [P, E])
        ring = sb("ring", [P, RING, 4, 512])
        xT = sb("xT", [P, KD, TOK])
        hT = sb("hT", [P, KD, TOK])
        featT = sb("featT", [P, NF, TOK])
        vtok = sb("vtok", [P, 4, VW])
        Wst = sb("Wst", [P, 2, 6, SEG])
        scratch_masks = Wst[:, 0, :, :].rearrange("p a t -> p (a t)")
        modT = sb("modT", [P, LAYERS, 48, 2])
        mod_rows = sb("mod_rows", [P, 2, 512])
        mscale = sb("mscale", [P, 2, KD, 2])
        sq = sb("sq", [P, 2, TOK])
        rs2 = sb("rs2", [P, 2, TOK])
        rs = rs2[:, 0, :]
        eps = sb("eps", [P, 1])
        scratch = sb("scratch", [P, 7 * TOK])
        dec = scratch[:, 0:3 * TOK].rearrange("p (a b t) -> p a b t", a=3, b=2)
        prob = scratch[:, 0:6 * TOK].rearrange("p (b m t) -> p b m t", b=3, m=2)
        rot = scratch[:, 6 * TOK:7 * TOK].rearrange("p (a t) -> p a t", a=2)
        fgs = scratch[:, 0:4 * TOK].rearrange("p (a t) -> p a t", a=4)
        qk = scratch[:, TOK:7 * TOK].rearrange("p (b a t) -> p b a t", b=3, a=2)
        hn = scratch[:, 5 * TOK:7 * TOK].rearrange("p (a t) -> p a t", a=2)
        cums = sb("cums", [P, 2, 2, 2, SEG + 1])
        stat = sb("stat", [P, 6, 4])
        def room(at, width, dt=F32):
            flat = featT[:, :, :].rearrange("p f t -> p (f t)")[:, at:at + width]
            return flat if dt == F32 else flat.bitcast(dt)
        flat_W, flat_v = Wst[:, :, :, :].rearrange("p a b t -> p (a b t)"), vtok[:, :, :].rearrange("p t n -> p (t n)")
        spare = [x.rearrange("p (k n) -> p k n", k=4) for x in
                 (flat_v[:, 0:2048], flat_W[:, 0:2048], scratch[:, 0:2048], room(3840, 2048), room(5888, 2048), room(7936, 2048))]
        h2tok = [room(0, 1024), scratch[:, 5 * TOK:7 * TOK]]
        xg = [room(1024, 1024)[0:ROWS, :], scratch[0:ROWS, 5 * TOK:7 * TOK]]
        scT = room(1024, TOK)[0:E, :]
        xgT = room(2048, 512).rearrange("p (k t) -> p k t", k=KD)
        sg = room(2560, 256)
        hm = room(2816, 256)
        hmT = room(3072, 256).rearrange("p (c t) -> p c t", c=2)
        ysb = [room(3328, 512), scratch[:, 2048:2560]]
        ytok = room(0, 8192).rearrange("p (b k d) -> p b k d", b=4, k=2)
        sc = sb("sc", [P, 4, E])
        sel = sb("sel", [P, 4, E])
        cmp1, cmp2 = sq[:, 0, :], sq[:, 1, :]
        past = flat_W[:, 2048:2048 + 8 * (MAXB + 1)].rearrange("p (a b) -> p a b", b=MAXB + 1)
        in_block = flat_W[:, 2560:2560 + 8 * MAXB].rearrange("p (a b) -> p a b", b=MAXB)
        in_slot = scratch[:, 2048:2048 + 8 * ROWS].rearrange("p (a s) -> p a s", s=ROWS)
        gsc = sb("gsc", [P, 4, G])
        gbest = sb("gbest", [P, 4, 2])
        goh = sb("goh", [P, 4, G])
        mask = sb("mask", [P, 5, E])
        gate = sb("gate", [P, 4, E])
        gsum = sb("gsum", [P, 4, 2])
        posn = room(10432, 4 * E).rearrange("p (a e) -> p a e", e=E)
        cnt = sb("cnt", [P, E])
        nblk = room(10688, 2 * E).rearrange("p (a e) -> p a e", e=E)
        tok2 = sb("tok2", [P, 8])
        row_of = sb("row_of", [P, 8])
        slot_of = sb("slot_of", [P, 8])
        zeros = sb("zeros", [P, 256])
        blk_end = sb("blk_end", [P, E])
        row0 = sb("row0", [P, E])
        end_row = sb("end_row", [1, E])
        row0_excess = sb("row0_excess", [P, 2])
        dst = room(10560, 4 * E).rearrange("p (a e) -> p a e", e=E)
        dd = sb("dd", [P, 4, 2])
        gk = sb("gk", [P, 4, 2])
        be_cmp = flat_v[:, 2048:2048 + MAXB * E]
        be = sb("be", [1, MAXB + 1])
        be_i = sb("be_i", [1, MAXB + 1], I32)
        idx = sb("idx", [ROWS, MAXB + 2], I32)
        idx_f = sb("idx_f", [ROWS, MAXB])
        filled = sb("filled", [ROWS, MAXB], I32)
        idx_now = sb("idx_now", [ROWS, 2], I32)
        dti2 = [sb(f"rows_of_token_{L}", [P, 8], I32) for L in range(LAYERS)]

        banks = [ctx.enter_context(nc.psum_tensor(f"bank{i}", [P, 512], F32)) for i in range(8)]
        dram = {}
        for L in range(LAYERS):
            nt = len(token_tiles(L)) * P
            nb = max_blocks(nt)
            dram[L] = dict(
                h2=nc.dram_tensor(f"h2_{L}", (nt, D), F32, kind="Internal").ap(),
                nb=nb)
        y_dram = nc.dram_tensor("y_rows", (MAXB * ROWS, D), F32, kind="Internal").ap()

        unit0 = [0]
        for L in range(LAYERS):
            unit0.append(unit0[-1] + 2 * len(DENSE[L]) + dram[L]["nb"] // 2 * 6)
        first_unit = {what: unit0[L] + 2 * n for L in range(LAYERS) for n, what in enumerate(DENSE[L])}
        landed = [sem("landed", i) for i in range(RING)]
        used = [sem("used", i) for i in range(RING)]
        spare_landed = [sem("spare_landed", i) for i in range(6)]
        ring_loads = [(unit0[L] + 2 * len(DENSE[L])) // RING for L in range(LAYERS)]
        spare_loads = [sum(dram[x]["nb"] // 2 for x in range(L)) for L in range(LAYERS)]
        full = [sem("bank_full", i) for i in range(8)]
        free = [sem("bank_free", i) for i in range(8)]

        def h2_stores(L, i):
            return sum(len(token_tiles(x)) // 2 for x in range(L)) + i // 2 + 1

        def bank(key):
            return banks[job_number[key] % 8]

        def wait_full(eng, key):
            n = job_number[key]
            eng.wait_ge(full[n % 8], n // 8 + 1)

        def free_sem(key):
            return free[job_number[key] % 8]

        def unit(n):
            return ring[:, n % RING, :, :]

        def weights(odd, i):
            if not odd:
                return ring[:, i, :, :] if i < 4 else down_unit(i)
            return spare[i] if i < 4 else spare[i].rearrange("p k n -> p (k n)").rearrange("p (k n) -> p k n", k=2)

        def down_unit(i):
            return ring[:, i, :, :].rearrange("p a n -> p (a n)").rearrange("p (k n) -> p k n", k=2)

        def load_dense(sp, L, n0, n1):
            for m in range(n0, n1):
                what, lw, c = DENSE[L][m // 2]
                n, k = unit0[L] + m, m % 2
                src = A["w_" + what][lw].rearrange("(k p) n -> p k n", p=P)[:, 4 * k:4 * k + 4, 512 * c:512 * c + 512]
                if n >= RING:
                    sp.wait_ge(used[n % RING], n // RING + spare_loads[L])
                sp.dma_start(unit(n), src).then_inc(landed[n % RING], 16)

        def release_after(pe, key, units):
            wait_full(pe, key)
            for n in units:
                pe.sem_inc(used[n % RING], 1)

        block = ctx.enter_context(nc.Block())

        @block.sync
        def _(sp):
            early = [(cc[:, :, :], A["cc"], "cc_in"), (xT[:, :, :], A["xT"], "x_in")]
            first = [(mats[:, :, :], A["k_mats"]), (mod_sel[:, :], A["k_mod_sel"]), (b_mod[:, :, :], A["b_mod"]),
                     (norm1[:, :, :], A["norm1"])]
            small = [
                (rope[:, :, :], A["k_rope"]), (head_g[:, :, :], A["head_g"]), (dist[:, :, :, :], A["k_dist"]),
                (decay_logit[:, :, :, :], A["decay"].partition_broadcast(P)),
                (scratch_masks[:, 0:TOK].bitcast(I32), A["k_later"]),
                (scratch_masks[:, TOK:TOK + len(LEVELS) * P].bitcast(I32), A["k_levels"]),
                (lb_logit[:, :, :, :], A["lb_logit"]), (lam_in[:, :, :, :], A["lam"].partition_broadcast(P)),
                (iota_e[:, :, :], A["k_before4"]), (g_rank[:, :], A["k_grank"]),
                (row_iota[:, :], A["k_rows"]), (tok_id[:, :], A["k_tok"]),
                (norm2[:, :, :], A["norm2"]), (normf[:, :], A["normf"]),
                (router_w[:, :, :], A["router_w"]), (router_b[:, :], A["router_b"].partition_broadcast(P)),
            ]
            for dst, src, name in early:
                sp.dma_start(dst, src).then_inc(sem(name), 16)
            for dst, src in first:
                sp.dma_start(dst, src).then_inc(sem("first_in"), 16)
            load_dense(sp, 0, 0, RING)
            for dst, src in small:
                sp.dma_start(dst, src).then_inc(sem("small_in"), 16)
            sp.wait_ge(sem("first_in"), 16 * len(first))
            sp.sem_inc(sem("first_ready"), 1)
            sp.wait_ge(sem("small_in"), 16 * len(small))
            sp.sem_inc(sem("small_ready"), 1)
            for L in range(LAYERS):
                if L:
                    sp.wait_ge(sem("y_all_gathered"), 1)
                load_dense(sp, L, RING if L == 0 else 0, 2 * len(DENSE[L]))
                d = dram[L]

                base = ring_loads[L] + spare_loads[L]

                def load_expert(e, odd, used_before):
                    for i in range(6):
                        if used_before is not None:
                            sp.wait_ge(used[i], used_before)
                        src = [A["w_gate"], A["w_up"], A["w_down"]][i // 2]
                        rows = src[L, bass.ds(e, 1), :, :].rearrange("o a b -> (o a) b")
                        if i < 4:
                            rows = rows.rearrange("(k p) n -> p k n", p=P)[:, 4 * (i % 2):4 * (i % 2) + 4, :]
                        else:
                            rows = rows.rearrange("(k p) n -> p k n", p=P)[:, 2 * (i % 2):2 * (i % 2) + 2, :]
                        sp.dma_start(weights(odd, i), rows).then_inc((spare_landed if odd else landed)[i], 16)

                load_expert(0, 0, base)
                sp.wait_ge(sem("mix_read"), L + 1)
                load_expert(1, 1, None)
                sp.wait_ge(sem("table"), L * PER_LAYER["table"] + 1)
                n = sp.value_load(be_i[0:1, MAXB:MAXB + 1], min_val=2, max_val=d["nb"])
                with sp.Fori(1, d["nb"] // 2) as pair:
                    for odd in range(2):
                        b = pair * 2 + odd
                        with sp.If(b < n):
                            e = sp.value_load(be_i[0:1, bass.ds(b, 1)], min_val=0, max_val=E - 1)
                            load_expert(e, odd, b + (base - 1))
                        with sp.Else():
                            for i in range(6):
                                if odd:
                                    sp.wait_ge(spare_landed[i], (pair + spare_loads[L]) * 16)
                                    sp.sem_inc(spare_landed[i], 16)
                                else:
                                    sp.wait_ge(landed[i], (pair + ring_loads[L]) * 16)
                                    sp.sem_inc(landed[i], 16)
            for half in range(2):
                ks = slice(KD // 2 * half, KD // 2 * (half + 1))
                sp.wait_ge(sem("final"), ks.stop)
                sp.dma_start(A["outT"][:, ks, :], hT[:, ks, SEG:TOK]).then_inc(sem("out_stored"), 16)
            sp.wait_ge(sem("out_stored"), 32)

        @block.tensor
        def _(pe):
            order = iter(jobs)

            def begin(*key):
                assert next(order) == key, key
                n = job_number[key]
                if n >= 8:
                    pe.wait_ge(free[n % 8], n // 8)
                return banks[n % 8]

            def end(ins, key):
                ins.then_inc(full[job_number[key] % 8], 1)

            def arrived(n):
                pe.wait_ge(landed[n % RING], 16 * (n // RING + 1))

            def mm(out, lhsT, rhs, start, stop, **kw):
                return pe.matmul(out, lhsT, rhs, start=start, stop=stop, skip_group_check=True, **kw)

            for L in range(LAYERS):
                segs, tts = segments(L), token_tiles(L)
                lo = 0 if 0 in segs else SEG

                def modulation(lm, u):
                    ps = begin(lm, "mod", u)
                    n = first_unit[("mod", lm, u)]
                    arrived(n)
                    arrived(n + 1)
                    for half in range(2):
                        for q in range(4):
                            ins = mm(ps[32 * q:32 * q + 32, :], ccs[:, 4 * half + q, :], unit(n + half)[:, q, :],
                                     half == 0, half == 1, tile_position=(0, 32 * q))
                    end(ins, (lm, "mod", u))
                    release_after(pe, (lm, "mod", u), [n, n + 1])

                def mod_turn(lm, u):
                    ps = begin(lm, "modT", u)
                    m = 12 * lm + u
                    pe.wait_ge(sem("mod_rows"), m + 1)
                    for q in range(4):
                        ins = mm(ps[:, 2 * q:2 * q + 2], mod_rows[:, m % 2, q * P:(q + 1) * P], mod_sel[:, :], True, True)
                    end(ins, (lm, "modT", u))

                def mean_squares(name, lo):
                    ps = begin(L, name)
                    for k in range(KD):
                        pe.wait_ge(sem(name, "sq", L), k + 1)
                        ins = mm(ps[:, lo:TOK], ALL_MEAN, sq[:, k % 2, lo:TOK], k == 0, k == KD - 1)
                        if k < KD - 1:
                            ins.then_inc(sem(name, "sq_read", L), 1)
                    end(ins, (L, name))

                if L == 0:
                    pe.wait_ge(sem("first_ready"), 1)
                mean_squares("ss1", 0)
                if L == 0:
                    pe.wait_ge(sem("cc_silu"), 1)
                    for u in range(MOD_FIRST):
                        modulation(0, u)
                        if u:
                            mod_turn(0, u - 1)
                    mod_turn(0, MOD_FIRST - 1)
                    pe.wait_ge(sem("small_ready"), 1)

                base = first_unit[("in", L, 0)]
                pe.wait_ge(sem("h_ready"), L * PER_LAYER["h_ready"] + KD)

                def project(item):
                    c, c0, w = chunk_of(item)
                    n = base + 2 * c
                    ps = begin(L, *item)
                    if first_of_chunk(item):
                        arrived(n)
                        arrived(n + 1)
                    for k in range(KD):
                        weights = unit(n + k // 4)[:, k % 4, c0:c0 + w]
                        if item[0] == "feat":
                            q_lo = lo if item[1] in QUERY_TILES else 0
                            ins = mm(ps[:, q_lo:TOK], weights, hT[:, k, q_lo:TOK], k == 0, k == KD - 1)
                        else:
                            t = item[2]
                            ins = mm(ps[:, 0:w], hT[:, k, t * P:(t + 1) * P], weights, k == 0, k == KD - 1)
                    end(ins, (L, *item))
                    if last_of_chunk(item):
                        release_after(pe, (L, *item), [n, n + 1])

                for item in PROJ_FIRST:
                    project(item)

                for i in range(3):
                    ps = begin(L, "gss", i)
                    pe.wait_ge(sem("gsq"), L * PER_LAYER["gsq"] + i + 1)
                    end(mm(ps[:, :], HEAD_MEAN, sq[:, i % 2, :], True, True), (L, "gss", i))
                def rotate(tiles):
                    for f in tiles:
                        ps = begin(L, "rope", f)
                        if f in (GQ, GQ + 1, GK):
                            pe.wait_ge(sem("gnorm"), L * PER_LAYER["gnorm"] + f - GQ + 1)
                        else:
                            pe.wait_ge(sem("feat_ready"), L * PER_LAYER["feat_ready"] + f + 1)
                        end(mm(ps[:, 0:SEG], ROT_HD if f < DQ else ROT_DF, featT[:, f, SEG:TOK], True, True), (L, "rope", f))

                rotate(ROPED_FIRST)

                def value_product(mixer, j):
                    ps = begin(L, "pv", mixer, j)
                    pe.wait_ge(sem("v_ready"), L * PER_LAYER["v_ready"] + (4 if mixer in ("ret", "gqa") else 8))
                    for hh in range(2):
                        pe.wait_ge(sem("W_ready", mixer), L * HEADS + 2 * j + hh + 1)
                        vh = j if mixer == "gqa" else 2 * j + hh
                        vc = VCOL[mixer] + HD * vh
                        for g in segs:
                            parts = [(0, 0), (1, 1)] if g == 0 else [(4, 0), (5, 1), (2, 2), (3, 3)]
                            for n, (w, t) in enumerate(parts):
                                ins = mm(ps[HD * hh:HD * hh + HD, g * SEG:(g + 1) * SEG], vtok[:, t, vc:vc + HD],
                                         Wst[:, hh, w, :], n == 0, n == len(parts) - 1, tile_position=(0, HD * hh))
                    end(ins, (L, "pv", mixer, j))

                def head_mean(x):
                    ps = begin(L, "oss", x)
                    pe.wait_ge(sem("osq"), L * PER_LAYER["osq"] + x + 1)
                    end(mm(ps[:, lo:TOK], HEAD_MEAN, sq[:, x % 2, lo:TOK], True, True), (L, "oss", x))

                def attention(mixer):
                    for step, (made, _, turned, j) in enumerate(softmax_steps(L, mixer)):
                        if made is not None:
                            h, i = softmax_pair(L, made)
                            keys = TOK if i >= 2 else SEG
                            for m in range(MAPS[mixer]):
                                if mixer == "gqa":
                                    r0, width, fq, fk = HD * (h // 2), HD, GQ + h % 2, GK
                                else:
                                    r0, width, fq, fk = HD * (h % 2) + 32 * m, 32, DQ + h // 2, DK + h // 2
                                r = slice(r0, r0 + width)
                                ps = begin(L, "s", mixer, m, made)
                                end(mm(ps[:, 0:keys], featT[r, fq, i * P:(i + 1) * P], featT[r, fk, 0:keys], True, True,
                                       tile_position=(r0, 0)), (L, "s", mixer, m, made))
                        if turned is not None:
                            h, i = softmax_pair(L, turned)
                            ps = begin(L, "t", mixer, turned)
                            pe.wait_ge(sem("prob", mixer, L), turned + 1)
                            for n, s in enumerate([0, 1] if i < 2 else [2, 3, 0, 1]):
                                ins = pe.transpose(ps[:, n * P:(n + 1) * P], prob[:, turned % 3, 0, s * P:(s + 1) * P], IDENT)
                            end(ins, (L, "t", mixer, turned))
                        if j is not None:
                            value_product(mixer, j)
                        if mixer == "gqa":
                            for item in proj_beside(L, 4 + step):
                                project(item)
                        else:
                            for x in norms_beside(L, step):
                                head_mean(x)

                pe.wait_ge(sem("roped"), L * PER_LAYER["roped"] + len(ROPED_FIRST))
                for j in range(2):
                    for hh in range(2):
                        r = slice(HD * hh, HD * hh + HD)
                        for part in ([0] if 0 in segs else []) + [1, 2]:
                            ps = begin(L, "rs", 2 * j + hh, part)
                            t0 = 0 if part == 0 else SEG
                            s0 = SEG if part == 2 else 0
                            for s in range(2):
                                ins = mm(ps[:, s * SEG:(s + 1) * SEG], featT[r, RK + j, s0 + s * P:s0 + s * P + P],
                                         featT[r, RQ + j, t0:t0 + SEG], True, True)
                            end(ins, (L, "rs", 2 * j + hh, part))
                        for item in proj_beside(L, 2 * j + hh):
                            project(item)
                    value_product("ret", j)
                attention("gqa")
                for j in range(2):
                    for lev in range(LEVELS_ALL):
                        m = j * LEVELS_ALL + lev
                        pe.wait_ge(sem("qk"), L * PER_LAYER["qk"] + m + 1)
                        for hh in range(2):
                            r = slice(HD * hh, HD * hh + HD)
                            Q, K = qk[r, m % 3, 0, :], qk[r, m % 3, 1, :]
                            ps = begin(L, "hl", j, lev, hh)
                            if lev < 9:
                                for t in tts:
                                    tq, tk = (t, t) if lev < 8 else (t ^ 1, t)
                                    ins = mm(ps[:, t * P:(t + 1) * P], K[:, tk * P:(tk + 1) * P], Q[:, tq * P:(tq + 1) * P],
                                             True, True)
                            else:
                                for s in range(2):
                                    for dr in range(2):
                                        ins = mm(ps[:, s * SEG:(s + 1) * SEG], K[:, dr * SEG + s * P:dr * SEG + s * P + P],
                                                 Q[:, dr * SEG:(dr + 1) * SEG], dr == 0, dr == 1)
                            end(ins, (L, "hl", j, lev, hh))
                        if L == 0:
                            modulation(*MOD_LATER[m])
                            if m:
                                mod_turn(*MOD_LATER[m - 1])
                            if m == len(MOD_LATER) - 1:
                                mod_turn(*MOD_LATER[m])
                    value_product("hg", j)
                rotate(ROPED_LAST)
                pe.wait_ge(sem("roped"), L * PER_LAYER["roped"] + len(ROPED))
                attention("df")
                for x in range(4, len(NORMED)):
                    head_mean(x)

                base = first_unit[("out", L, 0)]
                pe.wait_ge(sem("normed"), L * PER_LAYER["normed"] + len(NORMED))
                for f in range(KD):
                    n = base + 2 * (f // 4)
                    if f % 4 == 0:
                        arrived(n)
                        arrived(n + 1)
                    ps = begin(L, "out", f)
                    for k in range(KD):
                        mix = featT[:, MIXTILE[MIXERS[k // 2]] + k % 2, lo:TOK]
                        ins = mm(ps[:, lo:TOK], unit(n + k // 4)[:, k % 4, (f % 4) * P:(f % 4) * P + P], mix,
                                 k == 0, k == KD - 1)
                    end(ins, (L, "out", f))
                    if f % 4 == 3:
                        release_after(pe, (L, "out", f), [n, n + 1])
                pe.sem_inc(sem("mix_read"), 1)
                mean_squares("ss2", lo)

                ps = begin(L, "router")
                for k in range(KD):
                    pe.wait_ge(sem("h2_ready"), L * PER_LAYER["h2_ready"] + k + 1)
                    ins = mm(ps[0:E, lo:TOK], router_w[:, k, :], hT[:, k, lo:TOK], k == 0, k == KD - 1)
                end(ins, (L, "router"))
                ps = begin(L, "routerT")
                pe.wait_ge(sem("scores_T"), L * PER_LAYER["scores_T"] + 1)
                for i, t in enumerate(tts):
                    ins = pe.transpose(ps[:, i * E:(i + 1) * E], scT[:, t * P:(t + 1) * P], IDENT[0:E, 0:E])
                end(ins, (L, "routerT"))
                for i, t in enumerate(tts):
                    for half in range(2):
                        ps = begin(L, "h2t", i, half)
                        for q in range(4):
                            ins = pe.transpose(ps[:, q * P:(q + 1) * P], hT[:, 4 * half + q, t * P:(t + 1) * P], IDENT)
                        end(ins, (L, "h2t", i, half))
                ps = begin(L, "pos")
                pe.wait_ge(sem("mask"), L * PER_LAYER["mask"] + 1)
                w = (len(tts) + 1) * E
                flat_mask = mask[:, :, :].rearrange("p a e -> p (a e)")
                ins = mm(ps[:, 0:w], BEFORE, flat_mask[:, 0:w], True, False)
                for d in range(1, len(tts) + 1):
                    ins = mm(ps[:, d * E:w], ONES, flat_mask[:, 0:w - d * E], False, d == len(tts))
                end(ins, (L, "pos"))
                ps = begin(L, "idx")
                pe.wait_ge(sem("one_hots"), L * PER_LAYER["one_hots"] + 1)
                nb = dram[L]["nb"]
                for a in range(2 * len(tts)):
                    ins = mm(ps[0:ROWS, 0:MAXB], in_slot[:, a, :], in_block[:, a, :], a == 0, a == 2 * len(tts) - 1)
                end(ins, (L, "idx"))

                for b in range(8):
                    done = sum(1 for x in range(job_number[(L, "idx")] + 1) if x % 8 == b)
                    pe.wait_ge(free[b], done)
                pe.wait_ge(sem("table"), L * PER_LAYER["table"] + 1)
                n = pe.value_load(be_i[0:1, MAXB:MAXB + 1], min_val=2, max_val=nb)
                base = ring_loads[L] + spare_loads[L]

                def turn_rows(pair, odd):
                    pe.wait_ge(sem("gathered", L, odd), pair * 16 + 16)
                    pe.sem_inc(sem("turn"), 1)
                    for k in range(KD):
                        ins = pe.transpose(banks[0][:, k * ROWS:(k + 1) * ROWS], xg[odd][:, k * P:(k + 1) * P],
                                           IDENT[0:ROWS, 0:ROWS])
                    ins.then_inc(sem("turned", L), 1)

                pe.sem_inc(sem("turned", L), 2)
                pe.sem_inc(sem("hm_turned", L), 1)
                turn_rows(0, 0)
                def experts_block(pair, odd):
                    b = pair * 2 + odd

                    def arrived_block(i):
                        if odd:
                            pe.wait_ge(spare_landed[i], (pair + spare_loads[L]) * 16 + 16)
                        else:
                            pe.wait_ge(landed[i], (pair + ring_loads[L]) * 16 + 16)

                    pe.wait_ge(sem("xgT", L), b + 1)
                    for w in range(2):
                        for half in range(2):
                            i = 2 * w + half
                            arrived_block(i)
                            for q in range(4):
                                for c in range(2):
                                    ins = mm(banks[2 + w][ROWS * c:ROWS * c + ROWS, 0:256], xgT[:, 4 * half + q, :],
                                             weights(odd, i)[:, q, 256 * c:256 * c + 256],
                                             half == 0 and q == 0, half == 1 and q == 3, tile_position=(0, ROWS * c))
                            ins.then_inc(used[i], 1)
                    with pe.If(b + 1 < n):
                        turn_rows(pair + odd, 1 - odd)
                    pe.wait_ge(sem("hm", L), b + 2)
                    for c in range(2):
                        ins = pe.transpose(banks[4][:, c * P:(c + 1) * P], hm[:, c * P:(c + 1) * P], IDENT)
                    ins.then_inc(sem("hm_turned", L), 1)
                    pe.wait_ge(sem("hmT", L), b + 1)
                    pe.wait_ge(sem("y_read", L), b + 1)
                    for q in range(4):
                        i = 4 + q // 2
                        if q % 2 == 0:
                            arrived_block(i)
                        for c in range(2):
                            ins = mm(banks[5][ROWS * c:ROWS * c + ROWS, :], hmT[:, q % 2, ROWS * (q // 2):ROWS * (q // 2) + ROWS],
                                     weights(odd, i)[:, q % 2, 512 * c:512 * c + 512], q == 0, q == 3,
                                     tile_position=(0, ROWS * c))
                        if q % 2 == 1:
                            ins.then_inc(used[i], 1)

                with pe.Fori(0, nb // 2) as pair:
                    for odd in range(2):
                        with pe.If(pair * 2 + odd < n):
                            experts_block(pair, odd)
                        with pe.Else():
                            for i in range(6):
                                pe.wait_ge(used[i], pair * 2 + (odd + base))
                                pe.sem_inc(used[i], 1)
                for i in range(len(tts)):
                    for half in range(2):
                        ps = begin(L, "yt", i, half)
                        pe.wait_ge(sem("y_tok", L), i + 1)
                        for q in range(4):
                            ins = pe.transpose(ps[:, q * P:(q + 1) * P], ytok[:, i, 0, (4 * half + q) * P:(4 * half + q + 1) * P], IDENT)
                        end(ins, (L, "yt", i, half))

            L = LAYERS
            ps = begin(L, "ssf")
            for k in range(KD):
                pe.wait_ge(sem("ssf", "sq", L), k + 1)
                ins = mm(ps[:, SEG:TOK], ALL_MEAN, sq[:, k % 2, SEG:TOK], k == 0, k == KD - 1)
                if k < KD - 1:
                    ins.then_inc(sem("ssf", "sq_read", L), 1)
            end(ins, (L, "ssf"))

        @block.scalar
        def _(act):
            st = Steps(act, sem("act_steps"))

            def evac(key, out, in_, func=ACT.Copy, done=None, **kw):
                wait_full(act, key)
                st.did(act.activation(out, in_, func, **kw), done)
                st.settle()
                act.sem_inc(free_sem(key), 1)

            act.wait_ge(sem("cc_in"), 16)
            act.wait_ge(sem("ccs_zero"), 1)
            st.did(act.activation(ccs[:, :, 0:2], cc[:, :, :], ACT.Silu), sem("cc_silu"))
            def squares(L, name, lo):
                for k in range(KD):
                    if k >= 2:
                        act.wait_ge(sem(name, "sq_read", L), k - 1)
                    st.did(act.activation(sq[:, k % 2, lo:TOK], xT[:, k, lo:TOK], ACT.Square), sem(name, "sq", L))

            def root(key, out, lo, done):
                evac(key, out[:, lo:TOK], bank(key)[:, lo:TOK], ACT.Sqrt, done, bias=eps[:, 0:1])

            def modulate(L, which, segs, ready):
                for k in range(KD):
                    act.wait_ge(sem("hn"), 2 * L * KD + which * KD + k + 1)
                    for n, g in enumerate(segs):
                        c = 1 - g
                        st.did(act.activation(hT[:, k, g * SEG:(g + 1) * SEG], hn[:, k % 2, g * SEG:(g + 1) * SEG], ACT.Identity,
                                              scale=mscale[:, which, k, c:c + 1], bias=modT[:, L, 24 * which + k, c:c + 1]),
                               ready if n == len(segs) - 1 else None)

            for L in range(LAYERS):
                segs, tts = segments(L), token_tiles(L)
                lo = 0 if 0 in segs else SEG
                def mod_copy(lm, u):
                    m = 12 * lm + u
                    if m >= 2:
                        wait_full(act, ((m - 2) // 12, "modT", (m - 2) % 12))
                    evac((lm, "mod", u), mod_rows[:, m % 2, :], bank((lm, "mod", u))[:, :], done=sem("mod_rows"))

                if L == 0:
                    act.wait_ge(sem("x_in"), 16)
                else:
                    act.wait_ge(sem("x_done"), (L - 1) * PER_LAYER["x_done"] + 1)
                squares(L, "ss1", 0)
                if L == 0:
                    act.wait_ge(sem("eps_set"), 1)
                root((L, "ss1"), rs, 0, sem("root"))
                if L == 0:
                    for u in range(MOD_FIRST):
                        mod_copy(0, u)
                    act.wait_ge(sem("mscale"), 1)
                modulate(L, 0, [0, 1], sem("h_ready"))
                if L == 0:
                    act.wait_ge(sem("small_ready"), 1)
                    flat = lambda ap: ap.rearrange("p a b c -> p (a b c)")
                    st.did(act.activation(flat(log_decay[:, :, :, :]), flat(decay_logit[:, :, :, :]), ACT.Sigmoid), sem("decay_sig"))
                    act.wait_ge(sem("lb_sub"), 1)
                    st.did(act.activation(flat(lb_soft[:, :, :, :]), flat(lb_soft[:, :, :, :]), ACT.Exp), sem("lb_exp"))
                    act.wait_ge(sem("lam_sum"), 1)
                    st.did(act.activation(lam_ex[:, :, :].rearrange("p a b -> p (a b)"),
                                          lam_ex[:, :, :].rearrange("p a b -> p (a b)"), ACT.Exp), sem("lam_exp"))
                    act.wait_ge(sem("decay_max"), 1)
                    st.did(act.activation(flat(log_decay[:, :, :, :]), flat(log_decay[:, :, :, :]), ACT.Ln), sem("decay_ready"))

                def copy_projected(item):
                    if item[0] == "feat":
                        f = item[1]
                        q_lo = lo if f in QUERY_TILES else 0
                        func = ACT.Silu if f in (RG, RG + 1, HG, HG + 1) else ACT.Copy
                        evac((L, *item), featT[:, f, q_lo:TOK], bank((L, *item))[:, q_lo:TOK], func, sem("feat_ready"))
                    else:
                        c0, w = (0, 384) if item[1] == 0 else (384, 512)
                        evac((L, *item), vtok[:, item[2], c0:c0 + w], bank((L, *item))[:, 0:w], done=sem("v_ready"))

                for item in PROJ_FIRST:
                    copy_projected(item)
                for i in range(3):
                    q_lo = lo if i < 2 else 0
                    if i >= 2:
                        wait_full(act, (L, "gss", i - 2))
                    st.did(act.activation(sq[:, i % 2, :], featT[:, GQ + i, :], ACT.Square), sem("gsq"))
                for i in range(3):
                    if i >= 2:
                        act.wait_ge(sem("gnorm"), L * PER_LAYER["gnorm"] + i - 1)
                    root((L, "gss", i), rs2[:, i % 2, :], 0, sem("groot"))

                def head_square(x):
                    mixer, j = NORMED[x]
                    act.wait_ge(sem("mixed"), L * PER_LAYER["mixed"] + 2 * MIXERS.index(mixer) + j + 1)
                    if x >= 2:
                        wait_full(act, (L, "oss", x - 2))
                    st.did(act.activation(sq[:, x % 2, lo:TOK], featT[:, MIXTILE[mixer] + j, lo:TOK], ACT.Square), sem("osq"))

                def head_root(x, squared=False):
                    if not squared:
                        head_square(x)
                    if x >= 2:
                        act.wait_ge(sem("normed"), L * PER_LAYER["normed"] + x - 1)
                    root((L, "oss", x), rs2[:, x % 2, :], lo, sem("oroot"))

                def attention(mixer):
                    d = HD if mixer == "gqa" else 32
                    for step, (made, _, turned, j) in enumerate(softmax_steps(L, mixer)):
                        if made is not None:
                            h, i = softmax_pair(L, made)
                            keys = TOK if i >= 2 else SEG
                            for m in range(MAPS[mixer]):
                                key = (L, "s", mixer, m, made)
                                s4 = 2 * (made % 3) + m
                                act.wait_ge(sem("max", mixer, L), MAPS[mixer] * made + m + 1)
                                if made >= 3 and m == 0:
                                    wait_full(act, (L, "t", mixer, made - 3))
                                st.did(act.activation(prob[:, made % 3, m, 0:keys], bank(key)[:, 0:keys], ACT.Exp,
                                                      bias=stat[:, s4, 1:2], scale=d ** -0.5, accum_out=stat[:, s4, 2:3]),
                                       sem("exp", mixer, L))
                                st.settle()
                                act.sem_inc(free_sem(key), 1)
                        if turned is not None:
                            h, i = softmax_pair(L, turned)
                            key = (L, "t", mixer, turned)
                            if i == tts[0] and h % 2 == 0:
                                wait_full(act, (L, "pv", mixer, 0) if h else (L, "pv", {"gqa": "ret", "df": "hg"}[mixer], 1))
                            w0, ns = (0, 2) if i < 2 else (2, 4)
                            c0 = (i % 2) * P
                            last = i == tts[-1]
                            evac(key, Wst[:, h % 2, w0:w0 + ns, c0:c0 + P],
                                 bank(key)[:, 0:ns * P].rearrange("p (a t) -> p a t", a=ns),
                                 done=sem("W_ready", mixer) if last else None)
                        if mixer == "gqa":
                            for item in proj_beside(L, 4 + step):
                                copy_projected(item)
                        else:
                            for x in norms_beside(L, step):
                                head_root(x)

                if L == 0:
                    act.wait_ge(sem("setup_done"), 1)
                for j in range(2):
                    for hh in range(2):
                        h = 2 * j + hh
                        act.wait_ge(sem("dec_free"), L * PER_LAYER["dec_free"] + 2 * h + 1)
                        for n, (dr, table) in enumerate([(0, 0), (1, 0)]):
                            st.did(act.activation(dec[:, n, :, :].rearrange("p b t -> p (b t)"),
                                                  dist[:, table, :, :].rearrange("p b t -> p (b t)"), ACT.Exp,
                                                  scale=log_decay[:, L, dr, h:h + 1]), sem("dec"))
                        act.wait_ge(sem("dec_free"), L * PER_LAYER["dec_free"] + 2 * h + 2)
                        for n, rate in enumerate((log_decay, back_decay)):
                            st.did(act.activation(dec[:, 1 + n, :, :].rearrange("p b t -> p (b t)"),
                                                  dist[:, 1, :, :].rearrange("p b t -> p (b t)"), ACT.Exp,
                                                  scale=rate[:, L, n, h:h + 1], bias=seg_decay[:, L, n, h:h + 1]), sem("dec"))
                        for item in proj_beside(L, h):
                            copy_projected(item)
                attention("gqa")
                act.wait_ge(sem("fg_free"), L + 1)
                for x in range(4):
                    z = featT[:, (ZF, ZB)[x % 2] + x // 2, :]
                    st.did(act.activation(fgs[:, x, :], z, ACT.Sigmoid))
                    st.settle()
                    st.did(act.activation(z, z, ACT.Sigmoid, scale=-1.0), sem("gates"))
                for x in range(4):
                    act.wait_ge(sem("fgate"), L * PER_LAYER["fgate"] + x + 1)
                    st.did(act.activation(fgs[:, x, :], fgs[:, x, :], ACT.Ln), sem("flog"))
                for j in range(2):
                    for lev in range(LEVELS_ALL):
                        m = j * LEVELS_ALL + lev
                        if lev == 0:
                            if L == 0 and m:
                                mod_copy(*MOD_LATER[m - 1])
                            continue
                        act.wait_ge(sem("qk_arg"), L * PER_LAYER["qk_arg"] + j * 9 + lev)
                        st.did(act.activation(qk[:, m % 3, :, :].rearrange("p a t -> p (a t)"),
                                              qk[:, m % 3, :, :].rearrange("p a t -> p (a t)"), ACT.Exp), sem("qk_exp"))
                        if L == 0:
                            mod_copy(*MOD_LATER[m - 1])
                if L == 0:
                    mod_copy(*MOD_LATER[-1])
                attention("df")
                for x in range(4, len(NORMED)):
                    head_square(x)
                for x in range(4, len(NORMED)):
                    head_root(x, squared=True)
                act.wait_ge(sem("x_mixed"), L * PER_LAYER["x_mixed"] + 1)
                squares(L, "ss2", lo)
                root((L, "ss2"), rs, lo, sem("root"))
                act.wait_ge(sem("mix_read"), L + 1)
                modulate(L, 1, segs, sem("h2_ready"))
                evac((L, "router"), scT[:, lo:TOK], bank((L, "router"))[0:E, lo:TOK], done=sem("scores_T"))
                evac((L, "routerT"), sc[:, 0:len(tts), :].rearrange("p a e -> p (a e)"),
                     bank((L, "routerT"))[:, 0:len(tts) * E], ACT.Sigmoid, sem("scores"))
                for i in range(len(tts)):
                    if i >= 2:
                        act.wait_ge(sem("h2_stored", i % 2), 16 * h2_stores(L, i - 2))
                    for half in range(2):
                        evac((L, "h2t", i, half), h2tok[i % 2][:, 512 * half:512 * half + 512], bank((L, "h2t", i, half))[:, :])
                    act.dma_start(dram[L]["h2"][i * P:(i + 1) * P, :], h2tok[i % 2]).then_inc(sem("h2_stored", i % 2), 16)
                act.wait_ge(sem("table"), L * PER_LAYER["table"] + 1)
                nb = dram[L]["nb"]
                n = act.value_load(be_i[0:1, MAXB:MAXB + 1], min_val=2, max_val=nb)
                base = ring_loads[L] + spare_loads[L]

                act.sem_inc(sem("y_read", L), 1)
                for odd in range(2):
                    act.sem_inc(sem("y_stored", L, odd), 32)
                usual = usual_rows(L)
                act.wait_ge(sem("idx"), L * PER_LAYER["idx"] + 1)
                if L == 0:
                    act.wait_ge(sem("y_may_store"), 1)
                for i in (len(tts) - 2, len(tts) - 1):
                    act.wait_ge(sem("h2_stored", i % 2), 16 * h2_stores(L, i))
                def expert_block(pair, odd):
                    b = pair * 2 + odd
                    act.wait_ge(used[1], b + base + 1)
                    act.wait_ge(sem("hm", L), b + 1)
                    act.activation(sg, banks[2][:, 0:256], ACT.Silu).then_inc(sem("sg", L), 1)
                    act.wait_ge(used[5], b + base + 1)
                    act.wait_ge(sem("y_stored", L, odd), pair * 32 + 32)
                    act.activation(ysb[odd], banks[5][:, :], ACT.Copy).then_inc(sem("y_read", L), 1)
                    act.wait_ge(sem("y_read", L), b + 2)
                    more = act.value_load(filled[usual:usual + 1, bass.ds(b, 1)], min_val=0, max_val=TOK)
                    with act.If(more > 0):
                        for c in range(2):
                            act.dma_start(y_dram[bass.ds(b * ROWS, ROWS), 512 * c:512 * c + 512],
                                          ysb[odd][ROWS * c:ROWS * c + ROWS, :]).then_inc(sem("y_stored", L, odd), 16)
                    with act.Else():
                        for c in range(2):
                            act.dma_start(y_dram[bass.ds(b * ROWS, usual), 512 * c:512 * c + 512],
                                          ysb[odd][ROWS * c:ROWS * c + usual, :]).then_inc(sem("y_stored", L, odd), 16)

                with act.Fori(0, nb // 2) as pair:
                    with act.If(pair * 2 < n):
                        expert_block(pair, 0)
                        with act.If(pair * 2 + 1 < n):
                            expert_block(pair, 1)
                act.wait_ge(sem("y_stored", L, 0), ((n + 1) >> 1) * 32 + 32)
                act.wait_ge(sem("y_stored", L, 1), (n >> 1) * 32 + 32)
                act.sem_inc(sem("y_all"), 1)
                for i in range(len(tts)):
                    y1 = ytok[:, i, 1, :]
                    act.wait_ge(sem("y_gathered", i), 32 * (L + 1))
                    st.did(act.activation(y1, y1, ACT.Copy, scale=gk[:, i, 1:2]), sem("y1_scaled"))
            L = LAYERS
            act.wait_ge(sem("x_done"), (L - 1) * PER_LAYER["x_done"] + 1)
            squares(L, "ssf", SEG)
            root((L, "ssf"), rs, SEG, sem("root"))

        @block.gpsimd
        def _(pool):
            pool.wait_ge(sem("small_ready"), 1)
            st = Steps(pool, sem("pool_steps"))
            did, settle = st.did, st.settle
            pool.wait_ge(sem("zeros_set"), 1)
            pool.wait_ge(sem("h_ready"), KD)
            pool.dma_start(y_dram.rearrange("(p r) (c n) -> p (r c) n", p=P, n=256),
                           zeros[:, :].unsqueeze(1).to_broadcast([P, MAXB * ROWS * 4 // P, 256])).then_inc(sem("y_zeroed"), 16)
            for L in range(LAYERS):
                d, tts = dram[L], token_tiles(L)
                def pieces(ap, h):
                    return ap.rearrange("p s (b two h) -> p s b two h", two=2, h=h)

                def level_arguments(j, lev):
                    m = j * LEVELS_ALL + lev
                    if m >= 3:
                        jj, ll = divmod(m - 3, LEVELS_ALL)
                        for hh in range(2):
                            wait_full(pool, (L, "hl", jj, ll, hh))
                    Q, K = qk[:, m % 3, 0, :], qk[:, m % 3, 1, :]
                    if lev < 9:
                        h = LEVELS[lev] if lev < 8 else P
                        nb2 = SEG // (2 * h)
                        Qv = pieces(Q.rearrange("p (s t) -> p s t", s=2), h)
                        Kv = pieces(K.rearrange("p (s t) -> p s t", s=2), h)
                        incF = pieces(cums[:, j, 0, :, 1:SEG + 1], h)
                        excF = pieces(cums[:, j, 0, :, 0:SEG], h)
                        excB = pieces(cums[:, j, 1, :, 0:SEG], h)
                        for g in range(2):
                            midF = excF[:, g, :, 1, 0:1].to_broadcast([P, nb2, h])
                            midB = excB[:, g, :, 1, 0:1].to_broadcast([P, nb2, h])
                            did(pool.tensor_tensor(Qv[:, g, :, 1, :], incF[:, g, :, 1, :], midF, ALU.subtract))
                            did(pool.tensor_tensor(Kv[:, g, :, 0, :], midF, incF[:, g, :, 0, :], ALU.subtract))
                            did(pool.tensor_tensor(Qv[:, g, :, 0, :], midB, excB[:, g, :, 0, :], ALU.subtract))
                            did(pool.tensor_tensor(Kv[:, g, :, 1, :], excB[:, g, :, 1, :], midB, ALU.subtract))
                    else:
                        did(pool.tensor_copy(Q[:, 0:SEG], cums[:, j, 0, 1, 1:SEG + 1]))
                        did(pool.tensor_tensor(Q[:, SEG:TOK], cums[:, j, 1, 1, SEG:SEG + 1].to_broadcast([P, SEG]),
                                              cums[:, j, 1, 1, 0:SEG], ALU.subtract))
                        did(pool.tensor_tensor(K[:, 0:SEG], cums[:, j, 0, 0, SEG:SEG + 1].to_broadcast([P, SEG]),
                                              cums[:, j, 0, 0, 1:SEG + 1], ALU.subtract))
                        did(pool.tensor_copy(K[:, SEG:TOK], cums[:, j, 1, 0, 0:SEG]))
                    settle()
                    pool.sem_inc(sem("qk_arg"), 1)

                pool.wait_ge(sem("cum_ready"), L + 1)
                for j in range(2):
                    for lev in range(1, LEVELS_ALL):
                        level_arguments(j, lev)
                usual = usual_rows(L)
                pool.wait_ge(sem("one_hots"), L * PER_LAYER["one_hots"] + 1)
                n = pool.value_load(be_i[0:1, MAXB:MAXB + 1], min_val=2, max_val=d["nb"])
                for i in (len(tts) - 2, len(tts) - 1):
                    pool.wait_ge(sem("h2_stored", i % 2), 16 * h2_stores(L, i))
                pool.wait_ge(sem("idx"), L * PER_LAYER["idx"] + 1)
                if L == 0:
                    pool.wait_ge(sem("y_zeroed"), 16)
                    pool.sem_inc(sem("y_may_store"), 1)
                with pool.Fori(0, d["nb"] // 2) as pair:
                    for odd in range(2):
                        b = pair * 2 + odd
                        with pool.If(b < n):
                            pool.wait_ge(sem("turned", L), b + 1)
                            pool.wait_ge(sem("idx_col", L), b + 1)
                            pool.sem_inc(sem("gather_turn"), 1)
                            more = pool.value_load(filled[usual:usual + 1, bass.ds(b, 1)], min_val=0, max_val=TOK)
                            with pool.If(more > 0):
                                pool.indirect_dma_start(xg[odd], None, d["h2"], bass.IndirectOffsetOnAxis(idx_now[:, odd:odd + 1], 0)
                                                        ).then_inc(sem("gathered", L, odd), 16)
                            with pool.Else():
                                pool.indirect_dma_start(xg[odd][0:usual, :], None, d["h2"],
                                                        bass.IndirectOffsetOnAxis(idx_now[0:usual, odd:odd + 1], 0)
                                                        ).then_inc(sem("gathered", L, odd), 16)
                pool.wait_ge(sem("y_all"), L * PER_LAYER["y_all"] + 1)
                for i in range(len(tts)):
                    for k in range(2):
                        pool.indirect_dma_start(ytok[:, i, k, :], None, y_dram, bass.IndirectOffsetOnAxis(dti2[L][:, 2 * i + k:2 * i + k + 1], 0)
                                                ).then_inc(sem("y_gathered", i), 16)
                if L == 0:
                    for i in range(len(tts)):
                        pool.wait_ge(sem("y_gathered", i), 32)
                    pool.sem_inc(sem("y_all_gathered"), 1)

        @block.vector
        def _(dve):
            st = Steps(dve, sem("dve_steps"))
            did, settle = st.did, st.settle

            def release(key):
                settle()
                dve.sem_inc(free_sem(key), 1)

            did(dve.memset(ccs[:, :, :], 0.0), sem("ccs_zero"))
            did(dve.memset(zeros[:, :], 0.0), sem("zeros_set"))
            did(dve.memset(eps[:, :], EPS), sem("eps_set"))
            did(dve.memset(cums[:, :, :, :, :], 0.0))
            did(dve.memset(featT[:, :, :], 0.0))

            def inverse_root(n, lo):
                dve.wait_ge(sem("root"), n + 1)
                did(dve.reciprocal(rs[:, lo:TOK], rs[:, lo:TOK]))
                settle()

            def normalized(n, lo, ready, per_layer):
                for k in range(KD):
                    if k >= 2:
                        dve.wait_ge(ready, per_layer + k - 1)
                    did(dve.tensor_tensor(hn[:, k % 2, lo:TOK], xT[:, k, lo:TOK], rs[:, lo:TOK], ALU.mult), sem("hn"))

            for L in range(LAYERS):
                segs, tts = segments(L), token_tiles(L)
                lo = 0 if 0 in segs else SEG
                def mod_add(lm, u):
                    key = (lm, "modT", u)
                    wait_full(dve, key)
                    did(dve.tensor_tensor(modT[:, lm, 4 * u:4 * u + 4, :],
                                          bank(key)[:, 0:8].rearrange("p (a c) -> p a c", c=2),
                                          b_mod[:, lm, 4 * u:4 * u + 4].unsqueeze(2).to_broadcast([P, 4, 2]), ALU.add))
                    release(key)

                def mod_scale(which):
                    g_in = (norm1, norm2)[which]
                    did(dve.tensor_scalar(mscale[:, which, :, :].rearrange("p a b -> p (a b)"),
                                          modT[:, L, 24 * which + 8:24 * which + 16, :].rearrange("p a b -> p (a b)"),
                                          1.0, None, ALU.add))
                    settle()
                    did(dve.tensor_tensor(mscale[:, which, :, :], mscale[:, which, :, :],
                                          g_in[:, L, :].unsqueeze(2).to_broadcast([P, KD, 2]), ALU.mult))
                    settle()

                inverse_root(2 * L, 0)
                if L == 0:
                    dve.wait_ge(sem("first_ready"), 1)
                    for u in range(MOD_FIRST):
                        mod_add(0, u)
                    mod_scale(0)
                    dve.sem_inc(sem("mscale"), 1)
                else:
                    mod_scale(0)
                normalized(2 * L, 0, sem("h_ready"), L * PER_LAYER["h_ready"])
                if L == 0:
                    dve.wait_ge(sem("small_ready"), 1)
                    did(dve.tensor_copy(later[:, :, :].rearrange("p a t -> p (a t)"), scratch_masks[:, 0:TOK].bitcast(I32)))
                    did(dve.tensor_copy(levels[:, :, :].rearrange("p a t -> p (a t)"),
                                        scratch_masks[:, TOK:TOK + len(LEVELS) * P].bitcast(I32)))
                    settle()
                    for k in range(2):
                        did(dve.tensor_copy(tok2[:, :].rearrange("p (a k) -> p a k", k=2)[:, :, k], tok_id[:, :]))
                    l0, l1 = lb_logit[:, :, 0, :], lb_logit[:, :, 1, :]
                    did(dve.tensor_tensor(lb_tmp[:, 0, :, :], l0, l1, ALU.max))
                    settle()
                    did(dve.tensor_tensor(lb_soft[:, :, 0, :], l0, lb_tmp[:, 0, :, :], ALU.subtract))
                    did(dve.tensor_tensor(lb_soft[:, :, 1, :], l1, lb_tmp[:, 0, :, :], ALU.subtract))
                    settle()
                    dve.sem_inc(sem("lb_sub"), 1)
                    did(dve.tensor_tensor(lam_pr[:, :, 0, :], lam_in[:, :, 0, :], lam_in[:, :, 1, :], ALU.mult))
                    did(dve.tensor_tensor(lam_pr[:, :, 1, :], lam_in[:, :, 2, :], lam_in[:, :, 3, :], ALU.mult))
                    settle()
                    did(dve.tensor_reduce(lam_ex[:, :, :], lam_pr[:, :, :, :], AX_X, ALU.add), sem("lam_sum"))
                    dve.wait_ge(sem("decay_sig"), 1)
                    ld = log_decay[:, :, :, :].rearrange("p a b c -> p (a b c)")
                    did(dve.tensor_scalar(ld, ld, TINY, None, ALU.max), sem("decay_max"))
                    dve.wait_ge(sem("lb_exp"), 1)
                    e0, e1 = lb_soft[:, :, 0, :], lb_soft[:, :, 1, :]
                    did(dve.tensor_tensor(lb_tmp[:, 0, :, :], e0, e1, ALU.add))
                    settle()
                    did(dve.reciprocal(lb_tmp[:, 1, :, :], lb_tmp[:, 0, :, :]))
                    settle()
                    did(dve.tensor_tensor(e0, e0, lb_tmp[:, 1, :, :], ALU.mult))
                    did(dve.tensor_tensor(e1, e1, lb_tmp[:, 1, :, :], ALU.mult))
                    settle()
                    did(dve.tensor_tensor(lb[:, :, 0, :], e0, e0, ALU.subtract))
                    did(dve.tensor_tensor(lb_tmp[:, 0, :, :], e0, e1, ALU.add))
                    settle()
                    did(dve.tensor_tensor(lb[:, :, 1, :], lb_tmp[:, 0, :, :], e0, ALU.subtract))
                    settle()
                    did(dve.tensor_scalar(one_m_lb[:, :, :, :].rearrange("p a b c -> p (a b c)"),
                                          lb[:, :, :, :].rearrange("p a b c -> p (a b c)"), -1.0, 1.0, ALU.mult, ALU.add))
                    dve.wait_ge(sem("decay_ready"), 1)
                    bd, sd = (x[:, :, :, :].rearrange("p a b c -> p (a b c)") for x in (back_decay, seg_decay))
                    did(dve.tensor_scalar(bd, ld, -1.0, None, ALU.mult))
                    did(dve.tensor_scalar(sd, ld, float(SEG), None, ALU.mult))
                    dve.wait_ge(sem("lam_exp"), 1)
                    did(dve.tensor_tensor(neg_lam[:, :], lam_ex[:, :, 1], lam_ex[:, :, 0], ALU.subtract))
                    settle()
                    for lay in range(LAYERS):
                        init = 0.8 - 0.6 * math.exp(-0.3 * lay)
                        did(dve.tensor_scalar(neg_lam[:, lay:lay + 1], neg_lam[:, lay:lay + 1], -init, None, ALU.add))
                        did(dve.tensor_scalar(head_g[:, 4, lay:lay + 1], head_g[:, 4, lay:lay + 1], 1 - init, None, ALU.mult))
                    settle()
                    dve.sem_inc(sem("setup_done"), 1)

                for i in range(3):
                    dve.wait_ge(sem("groot"), L * PER_LAYER["groot"] + i + 1)
                    root_i = rs2[:, i % 2, :]
                    did(dve.reciprocal(root_i, root_i))
                    settle()
                    f = featT[:, GQ + i, :]
                    did(dve.scalar_tensor_tensor(out=f, in0=f, scalar=head_g[:, 1 + i // 2, L:L + 1], in1=root_i,
                                                 op0=ALU.mult, op1=ALU.mult), sem("gnorm"))
                    settle()
                def rotary(tiles):
                    for n, f in enumerate(tiles + [None]):
                        settle()
                        if f is not None:
                            key = (L, "rope", f)
                            wait_full(dve, key)
                            cs = 0 if f < DQ else 2
                            x = featT[:, f, SEG:TOK]
                            did(dve.tensor_tensor(rot[:, n % 2, :], bank(key)[:, 0:SEG], rope[:, cs + 1, :], ALU.mult))
                            did(dve.tensor_tensor(x, x, rope[:, cs, :], ALU.mult))
                        if n:
                            x = featT[:, tiles[n - 1], SEG:TOK]
                            did(dve.tensor_tensor(x, x, rot[:, (n - 1) % 2, :], ALU.add), sem("roped"))
                        if f is not None:
                            release(key)

                rotary(ROPED_FIRST)

                def readout(mixer, j):
                    key = (L, "pv", mixer, j)
                    wait_full(dve, key)
                    did(dve.tensor_copy(featT[:, MIXTILE[mixer] + j, lo:TOK], bank(key)[:, lo:TOK]))
                    release(key)
                    dve.sem_inc(sem("mixed"), 1)

                dve.sem_inc(sem("dec_free"), 1)
                for j in range(2):
                    for hh in range(2):
                        h = 2 * j + hh
                        dve.wait_ge(sem("dec"), L * PER_LAYER["dec"] + 4 * h + 2)
                        own = dec[:, 0, :, :]
                        did(dve.copy_predicated(own, later[:, :, :], dec[:, 1, :, :]))
                        settle()
                        for c in range(2):
                            diag = own[:, c, c * P:(c + 1) * P]
                            did(dve.tensor_tensor(diag, diag, IDENT, ALU.add))
                        settle()
                        dve.sem_inc(sem("dec_free"), 1)
                        for part in ([0] if 0 in segs else []) + [2]:
                            key = (L, "rs", h, part)
                            if part == 2:
                                cross = (L, "rs", h, 1)
                                dve.wait_ge(sem("dec"), L * PER_LAYER["dec"] + 4 * h + 4)
                                did(dve.tensor_tensor(dec[:, 1, :, :], dec[:, 1, :, :], dec[:, 2, :, :], ALU.add))
                                settle()
                                wait_full(dve, cross)
                                did(dve.scalar_tensor_tensor(out=Wst[:, hh, 4:6, :],
                                                             in0=bank(cross)[:, :].rearrange("p (a t) -> p a t", a=2),
                                                             scalar=HD ** -0.5, in1=dec[:, 1, :, :], op0=ALU.mult, op1=ALU.mult))
                                release(cross)
                            wait_full(dve, key)
                            w = 0 if part == 0 else 2
                            did(dve.scalar_tensor_tensor(out=Wst[:, hh, w:w + 2, :],
                                                         in0=bank(key)[:, :].rearrange("p (a t) -> p a t", a=2),
                                                         scalar=HD ** -0.5, in1=own, op0=ALU.mult, op1=ALU.mult))
                            release(key)
                        dve.sem_inc(sem("W_ready", "ret"), 1)
                        if h < 3:
                            dve.sem_inc(sem("dec_free"), 1)
                    readout("ret", j)

                def head_norm(x):
                    mixer, j = NORMED[x]
                    out = featT[:, MIXTILE[mixer] + j, lo:TOK]
                    root_x = rs2[:, x % 2, lo:TOK]
                    dve.wait_ge(sem("oroot"), L * PER_LAYER["oroot"] + x + 1)
                    did(dve.reciprocal(root_x, root_x))
                    settle()
                    g = head_g[:, {"ret": 0, "hg": 3, "df": 4}[mixer], L:L + 1]
                    did(dve.scalar_tensor_tensor(out=out, in0=out, scalar=g, in1=root_x, op0=ALU.mult, op1=ALU.mult))
                    settle()
                    if mixer != "df":
                        did(dve.tensor_tensor(out, out, featT[:, {"ret": RG, "hg": HG}[mixer] + j, lo:TOK], ALU.mult))
                        settle()
                    dve.sem_inc(sem("normed"), 1)

                def attention(mixer):
                    scale = (HD if mixer == "gqa" else 32) ** -0.5
                    for step, (made, turned, _, j) in enumerate(softmax_steps(L, mixer)):
                        if made is not None:
                            h, i = softmax_pair(L, made)
                            keys = TOK if i >= 2 else SEG
                            for m in range(MAPS[mixer]):
                                key = (L, "s", mixer, m, made)
                                s4 = 2 * (made % 3) + m
                                wait_full(dve, key)
                                did(dve.tensor_reduce(stat[:, s4, 0:1], bank(key)[:, 0:keys], AX_X, ALU.max))
                                settle()
                                did(dve.tensor_scalar(stat[:, s4, 1:2], stat[:, s4, 0:1], -scale, None, ALU.mult),
                                    sem("max", mixer, L))
                        if turned is not None:
                            h, i = softmax_pair(L, turned)
                            keys = TOK if i >= 2 else SEG
                            s4 = 2 * (turned % 3)
                            p0, p1 = prob[:, turned % 3, 0, 0:keys], prob[:, turned % 3, 1, 0:keys]
                            dve.wait_ge(sem("exp", mixer, L), MAPS[mixer] * (turned + 1))
                            did(dve.reciprocal(stat[:, s4:s4 + MAPS[mixer], 3], stat[:, s4:s4 + MAPS[mixer], 2]))
                            settle()
                            if mixer == "gqa":
                                did(dve.tensor_scalar(p0, p0, stat[:, s4, 3:4], None, ALU.mult), sem("prob", mixer, L))
                            else:
                                did(dve.tensor_scalar(p0, p0, stat[:, s4, 3:4], None, ALU.mult))
                                did(dve.tensor_scalar(stat[:, s4 + 1, 3:4], stat[:, s4 + 1, 3:4], neg_lam[:, L:L + 1], None, ALU.mult))
                                settle()
                                did(dve.scalar_tensor_tensor(out=p0, in0=p1, scalar=stat[:, s4 + 1, 3:4], in1=p0,
                                                             op0=ALU.mult, op1=ALU.add), sem("prob", mixer, L))
                        if j is not None:
                            readout(mixer, j)
                        if mixer == "df":
                            for x in norms_beside(L, step):
                                head_norm(x)

                attention("gqa")
                dve.wait_ge(sem("feat_ready"), L * PER_LAYER["feat_ready"] + HG + 2)
                dve.sem_inc(sem("fg_free"), 1)
                for x in range(4):
                    j, dr = divmod(x, 2)
                    z, fg = featT[:, (ZF, ZB)[dr] + j, :], fgs[:, x, :]
                    dve.wait_ge(sem("gates"), L * PER_LAYER["gates"] + x + 1)
                    did(dve.tensor_scalar(z, z, one_m_lb[:, dr, L, j:j + 1], None, ALU.mult))
                    did(dve.tensor_scalar(fg, fg, one_m_lb[:, dr, L, j:j + 1], lb[:, dr, L, j:j + 1], ALU.mult, ALU.add))
                    settle()
                    did(dve.tensor_scalar(fg, fg, TINY, None, ALU.max), sem("fgate"))
                for x in range(4):
                    j, dr = divmod(x, 2)
                    dve.wait_ge(sem("flog"), L * PER_LAYER["flog"] + x + 1)
                    for g in range(2):
                        did(dve.tensor_tensor_scan(cums[:, j, dr, g, 1:SEG + 1], fgs[:, x, g * SEG:(g + 1) * SEG],
                                                   fgs[:, x, g * SEG:(g + 1) * SEG], 0.0, ALU.add, ALU.bypass))
                settle()
                dve.sem_inc(sem("cum_ready"), 1)
                for j in range(2):
                    q = featT[:, HQ + j, :]
                    kf, kb = featT[:, ZF + j, :], featT[:, ZB + j, :]

                    def level_factors(lev):
                        m = j * LEVELS_ALL + lev
                        Q, K = qk[:, m % 3, 0, :], qk[:, m % 3, 1, :]
                        if lev == 0:
                            did(dve.tensor_copy(Q, q))
                            did(dve.tensor_tensor(K, kf, kb, ALU.add))
                        else:
                            dve.wait_ge(sem("qk_exp"), L * PER_LAYER["qk_exp"] + j * 9 + lev)
                            if lev < 9:
                                h = LEVELS[lev] if lev < 8 else P
                                did(dve.tensor_tensor(Q, Q, q, ALU.mult))
                                Kv, kfv, kbv = (x.rearrange("p (b two h) -> p b two h", two=2, h=h) for x in (K, kf, kb))
                                did(dve.tensor_tensor(Kv[:, :, 0, :], Kv[:, :, 0, :], kfv[:, :, 0, :], ALU.mult))
                                did(dve.tensor_tensor(Kv[:, :, 1, :], Kv[:, :, 1, :], kbv[:, :, 1, :], ALU.mult))
                            else:
                                did(dve.tensor_tensor(Q[:, 0:SEG], Q[:, 0:SEG], q[:, SEG:TOK], ALU.mult))
                                did(dve.tensor_tensor(Q[:, SEG:TOK], Q[:, SEG:TOK], q[:, SEG:TOK], ALU.mult))
                                did(dve.tensor_tensor(K[:, 0:SEG], K[:, 0:SEG], kf[:, 0:SEG], ALU.mult))
                                did(dve.tensor_tensor(K[:, SEG:TOK], K[:, SEG:TOK], kb[:, 0:SEG], ALU.mult))
                        settle()
                        dve.sem_inc(sem("qk"), 1)

                    def level_weights(lev):
                        for hh in range(2):
                            key = (L, "hl", j, lev, hh)
                            wait_full(dve, key)
                            ps = bank(key)
                            flat = Wst[:, hh, :, :].rearrange("p w t -> p (w t)")
                            if lev < 9:
                                for g in segs:
                                    src = ps[:, g * SEG:(g + 1) * SEG].rearrange("p (b t) -> p b t", b=2)
                                    if lev < 8:
                                        own = flat[:, 2 * g * SEG:2 * g * SEG + 6 * P].rearrange("p (b x) -> p b x", x=3 * P)[:, :, 0:P]
                                    else:
                                        own = flat[:, 2 * g * SEG + P:2 * g * SEG + 3 * P].rearrange("p (b x) -> p b x", x=P)
                                    if 0 < lev < 8:
                                        did(dve.copy_predicated(own, levels[:, lev, :].unsqueeze(1).to_broadcast([P, 2, P]), src))
                                    else:
                                        did(dve.tensor_copy(own, src))
                            else:
                                did(dve.tensor_copy(Wst[:, hh, 4:6, :], ps[:, :].rearrange("p (a t) -> p a t", a=2)))
                            release(key)
                        m = j * LEVELS_ALL + lev
                        if L == 0 and m:
                            mod_add(*MOD_LATER[m - 1])
                        if L == 0 and m == len(MOD_LATER) - 1:
                            mod_add(*MOD_LATER[m])

                    if j == 0:
                        wait_full(dve, (L, "pv", "gqa", 1))
                    for lev in range(-1, LEVELS_ALL + 1):
                        if lev + 1 < LEVELS_ALL and j * LEVELS_ALL + lev + 1 >= 3 and lev + 1 == 0:
                            jj, ll = divmod(j * LEVELS_ALL - 3, LEVELS_ALL)
                            for hh in range(2):
                                wait_full(dve, (L, "hl", jj, ll, hh))
                        if 0 <= lev < LEVELS_ALL:
                            level_factors(lev)
                        if lev >= 1:
                            level_weights(lev - 1)
                    dve.sem_inc(sem("W_ready", "hg"), 2)
                    readout("hg", j)

                rotary(ROPED_LAST)
                attention("df")
                for x in range(4, len(NORMED)):
                    head_norm(x)

                for f in range(KD):
                    key = (L, "out", f)
                    wait_full(dve, key)
                    for g in segs:
                        x = xT[:, f, g * SEG:(g + 1) * SEG]
                        did(dve.scalar_tensor_tensor(out=x, in0=bank(key)[:, g * SEG:(g + 1) * SEG],
                                                     scalar=modT[:, L, 16 + f, 1 - g:2 - g], in1=x, op0=ALU.mult, op1=ALU.add))
                    release(key)
                dve.sem_inc(sem("x_mixed"), 1)
                mod_scale(1)
                inverse_root(2 * L + 1, lo)
                normalized(2 * L + 1, lo, sem("h2_ready"), L * PER_LAYER["h2_ready"])

                nt, nb = len(tts), dram[L]["nb"]
                dve.wait_ge(sem("scores"), L * PER_LAYER["scores"] + 1)
                did(dve.tensor_tensor(sel[:, 0:nt, :], sc[:, 0:nt, :], router_b[:, :].unsqueeze(1).to_broadcast([P, nt, E]), ALU.add))
                settle()
                ng = nt * G
                flat3 = lambda ap: ap.rearrange("p a e -> p (a e)")
                s4 = flat3(sel[:, 0:nt, :]).rearrange("p (g e) -> p g e", e=4)
                of_j = s4.unsqueeze(2).to_broadcast([P, ng, 4, 4])
                of_e = s4.unsqueeze(3).to_broadcast([P, ng, 4, 4])
                c1 = cmp1[:, 0:16 * ng].rearrange("p (g e j) -> p g e j", e=4, j=4)
                c2 = cmp2[:, 0:16 * ng].rearrange("p (g e j) -> p g e j", e=4, j=4)
                did(dve.tensor_tensor(c1, of_j, of_e, ALU.is_gt))
                did(dve.tensor_tensor(c2, of_j, of_e, ALU.is_equal))
                settle()
                did(dve.tensor_tensor(c2, c2, iota_e[:, :, :].unsqueeze(1).to_broadcast([P, ng, 4, 4]), ALU.mult))
                settle()
                did(dve.tensor_tensor(c1, c1, c2, ALU.add))
                settle()
                mflat = flat3(mask[:, 0:nt, :])
                did(dve.memset(mask[:, nt, :], 0.0))
                m4 = mflat.rearrange("p (g e) -> p g e", e=4)
                did(dve.tensor_reduce(m4, c1, AX_X, ALU.add))
                settle()
                did(dve.tensor_scalar(mflat, mflat, 2.0, None, ALU.is_lt))
                settle()
                t4 = cmp1[:, 0:nt * E].rearrange("p (g e) -> p g e", e=4)
                did(dve.tensor_tensor(cmp1[:, 0:nt * E], mflat, flat3(sel[:, 0:nt, :]), ALU.mult))
                settle()
                did(dve.tensor_reduce(flat3(gsc[:, 0:nt, :]), t4, AX_X, ALU.add))
                settle()
                did(dve.tensor_reduce(gbest[:, 0:nt, 0], gsc[:, 0:nt, :], AX_X, ALU.max))
                settle()
                did(dve.tensor_tensor(goh[:, 0:nt, :], gsc[:, 0:nt, :], gbest[:, 0:nt, 0:1].to_broadcast([P, nt, G]), ALU.is_equal))
                settle()
                did(dve.tensor_tensor(goh[:, 0:nt, :], goh[:, 0:nt, :], g_rank[:, :].unsqueeze(1).to_broadcast([P, nt, G]), ALU.mult))
                settle()
                did(dve.tensor_reduce(gbest[:, 0:nt, 1], goh[:, 0:nt, :], AX_X, ALU.max))
                settle()
                did(dve.tensor_tensor(goh[:, 0:nt, :], goh[:, 0:nt, :], gbest[:, 0:nt, 1:2].to_broadcast([P, nt, G]), ALU.is_equal))
                settle()
                did(dve.tensor_tensor(m4, m4, flat3(goh[:, 0:nt, :]).unsqueeze(2).to_broadcast([P, ng, 4]), ALU.mult))
                settle()
                dve.sem_inc(sem("mask"), 1)
                key = (L, "pos")
                wait_full(dve, key)
                did(dve.tensor_copy(posn[:, 0:nt, :].rearrange("p a e -> p (a e)"), bank(key)[:, 0:nt * E]))
                did(dve.tensor_copy(cnt[:, :], bank(key)[:, nt * E:(nt + 1) * E]))
                release(key)
                did(dve.tensor_scalar(nblk[:, 0, :], cnt[:, :], 0.0, None, ALU.is_gt))
                settle()
                did(dve.memset(nblk[:, 0, 0:2], 1.0))
                for q in range(1, nt * P // ROWS):
                    settle()
                    did(dve.scalar_tensor_tensor(out=nblk[:, q % 2, :], in0=cnt[:, :], scalar=float(q * ROWS),
                                                 in1=nblk[:, (q - 1) % 2, :], op0=ALU.is_gt, op1=ALU.add))
                n_blk = nblk[:, (nt * P // ROWS - 1) % 2, :]
                settle()
                did(dve.tensor_scalar(n_blk[:, 0:2], n_blk[:, 0:2], -1.0, None, ALU.add))
                settle()
                did(dve.tensor_tensor_scan(blk_end[:, :], n_blk, n_blk, 2.0, ALU.add, ALU.bypass))
                settle()
                did(dve.tensor_tensor(row0[:, :], blk_end[:, :], n_blk, ALU.subtract))
                did(dve.tensor_copy(be_i[0:1, MAXB:MAXB + 1], blk_end[0:1, E - 1:E]))
                settle()
                did(dve.tensor_scalar(row0[:, :], row0[:, :], float(ROWS), 1.0, ALU.mult, ALU.add))
                settle()
                d_ = dst[:, 0:nt, :]
                did(dve.tensor_tensor(d_, posn[:, 0:nt, :], row0[:, :].unsqueeze(1).to_broadcast([P, nt, E]), ALU.add))
                first = cmp1[:, 0:2 * nt].rearrange("p (a e) -> p a e", e=2)
                did(dve.tensor_scalar(first, posn[:, 0:nt, 0:2], float(ROWS), None, ALU.is_lt))
                did(dve.scalar_tensor_tensor(out=row0_excess[:, :], in0=row0[:, 0:2], scalar=1.0, in1=row_iota[:, 1:3],
                                             op0=ALU.subtract, op1=ALU.subtract))
                settle()
                did(dve.tensor_tensor(first, first, row0_excess[:, :].unsqueeze(1).to_broadcast([P, nt, 2]), ALU.mult))
                settle()
                did(dve.scalar_tensor_tensor(out=d_[:, :, 0:2], in0=d_[:, :, 0:2], scalar=float(ROWS), in1=first,
                                             op0=ALU.subtract, op1=ALU.subtract))
                settle()
                did(dve.tensor_tensor(d_, d_, mask[:, 0:nt, :], ALU.mult))
                settle()
                did(dve.tensor_reduce(dd[:, 0:nt, 1:2].rearrange("p a o -> p (a o)"), d_, AX_X, ALU.max))
                did(dve.tensor_reduce(dd[:, 0:nt, 0:1].rearrange("p a o -> p (a o)"), d_, AX_X, ALU.add))
                settle()
                did(dve.tensor_tensor(dd[:, 0:nt, 0:1], dd[:, 0:nt, 0:1], dd[:, 0:nt, 1:2], ALU.subtract))
                settle()
                did(dve.tensor_scalar(row_of[:, 0:2 * nt], dd[:, 0:nt, :].rearrange("p a k -> p (a k)"), -1.0, None, ALU.add))
                settle()
                did(dve.tensor_copy(dti2[L][:, 0:2 * nt], row_of[:, 0:2 * nt]))
                row_b = row_of[:, 0:2 * nt].unsqueeze(2)
                did(dve.tensor_tensor(past[:, 0:2 * nt, :], row_b.to_broadcast([P, 2 * nt, MAXB + 1]),
                                      row_iota[:, 0:MAXB + 1].unsqueeze(1).to_broadcast([P, 2 * nt, MAXB + 1]), ALU.is_ge))
                settle()
                did(dve.tensor_reduce(slot_of[:, 0:2 * nt], past[:, 0:2 * nt, :], AX_X, ALU.add))
                did(dve.tensor_tensor(in_block[:, 0:2 * nt, :], past[:, 0:2 * nt, 0:MAXB], past[:, 0:2 * nt, 1:MAXB + 1], ALU.subtract))
                settle()
                did(dve.scalar_tensor_tensor(out=slot_of[:, 0:2 * nt], in0=slot_of[:, 0:2 * nt], scalar=-float(ROWS),
                                             in1=row_of[:, 0:2 * nt], op0=ALU.mult, op1=ALU.add))
                did(dve.tensor_tensor(in_block[:, 0:2 * nt, :], in_block[:, 0:2 * nt, :],
                                      tok2[:, 0:2 * nt].unsqueeze(2).to_broadcast([P, 2 * nt, MAXB]), ALU.mult))
                settle()
                did(dve.tensor_scalar(slot_of[:, 0:2 * nt], slot_of[:, 0:2 * nt], float(ROWS), None, ALU.add))
                settle()
                did(dve.tensor_tensor(in_slot[:, 0:2 * nt, :], slot_of[:, 0:2 * nt].unsqueeze(2).to_broadcast([P, 2 * nt, ROWS]),
                                      row_iota[:, MAXB + 1:].unsqueeze(1).to_broadcast([P, 2 * nt, ROWS]), ALU.is_equal))
                settle()
                dve.sem_inc(sem("one_hots"), 1)
                key = (L, "idx")
                wait_full(dve, key)
                did(dve.tensor_copy(filled[:, 0:nb], bank(key)[0:ROWS, 0:nb]))
                did(dve.tensor_scalar(idx_f[:, 0:nb], bank(key)[0:ROWS, 0:nb], -1.0, 0.0, ALU.add, ALU.max))
                settle()
                did(dve.tensor_copy(idx[:, 0:nb], idx_f[:, 0:nb]))
                release(key)
                dve.sem_inc(sem("idx"), 1)
                n = dve.value_load(be_i[0:1, MAXB:MAXB + 1], min_val=2, max_val=nb)
                base = ring_loads[L] + spare_loads[L]

                def copy_rows(b):
                    dve.wait_ge(sem("turned", L), b + 3)
                    dve.tensor_copy(xgT.rearrange("p k t -> p (k t)"), banks[0][:, :]).then_inc(sem("xgT", L), 1)

                def index_column(b, odd):
                    dve.tensor_copy(idx_now[:, odd:odd + 1], idx[:, bass.ds(b, 1)]).then_inc(sem("idx_col", L), 1)

                dve.sem_inc(sem("hm", L), 1)
                index_column(0, 0)
                index_column(1, 1)
                cmpb = be_cmp[0:1, 0:nb * E].rearrange("p (b e) -> p b e", e=E)
                did(dve.tensor_scalar(end_row[0:1, :], blk_end[0:1, :], float(ROWS), None, ALU.mult))
                settle()
                did(dve.tensor_tensor(cmpb, end_row[0:1, :].unsqueeze(1).to_broadcast([1, nb, E]),
                                      row_iota[0:1, 0:nb].unsqueeze(2).to_broadcast([1, nb, E]), ALU.is_le))
                settle()
                did(dve.tensor_reduce(be[0:1, 0:nb], cmpb, AX_X, ALU.add))
                settle()
                did(dve.tensor_scalar(be[0:1, 0:nb], be[0:1, 0:nb], float(E - 1), None, ALU.min))
                settle()
                did(dve.tensor_copy(be_i[0:1, 0:nb], be[0:1, 0:nb]))
                settle()
                dve.sem_inc(sem("table"), 1)
                did(dve.tensor_tensor(gate[:, 0:nt, :], sc[:, 0:nt, :], mask[:, 0:nt, :], ALU.mult))
                settle()
                did(dve.tensor_reduce(gsum[:, 0:nt, 0], gate[:, 0:nt, :], AX_X, ALU.add))
                settle()
                did(dve.reciprocal(gsum[:, 0:nt, 1], gsum[:, 0:nt, 0]))
                settle()
                did(dve.tensor_tensor(gate[:, 0:nt, :], gate[:, 0:nt, :], gsum[:, 0:nt, 1:2].to_broadcast([P, nt, E]), ALU.mult))
                for k in range(2):
                    pick = cmp1[:, 0:nt * E].rearrange("p (a e) -> p a e", e=E)
                    did(dve.tensor_tensor(pick, d_, dd[:, 0:nt, k:k + 1].to_broadcast([P, nt, E]), ALU.is_equal))
                    settle()
                    did(dve.tensor_tensor(pick, pick, gate[:, 0:nt, :], ALU.mult))
                    settle()
                    did(dve.tensor_reduce(gk[:, 0:nt, k], pick, AX_X, ALU.add))
                    settle()
                copy_rows(0)
                with dve.Fori(0, nb // 2) as pair:
                    for odd in range(2):
                        b = pair * 2 + odd
                        with dve.If(b < n):
                            with dve.If(b + 2 < n):
                                dve.wait_ge(sem("gathered", L, odd), pair * 16 + 16)
                                index_column(b + 2, odd)
                            dve.wait_ge(sem("sg", L), b + 1)
                            dve.wait_ge(used[3], b + base + 1)
                            dve.wait_ge(sem("hm_turned", L), b + 1)
                            dve.tensor_tensor(hm, sg, banks[3][:, 0:256], ALU.mult).then_inc(sem("hm", L), 1)
                            with dve.If(b + 1 < n):
                                copy_rows(b + 1)
                            dve.wait_ge(sem("hm_turned", L), b + 2)
                            dve.wait_ge(used[5], b + base)
                            dve.tensor_copy(hmT.rearrange("p c t -> p (c t)"), banks[4][:, 0:256]).then_inc(sem("hmT", L), 1)
                def weigh(i):
                    y0, y1 = ytok[:, i, 0, :], ytok[:, i, 1, :]
                    dve.wait_ge(sem("y_gathered", i), 32 * (L + 1))
                    dve.wait_ge(sem("y1_scaled"), i + 1 + 4 * L)
                    did(dve.scalar_tensor_tensor(out=y0, in0=y0, scalar=gk[:, i, 0:1], in1=y1, op0=ALU.mult, op1=ALU.add),
                        sem("y_tok", L))

                weigh(0)
                for i, t in enumerate(tts):
                    if i + 1 < len(tts):
                        weigh(i + 1)
                    for half in range(2):
                        key = (L, "yt", i, half)
                        wait_full(dve, key)
                        for q in range(4):
                            k = 4 * half + q
                            x = xT[:, k, t * P:(t + 1) * P]
                            g = t // 2
                            did(dve.scalar_tensor_tensor(out=x, in0=bank(key)[:, q * P:(q + 1) * P],
                                                         scalar=modT[:, L, 40 + k, 1 - g:2 - g], in1=x, op0=ALU.mult, op1=ALU.add))
                        release(key)
                dve.sem_inc(sem("x_done"), 1)
            L = LAYERS
            inverse_root(2 * L, SEG)
            for k in range(KD):
                did(dve.scalar_tensor_tensor(out=hT[:, k, SEG:TOK], in0=xT[:, k, SEG:TOK], scalar=normf[:, k:k + 1],
                                             in1=rs[:, SEG:TOK], op0=ALU.mult, op1=ALU.mult), sem("final"))


def constants():
    f = np.float32
    p = np.arange(P)
    same_head = (p[:, None] // HD == p[None, :] // HD).astype(f) / HD

    def rotation(d):
        r = np.zeros((P, P), f)
        for m in range(P):
            base, o = m // d * d, m % d
            if o < d // 2:
                r[base + o + d // 2, m] = -1
            else:
                r[base + o - d // 2, m] = 1
        return r

    mats = np.stack([np.eye(P, dtype=f), same_head, np.full((P, P), 1 / D, f),
                     (p[:, None] < p[None, :]).astype(f), np.ones((P, P), f), rotation(HD), rotation(HD // 2)], 1)

    def axial(d):
        n = d // 4
        inv = (np.float32(10000.0) ** (-np.arange(n, dtype=f) / f(n))).astype(f)
        t = np.arange(SEG)
        ang = np.concatenate([(t // GRID_W).astype(f)[:, None] * inv, (t % GRID_W).astype(f)[:, None] * inv], 1).astype(f)
        c = np.tile(np.cos(ang).astype(f).T, (2 * P // d, 1))
        s = np.tile(np.sin(ang).astype(f).T, (2 * P // d, 1))
        return c, s

    rope = np.stack([*axial(HD), *axial(HD // 2)], 1)
    s = (np.arange(2)[None, :, None] * P + p[:, None, None])
    t = np.arange(SEG)[None, None, :]
    dist = np.stack([np.abs(t - s), t - s], 1).astype(f)
    lev = np.zeros((P, len(LEVELS), P), np.uint8)
    for n, h in enumerate(LEVELS):
        if h:
            a, b = p[:, None], p[None, :]
            lev[:, n, :] = (a // (2 * h) == b // (2 * h)) & (a // h != b // h)
    return {
        "k_mats": mats, "k_mod_sel": (p[:, None] % 32 == np.arange(2)[None]).astype(f), "k_rope": rope.astype(f),
        "k_dist": dist, "k_later": (s > t).astype(np.int32).reshape(P, TOK), "k_levels": lev.astype(np.int32).reshape(P, -1),
        "k_before4": np.broadcast_to((np.arange(4)[None, :] < np.arange(4)[:, None]).astype(f), (P, 4, 4)),
        "k_grank": np.broadcast_to((G - np.arange(G)).astype(f), (P, G)),
        "k_rows": np.broadcast_to(np.concatenate([ROWS * np.arange(MAXB + 1), np.arange(ROWS)]).astype(f), (P, MAXB + 1 + ROWS)),
        "k_tok": (p[:, None] + P * np.arange(4)[None] + 1).astype(f),
    }


def kernel(**inputs):
    import concourse.bacc as bacc
    from concourse.bass_utils import run_bass_kernel_spmd

    a = {k: np.asarray(v) for k, v in inputs.items()}

    def feature_major(v):
        return np.moveaxis(v.reshape(*v.shape[:-1], v.shape[-1] // P, P), -1, 0)

    w = a["w_in"]
    col = lambda i, n: w[:, :, i:i + n]
    gq = w[:, :, 1024:1280].reshape(LAYERS, D, 4, HD)[:, :, [0, 2, 1, 3], :].reshape(LAYERS, D, 256)
    w_in = np.concatenate([
        col(0, 256), col(256, 256), col(768, 256), gq, col(1280, 128), col(512, 256), col(1408, 128),
        col(1536, 256), col(1792, 256), col(2048, 256), col(2560, 256), col(2304, 256), col(3328, 256),
        col(2816, 256), col(3072, 256)], axis=2)
    both = np.concatenate([a["ctx"][0], a["x"][0]], 0)
    twice = lambda g: np.concatenate([g, g], 1).T
    arrays = {
        "xT": np.moveaxis(both.reshape(TOK, KD, P), -1, 0).transpose(0, 2, 1),
        "cc": np.stack([a["c"][0], a["c_ctx"]], -1).reshape(KD, P, 2).transpose(1, 0, 2),
        "w_mod": a["w_mod"], "w_in": w_in, "w_out": a["w_out"],
        "b_mod": feature_major(a["b_mod"]), "norm1": feature_major(a["norm1_g"]), "norm2": feature_major(a["norm2_g"]),
        "normf": feature_major(a["final_norm_g"]),
        "head_g": np.stack([twice(a[k]) for k in ("ret_norm_g", "gqa_qnorm_g", "gqa_knorm_g", "hgrn_norm_g", "diff_norm_g")], 1),
        "decay": a["ret_decay_logit"], "lb_logit": feature_major(a["hgrn_lb_logit"]), "lam": a["diff_lambda"],
        "router_w": a["router_w"].reshape(KD, P, E).transpose(1, 0, 2), "router_b": a["router_bias"],
        "w_gate": a["moe_w_gate"], "w_up": a["moe_w_up"], "w_down": a["moe_w_down"], **constants(),
    }
    arrays = {k: np.ascontiguousarray(v) for k, v in arrays.items()}
    nc = bacc.Bacc("TRN2", target_bir_lowering=False, num_devices=1)
    A = {k: nc.dram_tensor(f"in_{k}", v.shape, mybir.dt.from_np(v.dtype), kind="ExternalInput").ap() for k, v in arrays.items()}
    A["outT"] = nc.dram_tensor("out_T", (P, KD, SEG), F32, kind="ExternalOutput").ap()
    build_program(nc, A)
    r = run_bass_kernel_spmd(nc, [{f"in_{k}": v for k, v in arrays.items()}], core_ids=[0])
    out = r.results[0]["out_T"]
    return np.ascontiguousarray(out.transpose(2, 1, 0).reshape(1, SEG, D))
```
